# Optimizing a Trainium2 kernel written in Bass

```python
import jax, jax.numpy as jnp
from jax import lax
import numpy as np

D_MODEL = 1024
BATCH = 1
SEQ = 256
DEPTH = 2

N_A_LAYERS = DEPTH // 2
RET_HEADS = D_MODEL // 256
RET_DK = 256
RET_DV = 512
RET_CHUNK = 128
ATT_HEADS = D_MODEL // 128
ATT_HD = 128
MOBA_BLOCK = 256
MOBA_TOPK = 3
MOBA_QCHUNK = 16
D_FF = 2816
N_EXPERTS = 8
MOE_TOP_K = 2
D_FF_EXPERT = 3584
ALPHA = (2 * DEPTH) ** 0.25
BETA = (8 * DEPTH) ** -0.25
LN_EPS = 1e-5
GN_EPS = 1e-6
NEG_INF = -1e30

kernel_name = 'hybrid_retnet_moba_yoco_moe'

def layer_norm(x, g, b):
    xf = x.astype(jnp.float32)
    mu = jnp.mean(xf, -1, keepdims=True)
    var = jnp.mean(jnp.square(xf - mu), -1, keepdims=True)
    return ((xf - mu) * lax.rsqrt(var + LN_EPS) * g + b).astype(x.dtype)

def swiglu(x, w_in, w_out):
    gate, up = jnp.split(x @ w_in, 2, axis=-1)
    return (jax.nn.silu(gate) * up) @ w_out

def moe_swiglu(x, router, w_in, w_out):
    B, T, D = x.shape
    xt = x.reshape(B * T, D)
    logits = (xt @ router).astype(jnp.float32)
    top_v, top_i = lax.top_k(logits, MOE_TOP_K)
    top_w = jax.nn.softmax(top_v, axis=-1)
    gates = jnp.sum(jax.nn.one_hot(top_i, N_EXPERTS, dtype=jnp.float32) * top_w[..., None], axis=1)
    out = jnp.zeros_like(xt)
    for e in range(N_EXPERTS):
        out = out + gates[:, e:e + 1].astype(x.dtype) * swiglu(xt, w_in[e], w_out[e])
    return out.reshape(B, T, D)

def retention(x, w_in, gn_g, gn_b, w_out):
    B, T, _ = x.shape
    H, DK, DV, C = RET_HEADS, RET_DK, RET_DV, RET_CHUNK
    n = T // C
    q, k, v, g = jnp.split(x @ w_in, [H * DK, 2 * H * DK, 2 * H * DK + H * DV], axis=-1)

    def to_chunks(t, d):
        return t.astype(jnp.float32).reshape(B, n, C, H, d).transpose(1, 0, 3, 2, 4)

    qc = to_chunks(q, DK)
    kc = to_chunks(k * DK ** -0.5, DK)
    vc = to_chunks(v, DV)
    lg = jnp.log1p(-jnp.exp2(-5.0 - jnp.arange(H, dtype=jnp.float32)))
    i = jnp.arange(C)
    rel = i[:, None] - i[None, :]
    inner_decay = jnp.where(rel >= 0, jnp.exp(jnp.maximum(rel, 0) * lg[:, None, None]), 0.0)
    q_decay = jnp.exp((i + 1) * lg[:, None])[..., None]
    k_decay = jnp.exp((C - 1 - i) * lg[:, None])[..., None]
    chunk_decay = jnp.exp(C * lg)[:, None, None]

    def step(state, inp):
        qi, ki, vi = inp
        att = jnp.einsum('bhid,bhjd->bhij', qi, ki) * inner_decay
        y = (jnp.einsum('bhij,bhjv->bhiv', att, vi)
             + jnp.einsum('bhid,bhdv->bhiv', qi * q_decay, state))
        state = state * chunk_decay + jnp.einsum('bhjd,bhjv->bhdv', ki * k_decay, vi)
        return state, y

    s0 = jnp.zeros((B, H, DK, DV), jnp.float32)
    _, ys = lax.scan(step, s0, (qc, kc, vc))
    y = ys.transpose(1, 0, 3, 2, 4).reshape(B, T, H, DV)
    mu = jnp.mean(y, -1, keepdims=True)
    var = jnp.mean(jnp.square(y - mu), -1, keepdims=True)
    yn = ((y - mu) * lax.rsqrt(var + GN_EPS)).reshape(B, T, H * DV) * gn_g + gn_b
    return (jax.nn.silu(g) * yn.astype(x.dtype)) @ w_out

def shared_kv(h, kv_w):
    B, T, _ = h.shape
    k, v = jnp.split(h @ kv_w, 2, axis=-1)
    nb = -(-T // MOBA_BLOCK)
    pad = nb * MOBA_BLOCK - T

    def to_heads(t):
        t = t.reshape(B, T, ATT_HEADS, ATT_HD).transpose(0, 2, 1, 3)
        return jnp.pad(t, ((0, 0), (0, 0), (0, pad), (0, 0)))

    kp, vp = to_heads(k), to_heads(v)
    k_mean = kp.reshape(B, ATT_HEADS, nb, MOBA_BLOCK, ATT_HD).mean(axis=3)
    return kp, vp, k_mean

def moba_attention(x, w_q, w_out, kp, vp, k_mean):
    B, T, _ = x.shape
    H, HD, BL = ATT_HEADS, ATT_HD, MOBA_BLOCK
    nb = k_mean.shape[2]
    ks = min(MOBA_TOPK, nb)
    scale = HD ** -0.5
    slopes = jnp.exp2(-8.0 / H * (jnp.arange(H, dtype=jnp.float32) + 1.0))
    q = (x @ w_q).reshape(B, T, H, HD).transpose(0, 2, 1, 3)
    gate = jnp.einsum('bhtd,bhnd->bhtn', q, k_mean).astype(jnp.float32)
    qblk = jnp.arange(T) // BL
    past = jnp.arange(nb)[None, :] < qblk[:, None]
    _, sel = lax.top_k(jnp.where(past, gate, NEG_INF), ks)
    kb = kp.reshape(B, H, nb, BL, HD)
    vb = vp.reshape(B, H, nb, BL, HD)
    gather = jax.vmap(jax.vmap(lambda blocks, ix: blocks[ix]))
    offs = jnp.arange(BL)

    def attend(c):
        t0 = c * MOBA_QCHUNK
        blk = t0 // BL
        tq = t0 + jnp.arange(MOBA_QCHUNK)
        qc = lax.dynamic_slice_in_dim(q, t0, MOBA_QCHUNK, axis=2)
        ic = lax.dynamic_slice_in_dim(sel, t0, MOBA_QCHUNK, axis=2)
        kg, vg = gather(kb, ic), gather(vb, ic)
        sg = jnp.einsum('bhqd,bhqnkd->bhqnk', qc, kg).astype(jnp.float32) * scale
        kpos = ic[..., None] * BL + offs
        dist_g = (tq[None, None, :, None, None] - kpos).astype(jnp.float32)
        sg = sg - slopes[None, :, None, None, None] * dist_g
        sg = jnp.where((ic < blk)[..., None], sg, NEG_INF)
        ko = lax.dynamic_slice_in_dim(kp, blk * BL, BL, axis=2)
        vo = lax.dynamic_slice_in_dim(vp, blk * BL, BL, axis=2)
        so = jnp.einsum('bhqd,bhkd->bhqk', qc, ko).astype(jnp.float32) * scale
        opos = blk * BL + offs
        dist_o = (tq[:, None] - opos[None, :]).astype(jnp.float32)
        so = so - slopes[None, :, None, None] * dist_o[None, None]
        so = jnp.where((opos[None, :] <= tq[:, None])[None, None], so, NEG_INF)
        s_all = jnp.concatenate([sg.reshape(B, H, MOBA_QCHUNK, ks * BL), so], axis=-1)
        p = jax.nn.softmax(s_all, axis=-1).astype(vp.dtype)
        pg = p[..., :ks * BL].reshape(B, H, MOBA_QCHUNK, ks, BL)
        po = p[..., ks * BL:]
        return (jnp.einsum('bhqnk,bhqnkd->bhqd', pg, vg)
                + jnp.einsum('bhqk,bhkd->bhqd', po, vo))

    outs = lax.map(attend, jnp.arange(T // MOBA_QCHUNK))
    o = outs.transpose(1, 0, 3, 2, 4).reshape(B, T, H * HD)
    return o @ w_out

def setup_inputs(seed: int = 0) -> dict:
    key = jax.random.key(seed)
    ks = jax.random.split(key, 16)
    D = D_MODEL
    n_a = N_A_LAYERS
    n_b = DEPTH - n_a
    n_dense = (DEPTH + 1) // 2
    n_moe = DEPTH // 2
    qk_w = RET_HEADS * RET_DK
    v_w = RET_HEADS * RET_DV

    def nrm(k, shape, scale):
        return jax.random.normal(k, shape, jnp.float32) * scale

    x = nrm(ks[0], (BATCH, SEQ, D), 1.0)
    ln_g = 1.0 + nrm(ks[1], (DEPTH, 2, D), 0.02)
    ln_b = nrm(ks[2], (DEPTH, 2, D), 0.02)
    col_scale = jnp.concatenate([jnp.ones((2 * qk_w,), jnp.float32),
                                 jnp.full((v_w,), BETA, jnp.float32),
                                 jnp.ones((v_w,), jnp.float32)])
    ret_w_in = nrm(ks[3], (n_a, D, 2 * qk_w + 2 * v_w), D ** -0.5) * col_scale
    ret_gn_g = 1.0 + nrm(ks[4], (n_a, v_w), 0.02)
    ret_gn_b = nrm(ks[5], (n_a, v_w), 0.02)
    ret_w_out = nrm(ks[6], (n_a, v_w, D), BETA * v_w ** -0.5)
    kv_scale = jnp.concatenate([jnp.ones((D,), jnp.float32), jnp.full((D,), BETA, jnp.float32)])
    kv_w = nrm(ks[7], (D, 2 * ATT_HEADS * ATT_HD), D ** -0.5) * kv_scale
    moba_w_q = nrm(ks[8], (n_b, D, ATT_HEADS * ATT_HD), D ** -0.5)
    moba_w_out = nrm(ks[9], (n_b, ATT_HEADS * ATT_HD, D), BETA * D ** -0.5)
    ffn_w_in = nrm(ks[10], (n_dense, D, 2 * D_FF), D ** -0.5)
    ffn_w_out = nrm(ks[11], (n_dense, D_FF, D), BETA * D_FF ** -0.5)
    moe_router = nrm(ks[12], (n_moe, D, N_EXPERTS), D ** -0.5)
    moe_w_in = nrm(ks[13], (n_moe, N_EXPERTS, D, 2 * D_FF_EXPERT), D ** -0.5)
    moe_w_out = nrm(ks[14], (n_moe, N_EXPERTS, D_FF_EXPERT, D), BETA * D_FF_EXPERT ** -0.5)
    return {'x': x, 'ln_g': ln_g, 'ln_b': ln_b,
            'ret_w_in': ret_w_in, 'ret_gn_g': ret_gn_g, 'ret_gn_b': ret_gn_b, 'ret_w_out': ret_w_out,
            'kv_w': kv_w, 'moba_w_q': moba_w_q, 'moba_w_out': moba_w_out,
            'ffn_w_in': ffn_w_in, 'ffn_w_out': ffn_w_out,
            'moe_router': moe_router, 'moe_w_in': moe_w_in, 'moe_w_out': moe_w_out}

def reference(x, ln_g, ln_b, ret_w_in, ret_gn_g, ret_gn_b, ret_w_out, kv_w, moba_w_q, moba_w_out,
              ffn_w_in, ffn_w_out, moe_router, moe_w_in, moe_w_out):
    h = x
    kp = vp = k_mean = None
    for layer in range(DEPTH):
        if layer < N_A_LAYERS:
            mix = retention(h, ret_w_in[layer], ret_gn_g[layer], ret_gn_b[layer], ret_w_out[layer])
        else:
            j = layer - N_A_LAYERS
            mix = moba_attention(h, moba_w_q[j], moba_w_out[j], kp, vp, k_mean)
        h = layer_norm(ALPHA * h + mix, ln_g[layer, 0], ln_b[layer, 0])
        if layer % 2 == 0:
            f = swiglu(h, ffn_w_in[layer // 2], ffn_w_out[layer // 2])
        else:
            f = moe_swiglu(h, moe_router[layer // 2], moe_w_in[layer // 2], moe_w_out[layer // 2])
        h = layer_norm(ALPHA * h + f, ln_g[layer, 1], ln_b[layer, 1])
        if layer == N_A_LAYERS - 1:
            kp, vp, k_mean = shared_kv(h, kv_w)
    return h


_drawn_inputs = setup_inputs


def setup_inputs(seed=0):
    import zlib

    import numpy as np

    out = dict(_drawn_inputs(seed))
    spreads = {}
    factors = {'ret_gn_g': 7.605, 'ret_gn_b': 8.0}
    for name, (base, spread) in spreads.items():
        noise = np.random.default_rng([zlib.crc32(name.encode()), seed]).standard_normal(out[name].shape)
        drawn = base * np.exp(spread * noise) if base else spread * noise
        out[name] = __import__('jax').numpy.asarray(drawn.astype(out[name].dtype))
    for name, factor in factors.items():
        out[name] = (out[name] * factor).astype(out[name].dtype)
    return out
```

```python
import math
from contextlib import ExitStack

import concourse.bass as bass
import concourse.mybir as mybir

ALU = mybir.AluOpType
ACT = mybir.ActivationFunctionType
AX = mybir.AxisListType
F32 = mybir.dt.float32
F32R = mybir.dt.float32r
U32 = mybir.dt.uint32
I32 = mybir.dt.int32

P = 128
BANK = 512
RAW = 6
SPLIT = 3
AHEAD = 3
UNIT = 2048

LN_EPS, GN_EPS = 1e-5, 1e-6
NEVER = 3e38


def build(nc, x, ln_g, ln_b, ret_w_in, ret_gn_g, ret_gn_b, ret_w_out, kv_w, moba_w_q, moba_w_out,
          ffn_w_in, ffn_w_out, moe_router, moe_w_in, moe_w_out, out):
    _, SEQ, D = x.shape
    T = SEQ // P
    KD = D // P
    DEPTH = ln_g.shape[0]
    ALPHA = (2 * DEPTH) ** 0.25
    RH = D // 256
    VW = ret_w_out.shape[1]
    DV = VW // RH
    RIN = ret_w_in.shape[2]
    AH = D // P
    FF = ffn_w_out.shape[1]
    FB = 256
    NFB = FF // FB
    EX = moe_router.shape[2]
    EFF = moe_w_out.shape[2]
    NEB = EFF // BANK
    assert T == 2 and KD == 8 and DV == BANK and NFB % 2 == 1 and EX == 8

    U_RET_IN = 0
    U_RET_OUT = U_RET_IN + RIN // BANK * 2
    U_FFN = U_RET_OUT + VW // P // 2
    U_KVQ = U_FFN + 3 * NFB
    U_ATT_OUT = U_KVQ + 3 * D // BANK * 2
    U_MOE = U_ATT_OUT + KD // 2
    JOB_UNITS = 6 * NEB
    assert JOB_UNITS % RAW == 0 and RAW % SPLIT == 0

    DR_XT = [0, 20, 24, 38]
    DR_PROJ = [4, 28]
    DR_QK = [16, 34]

    ret_in = ret_w_in.rearrange("a (k p) n -> p (a k) n", p=P)
    ret_out = ret_w_out.rearrange("a (k p) n -> p (a k) n", p=P)
    kv_in = kv_w.rearrange("(k p) n -> p k n", p=P)
    q_in = moba_w_q.rearrange("a (k p) n -> p (a k) n", p=P)
    att_out = moba_w_out.rearrange("a (k p) n -> p (a k) n", p=P)
    ffn_in = ffn_w_in.rearrange("a (k p) n -> p (a k) n", p=P)
    ffn_out = ffn_w_out.rearrange("a (k p) n -> p (a k) n", p=P)
    moe_in = moe_w_in.rearrange("a e (k p) n -> p (a e k) n", p=P)
    moe_out = moe_w_out.rearrange("a e (k p) n -> p (a e k) n", p=P)
    router_in = moe_router.rearrange("a (k p) n -> p (a k) n", p=P)
    x_rows = x.rearrange("b (t p) d -> p (b t) d", p=P)
    out_rows = out.rearrange("b (t p) d -> p (b t) d", p=P)

    XT_BANKS = [6, 7, 0, 1]
    PROJ_BANKS = [(2, 3), (4, 5), (0, 1)]
    FILLED_XT = [0, 12, 16, 28]
    FILLED_QK = [4, 20]
    LAST_SUM = [U_FFN - 1, U_KVQ - 1, U_MOE - 1]

    ctx = ExitStack()
    with ctx:
        def sem(name):
            return ctx.enter_context(nc.semaphore(name))

        map_at = [(nc.sbuf_base + 31) // 32 * 32]

        def place(name, shape, dt=F32, at=None):
            start = map_at[0] if at is None else at
            size = (math.prod(shape[1:]) * 4 + 31) // 32 * 32
            assert start + size <= nc.sbuf_usable_end, name
            if at is None:
                map_at[0] = start + size
            return nc.alloc_sbuf_tensor_at(name, shape, dt, offset=start), start

        raw, _ = place("raw", [P, RAW, UNIT])
        whi, _ = place("whi", [P, SPLIT, UNIT], F32R)
        wlo, _ = place("wlo", [P, SPLIT, UNIT], F32R)
        h, _ = place("h", [P, T, D])
        xT_hi, xT_at = place("xT_hi", [P, KD, SEQ], F32R)
        xT_lo, _ = place("xT_lo", [P, KD, SEQ], F32R)
        ident, _ = place("ident", [P, P])
        eps, _ = place("eps", [P, 2])
        stats, _ = place("stats", [P, T, 2, 6])
        mean_var, _ = place("mean_var", [P, T, 2])
        std, _ = place("std", [P, T])
        rstd, _ = place("rstd", [P, T])

        router, _ = place("router", [P, KD, EX])
        router_hi, _ = place("router_hi", [P, KD, EX], F32R)
        router_lo, _ = place("router_lo", [P, KD, EX], F32R)

        area = map_at[0]
        qkT, _ = place("qkT", [P, 2 * KD, SEQ])
        rows, rows_at = place("rows", [P, RIN // BANK, T, BANK])
        rows_flat = rows.rearrange("p c t n -> p (c t n)")
        vals = rows[:, RH:2 * RH]
        gated = rows[:, 2 * RH:3 * RH]
        decay, _ = place("decay", [P, RH, SEQ])
        attT, _ = place("attT", [P, 2, 3 * P])
        gn, _ = place("gn", [P, 2, 2, DV])
        normed, _ = place("normed", [P, T, DV])
        gstats, _ = place("gstats", [P, T, 6])
        gmv, _ = place("gmv", [P, T, 2])
        gstd, _ = place("gstd", [P, T])
        grstd, _ = place("grstd", [P, T])
        zT_hi, _ = place("zT_hi", [P, VW // P, SEQ], F32R, at=rows_at)
        zT_lo, _ = place("zT_lo", [P, VW // P, SEQ], F32R, at=xT_at)

        map_at[0] = area
        ln_gb, _ = place("ln_gb", [P, 2, D])
        ones, _ = place("ones", [P, P])
        before, _ = place("before", [P, P])
        iota_slot, _ = place("iota_slot", [P, P])
        past, _ = place("past", [P, T, SEQ])
        assert map_at[0] <= rows_at
        shared = map_at[0]
        act2, _ = place("act2", [P, T, FB])
        hid2, _ = place("hid2", [P, T, FB])
        fT_hi, _ = place("fT_hi", [P, 2, SEQ], F32R)
        fT_lo, _ = place("fT_lo", [P, 2, SEQ], F32R)
        kvq, _ = place("kvq", [P, 3 * D // BANK, T, BANK])
        kvq_flat = kvq.rearrange("p c t n -> p (c t n)")
        kqT, _ = place("kqT", [P, 2 * KD, SEQ])
        prob, _ = place("prob", [P, T, AH, SEQ])
        pT, _ = place("pT", [P, 2, 3 * P])
        neg_max, _ = place("neg_max", [P, T, AH])
        psum_p, _ = place("psum_p", [P, T, AH])
        inv_p, _ = place("inv_p", [P, T, AH])

        map_at[0] = shared
        h_hi, _ = place("h_hi", [P, T, D], F32R)
        h_lo, _ = place("h_lo", [P, T, D], F32R)
        xg_hi, _ = place("xg_hi", [P, KD, P], F32R)
        xg_lo, _ = place("xg_lo", [P, KD, P], F32R)
        act4, _ = place("act4", [P, BANK])
        hid4, _ = place("hid4", [P, BANK])
        gT_hi, _ = place("gT_hi", [P, 4, P], F32R)
        gT_lo, _ = place("gT_lo", [P, 4, P], F32R)
        y_hi, _ = place("y_hi", [P, D], F32R)
        y_lo, _ = place("y_lo", [P, D], F32R)
        sel, _ = place("sel", [P, T, P], F32R)
        selT, _ = place("selT", [P, T * P], F32R)
        logits, _ = place("logits", [P, T, EX])
        top, _ = place("top", [P, T, 8])
        top_i, _ = place("top_i", [P, T, 8], U32)
        top_f, _ = place("top_f", [P, T, 2])
        hot, _ = place("hot", [P, 2, T, EX])
        hot_w, _ = place("hot_w", [P, T, EX])
        member, _ = place("member", [P, T, EX])
        two, _ = place("two", [P, 4, T])
        slot_of, _ = place("slot_of", [P, T, 2 * EX + 1])
        gate_of, _ = place("gate_of", [P, T, 2 * EX + 1])
        most, _ = place("most", [P, 1])
        over, _ = place("over", [P, 1], I32)

        ps = ctx.enter_context(nc.psum_tensor("ps", [P, 8, BANK], F32))

        landed = [sem(f"landed{i}") for i in range(RAW)]
        hi_done = sem("hi_done")
        lo_done = sem("lo_done")
        unit_used = sem("unit_used")
        x_landed = sem("x_landed")
        gn_landed = [sem(f"gn_landed{i}") for i in range(RH)]
        ln_landed = [sem(f"ln_landed{i}") for i in range(4)]
        router_landed = sem("router_landed")
        stored = sem("stored")
        zeroed = sem("zeroed")
        tables = sem("tables")
        rel_ready = sem("rel_ready")
        decay_exp = sem("decay_exp")
        decay_ready = sem("decay_ready")
        filled = sem("filled")
        act_drained = sem("act_drained")
        dve_drained = sem("dve_drained")
        score_done = sem("score_done")
        att_ready = sem("att_ready")
        silu_g = sem("silu_g")
        ret_y = sem("ret_y")
        gn_var = sem("gn_var")
        gn_std = sem("gn_std")
        y_read = sem("y_read")
        norm_ready = sem("norm_ready")
        z_ready = sem("z_ready")
        zT_done = sem("zT_done")
        zT_hi_done = sem("zT_hi_done")
        zT_lo_done = sem("zT_lo_done")
        ln_var = sem("ln_var")
        ln_std = sem("ln_std")
        h_ready = sem("h_ready")
        f_silu = sem("f_silu")
        f_mul = sem("f_mul")
        fT_done = sem("fT_done")
        fT_hi_done = sem("fT_hi_done")
        fT_lo_done = sem("fT_lo_done")
        s_done = sem("s_done")
        max_ready = sem("max_ready")
        p_exp = sem("p_exp")
        p_ready = sem("p_ready")
        pT_done = sem("pT_done")
        pT_act = sem("pT_act")
        pT_dve = sem("pT_dve")
        o_done = sem("o_done")
        oT_hi_done = sem("oT_hi_done")
        oT_lo_done = sem("oT_lo_done")
        router_split = sem("router_split")
        logit_done = sem("logit_done")
        gap_ready = sem("gap_ready")
        gap_exp = sem("gap_exp")
        member_ready = sem("member_ready")
        rank_done = sem("rank_done")
        over_ready = sem("over_ready")
        h_hi_done = sem("h_hi_done")
        h_split = sem("h_split")
        sel_ready = sem("sel_ready")
        gathered = sem("gathered")
        xg_hi_done = sem("xg_hi_done")
        xg_lo_done = sem("xg_lo_done")
        e_silu = sem("e_silu")
        e_mul = sem("e_mul")
        gT_done = sem("gT_done")
        gT_hi_done = sem("gT_hi_done")
        gT_lo_done = sem("gT_lo_done")
        y_hi_done = sem("y_hi_done")
        y_lo_done = sem("y_lo_done")
        selT_done = sem("selT_done")
        selT_ready = sem("selT_ready")
        scattered = sem("scattered")
        summed = sem("summed")
        dve_step = sem("dve_step")

        def number(u, r):
            return u + RAW * r

        def unit_done(eng, u, r):
            eng.wait_ge(unit_used, number(u + 1, r))

        def bank(n, k):
            return ps[:, n, :].rearrange("p (k n) -> p k n", k=k)

        def load_unit(sp, u, r, src, rows):
            if u >= RAW or not isinstance(r, int):
                sp.wait_ge(lo_done, number(u - RAW + 1, r))
            dst = raw[:, u % RAW, :].rearrange("p (k n) -> p k n", k=rows)
            sp.dma_start(dst, src).then_inc(landed[u % RAW], 16)

        def split_hi(act, u, r=0):
            act.wait_ge(landed[u % RAW], 16 * (u // RAW + 1) + 16 * r)
            if u >= SPLIT:
                act.wait_ge(unit_used, number(u - SPLIT + 1, r))
            nc.scalar.activation(whi[:, u % SPLIT, :], raw[:, u % RAW, :], ACT.Copy).then_inc(hi_done, 1)

        def split_lo(dve, u, r=0):
            dve.wait_ge(hi_done, number(u + 1, r))
            nc.vector.tensor_tensor(wlo[:, u % SPLIT, :], raw[:, u % RAW, :],
                                    whi[:, u % SPLIT, :].bitcast(F32), ALU.subtract).then_inc(lo_done, 1)

        def moe_source(i, e, b):
            if i < 4:
                b, part = 0, i
            elif i < JOB_UNITS - 2:
                part = (i - 4) % 6
            else:
                b, part = NEB, i - (JOB_UNITS - 2) + 4
            if part < 4:
                col = (part // 2) * EFF
                return moe_in[:, bass.ds(e * KD + 4 * (part % 2), 4), bass.ds(col + b * BANK, BANK)], 4
            return moe_out[:, bass.ds(e * (EFF // P) + (b - 1) * 4 + 2 * (part - 4), 2), :], 2

        block = ctx.enter_context(nc.Block())

        @block.sync
        def _(sp):
            for t in range(T):
                sp.dma_start(h[:, t, :], x_rows[:, t, :]).then_inc(x_landed, 16)

            def ret_in_units(r):
                for m in range(3):
                    for part in range(2):
                        load_unit(sp, U_RET_IN + 2 * m + part, r,
                                  ret_in[:, 4 * part:4 * part + 4, bass.ds((3 * r + m) * BANK, BANK)], 4)

            ret_in_units(0)
            with sp.Fori(1, RIN // BANK // 3) as r:
                ret_in_units(r)
            for i in range(VW // P // 2):
                load_unit(sp, U_RET_OUT + i, 0, ret_out[:, 2 * i:2 * i + 2, :], 2)

            def ffn_unit(u, r, part, b):
                if part < 2:
                    src, rows = ffn_in[:, 0:KD, bass.ds(part * FF + b * FB, FB)], KD
                else:
                    src, rows = ffn_out[:, bass.ds(2 * b, 2), :], 2
                load_unit(sp, u, r, src, rows)

            ffn_unit(U_FFN, 0, 0, 0)
            ffn_unit(U_FFN + 1, 0, 1, 0)
            with sp.Fori(0, NFB // 2) as r:
                for half in range(2):
                    u = U_FFN + 2 + 3 * half
                    ffn_unit(u, r, 0, 2 * r + 1 + half)
                    ffn_unit(u + 1, r, 1, 2 * r + 1 + half)
                    ffn_unit(u + 2, r, 2, 2 * r + half)
            ffn_unit(U_FFN + 3 * NFB - 1, 0, 2, NFB - 1)
            for m in range(6):
                for part in range(2):
                    w, col = (kv_in, m * BANK) if m < 4 else (q_in, (m - 4) * BANK)
                    load_unit(sp, U_KVQ + 2 * m + part, 0, w[:, 4 * part:4 * part + 4, col:col + BANK], 4)
            for i in range(KD // 2):
                load_unit(sp, U_ATT_OUT + i, 0, att_out[:, 2 * i:2 * i + 2, :], 2)

            for i in range(AHEAD):
                load_unit(sp, U_MOE + i, 0, *moe_source(i, 0, 0))

            def job_loads(e, e_next, j):
                load_unit(sp, U_MOE + 3, NEB * j, *moe_source(3, e, 0))
                with sp.Fori(1, NEB) as b:
                    for i in range(4, 10):
                        load_unit(sp, U_MOE + i - 6, NEB * j + b, *moe_source(i, e, b))
                for i in (JOB_UNITS - 2, JOB_UNITS - 1):
                    load_unit(sp, U_MOE + i, NEB * j, *moe_source(i, e, 0))
                for i in range(AHEAD):
                    load_unit(sp, U_MOE + JOB_UNITS + i, NEB * j, *moe_source(i, e_next, 0))

            def pass_loads(first):
                with sp.Fori(0, EX - 1) as e:
                    job_loads(e, e + 1, e + first)
                job_loads(EX - 1, 0, EX - 1 + first)

            pass_loads(0)
            sp.wait_ge(over_ready, 1)
            more = sp.value_load(over[0:1, 0:1], min_val=0, max_val=1)
            with sp.If(more > 0):
                pass_loads(EX)
            for t in range(T):
                sp.wait_ge(h_ready, 6 + t + 1)
                sp.dma_start(out_rows[:, t, :], h[:, t, :]).then_inc(stored, 16)
            sp.wait_ge(stored, 16 * T)

        @block.gpsimd
        def _(pool):
            def load_gn(head):
                cols = slice(head * DV, (head + 1) * DV)
                for n, w in enumerate((ret_gn_g, ret_gn_b)):
                    pool.dma_start(gn[:, head % 2, n, :], w[0:1, cols].partition_broadcast(P)
                                   ).then_inc(gn_landed[head], 16)

            def load_ln(n):
                for k, w in enumerate((ln_g, ln_b)):
                    pool.dma_start(ln_gb[:, k, :], w[n // 2:n // 2 + 1, n % 2, :].partition_broadcast(P)
                                   ).then_inc(ln_landed[n], 16)

            pool.memset(ident[:, :], 0.0).then_inc(zeroed, 1)
            pool.memset(eps[:, 0:1], LN_EPS).then_inc(zeroed, 1)
            pool.memset(eps[:, 1:2], GN_EPS).then_inc(zeroed, 1)
            pool.wait_ge(zeroed, 3)
            pool.affine_select(out=ident[:, :], in_=ident[:, :], compare_op=ALU.not_equal, fill=1.0, base=0,
                               pattern=[[-1, P]], channel_multiplier=1).then_inc(tables, 1)
            pool.iota(decay[:, :, :], pattern=[[0, RH], [1, SEQ]], base=0, channel_multiplier=-1,
                      allow_small_or_imprecise_dtypes=True).then_inc(rel_ready, 1)
            pool.dma_start(router[:, :, :], router_in).then_inc(router_landed, 16)
            load_gn(0)
            load_gn(1)
            pool.wait_ge(decay_exp, RH)
            pool.affine_select(out=decay[:, :, :], in_=decay[:, :, :], compare_op=ALU.is_ge, fill=0.0, base=0,
                               pattern=[[0, RH], [1, SEQ]], channel_multiplier=-1).then_inc(decay_ready, 1)
            for head in range(RH):
                for t in range(T):
                    pool.wait_ge(norm_ready, T * head + t + 1)
                    if head == 0:
                        pool.wait_ge(silu_g, t + 1)
                    g = gated[:, head, t, :]
                    pool.tensor_tensor(g, g, normed[:, t, :], ALU.mult).then_inc(z_ready, 1)
                if head + 2 < RH:
                    load_gn(head + 2)
            pool.wait_ge(score_done, RH)
            load_ln(0)
            pool.memset(ones[:, :], 1.0).then_inc(zeroed, 1)
            pool.wait_ge(zeroed, 4)
            pool.affine_select(out=before[:, :], in_=ones[:, :], compare_op=ALU.is_gt, fill=0.0, base=0,
                               pattern=[[1, P]], channel_multiplier=-1).then_inc(tables, 1)
            pool.iota(iota_slot[:, :], pattern=[[1, P]], base=0, channel_multiplier=0,
                      allow_small_or_imprecise_dtypes=True).then_inc(tables, 1)
            for t in range(T):
                pool.iota(past[:, t, :], pattern=[[-1, SEQ]], base=t * P, channel_multiplier=1,
                          allow_small_or_imprecise_dtypes=True).then_inc(zeroed, 1)
            pool.wait_ge(zeroed, 6)
            for t in range(T):
                pool.affine_select(out=past[:, t, :], in_=past[:, t, :], compare_op=ALU.is_ge, fill=NEVER,
                                   base=t * P, pattern=[[-1, SEQ]], channel_multiplier=1).then_inc(tables, 1)
            for n in (1, 2, 3):
                pool.wait_ge(h_ready, T * n)
                load_ln(n)

        @block.scalar
        def _(act):
            def drain_xT(n):
                for g in range(4):
                    t, c = g // 2, 4 * (g % 2)
                    act.wait_ge(filled, FILLED_XT[n] + g + 1)
                    nc.scalar.activation(xT_hi[:, c:c + 4, t * P:(t + 1) * P], bank(XT_BANKS[g], 4),
                                         ACT.Copy).then_inc(act_drained, 1)

            def drain_proj(u0, iters, dst):
                with act.Fori(0, iters) as r:
                    for m in range(3):
                        split_hi(act, u0 + 2 * m + AHEAD, r)
                        unit_done(act, u0 + 2 * m + 1, r)
                        nc.scalar.activation(dst[:, bass.ds((3 * r + m) * T * BANK, BANK)],
                                             ps[:, PROJ_BANKS[m][0], :], ACT.Copy).then_inc(act_drained, 1)
                        split_hi(act, u0 + 2 * m + 1 + AHEAD, r)

            def norm_std(n):
                for t in range(T):
                    act.wait_ge(ln_var, T * n + t + 1)
                    nc.scalar.activation(std[:, t:t + 1], mean_var[:, t, 1:2], ACT.Sqrt,
                                         bias=eps[:, 0:1]).then_inc(ln_std, 1)

            act.wait_ge(rel_ready, 1)
            for head in range(RH):
                nc.scalar.activation(decay[:, head, :], decay[:, head, :], ACT.Exp,
                                     scale=math.log1p(-2.0 ** (-5 - head))).then_inc(decay_exp, 1)
            drain_xT(0)
            for u in range(AHEAD):
                split_hi(act, u)
            act.wait_ge(router_landed, 16)
            nc.scalar.activation(router_hi[:, :, :], router[:, :, :], ACT.Copy).then_inc(router_split, 1)
            drain_proj(U_RET_IN, RIN // BANK // 3, rows_flat)
            for g in range(0, 8, 2):
                act.wait_ge(filled, FILLED_QK[0] + g + 1)
                nc.scalar.activation(qkT[:, 4 * (g // 2):4 * (g // 2) + 4, 0:P], bank(XT_BANKS[g % 4], 4),
                                     ACT.Copy).then_inc(act_drained, 1)
            act.wait_ge(dve_drained, DR_QK[0])
            act.wait_ge(act_drained, DR_QK[0])
            for t in range(T):
                nc.scalar.activation(gated[:, :, t, :], gated[:, :, t, :], ACT.Silu).then_inc(silu_g, 1)
            for head in range(RH + 1):
                if head < RH:
                    act.wait_ge(gn_var, T * (head + 1))
                    nc.scalar.activation(gstd[:, :], gmv[:, :, 1], ACT.Sqrt, bias=eps[:, 1:2]).then_inc(gn_std, 1)
                if head >= 1:
                    for t in range(T):
                        act.wait_ge(zT_done, T * (head - 1) + t + 1)
                        nc.scalar.activation(zT_hi[:, 4 * (head - 1):4 * head, t * P:(t + 1) * P],
                                             bank(6 + t, 4), ACT.Copy).then_inc(zT_hi_done, 1)
            for u in range(U_RET_OUT, U_FFN):
                split_hi(act, u + AHEAD)
            norm_std(0)
            drain_xT(1)

            def silu_block(*u_up):
                unit_done(act, *u_up)
                nc.scalar.activation(act2[:, :, :], ps[:, 0:2, 0:FB], ACT.Silu).then_inc(f_silu, 1)

            def drain_fT(b):
                act.wait_ge(fT_done, b + 1)
                nc.scalar.activation(fT_hi[:, :, :], bank(6, 2), ACT.Copy).then_inc(fT_hi_done, 1)

            split_hi(act, U_FFN + AHEAD)
            silu_block(U_FFN + 1, 0)
            split_hi(act, U_FFN + 1 + AHEAD)
            with act.Fori(0, NFB // 2) as r:
                for half in range(2):
                    u = U_FFN + 2 + 3 * half + AHEAD
                    split_hi(act, u, r)
                    drain_fT(2 * r + half)
                    split_hi(act, u + 1, r)
                    silu_block(U_FFN + 3 + 3 * half, r)
                    split_hi(act, u + 2, r)
            drain_fT(NFB - 1)
            split_hi(act, U_KVQ - 1 + AHEAD)
            norm_std(1)
            drain_xT(2)
            drain_proj(U_KVQ, 2, kvq_flat)
            for g in range(0, 8, 2):
                act.wait_ge(filled, FILLED_QK[1] + g + 1)
                nc.scalar.activation(kqT[:, 4 * (g // 2):4 * (g // 2) + 4, 0:P], bank(XT_BANKS[g % 4], 4),
                                     ACT.Copy, scale=1.0 if g < 4 else P ** -0.5).then_inc(act_drained, 1)
            for t in range(T):
                for head in range(AH):
                    if head == 0:
                        act.wait_ge(max_ready, t + 1)
                    w = P * (t + 1)
                    nc.scalar.activation(prob[:, t, head, 0:w], prob[:, t, head, 0:w], ACT.Exp,
                                         bias=neg_max[:, t, head:head + 1],
                                         accum_out=psum_p[:, t, head:head + 1]).then_inc(p_exp, 1)
            for head in range(AH):
                if head % 2 == 0:
                    act.wait_ge(pT_done, head + 1)
                    nc.scalar.activation(pT[:, 0, :], ps[:, XT_BANKS[head % 4], 0:3 * P], ACT.Copy).then_inc(pT_act, 1)
                elif head >= 3:
                    act.wait_ge(o_done, (head - 1) // 2)
                    nc.scalar.activation(xT_hi[:, head - 3:head - 1, :], bank(2 + (head - 3) // 2, 2),
                                         ACT.Copy).then_inc(oT_hi_done, 1)
            act.wait_ge(o_done, AH // 2)
            nc.scalar.activation(xT_hi[:, AH - 2:AH, :], bank(1 + AH // 2, 2), ACT.Copy).then_inc(oT_hi_done, 1)
            for u in range(U_ATT_OUT, U_MOE):
                split_hi(act, u + AHEAD)
            norm_std(2)
            drain_xT(3)
            act.wait_ge(h_ready, T * 3)
            nc.scalar.activation(h_hi[:, :, :], h[:, :, :], ACT.Copy).then_inc(h_hi_done, 1)
            act.wait_ge(gap_ready, 1)
            nc.scalar.activation(two[:, 1, :], two[:, 0, :], ACT.Exp).then_inc(gap_exp, 1)

            def drain_xg(j):
                act.wait_ge(gathered, j + 1)
                nc.scalar.activation(xg_hi[:, :, :].rearrange("p k n -> p (k n)"),
                                     ps[:, 4:6, :].rearrange("p b n -> p (b n)"), ACT.Copy).then_inc(xg_hi_done, 1)

            def silu_e(u_gate, r):
                unit_done(act, u_gate, r)
                nc.scalar.activation(act4[:, :], ps[:, 0, :], ACT.Silu).then_inc(e_silu, 1)

            def drain_gT(n):
                act.wait_ge(gT_done, n + 1)
                nc.scalar.activation(gT_hi[:, :, :], bank(6, 4), ACT.Copy).then_inc(gT_hi_done, 1)

            def job(j):
                split_hi(act, U_MOE + 3, NEB * j)
                silu_e(U_MOE + 1, NEB * j)
                split_hi(act, U_MOE + 4, NEB * j)
                split_hi(act, U_MOE + 5, NEB * j)
                split_hi(act, U_MOE + 6, NEB * j)
                act.wait_ge(selT_done, j + 1)
                nc.scalar.activation(selT[:, :], ps[:, 7, 0:T * P], ACT.Copy).then_inc(selT_ready, 1)
                with act.Fori(1, NEB) as b:
                    n = NEB * j + b
                    u = U_MOE - 2 + AHEAD
                    split_hi(act, u, n)
                    act.wait_ge(e_mul, n)
                    silu_e(U_MOE - 1, n)
                    drain_gT(n - 1)
                    for k in range(1, 6):
                        split_hi(act, u + k, n)
                drain_gT(NEB * j + NEB - 1)
                drain_xg(j + 1)
                split_hi(act, U_MOE + JOB_UNITS - 2 + AHEAD, NEB * j)
                unit_done(act, U_MOE + JOB_UNITS - 1, NEB * j)
                nc.scalar.activation(y_hi[:, :], ps[:, 2:4, :].rearrange("p b n -> p (b n)"), ACT.Copy).then_inc(y_hi_done, 1)
                split_hi(act, U_MOE + JOB_UNITS - 1 + AHEAD, NEB * j)

            drain_xg(0)
            with act.Fori(0, EX) as j:
                job(j)
            act.wait_ge(over_ready, 1)
            more = act.value_load(over[0:1, 0:1], min_val=0, max_val=1)
            with act.If(more > 0):
                with act.Fori(EX, 2 * EX) as j:
                    job(j)
            norm_std(3)

        @block.vector
        def _(dve):
            step = [0]

            def then(ins):
                step[0] += 1
                ins.then_inc(dve_step, 1)
                dve.wait_ge(dve_step, step[0])

            def lo_of(dst, src, hi):
                return nc.vector.tensor_tensor(dst, src, hi.bitcast(F32), ALU.subtract)

            def drain_xT(n):
                for g in range(4):
                    t, c = g // 2, 4 * (g % 2)
                    dve.wait_ge(act_drained, DR_XT[n] + g + 1)
                    lo_of(xT_lo[:, c:c + 4, t * P:(t + 1) * P], bank(XT_BANKS[g], 4),
                          xT_hi[:, c:c + 4, t * P:(t + 1) * P]).then_inc(dve_drained, 1)

            def drain_proj(u0, iters, dst):
                with dve.Fori(0, iters) as r:
                    for m in range(3):
                        split_lo(dve, u0 + 2 * m + AHEAD, r)
                        unit_done(dve, u0 + 2 * m + 1, r)
                        nc.vector.tensor_copy(dst[:, bass.ds((3 * r + m) * T * BANK + BANK, BANK)],
                                              ps[:, PROJ_BANKS[m][1], :]).then_inc(dve_drained, 1)
                        split_lo(dve, u0 + 2 * m + 1 + AHEAD, r)

            def norm(n):
                if n < 3:
                    unit_done(dve, LAST_SUM[n], 0)
                    for t in range(T):
                        nc.vector.scalar_tensor_tensor(out=h[:, t, :], in0=h[:, t, :], scalar=ALPHA,
                                                       in1=ps[:, 2 + 2 * t:4 + 2 * t, :].rearrange("p b n -> p (b n)"),
                                                       op0=ALU.mult, op1=ALU.add)\
                            .then_inc(dve_step, 1)
                        step[0] += 1
                    dve.wait_ge(dve_step, step[0])
                for t in range(T):
                    for k in range(2):
                        ins = nc.vector.bn_stats(stats[:, t, k, :], h[:, t, k * BANK:(k + 1) * BANK])
                    then(ins)
                    nc.vector.bn_aggr(mean_var[:, t, :], stats[:, t, :, :].rearrange("p k s -> p (k s)")).then_inc(ln_var, 1)
                dve.wait_ge(ln_landed[n], 32)
                for t in range(T):
                    dve.wait_ge(ln_std, T * n + t + 1)
                    then(nc.vector.reciprocal(rstd[:, t:t + 1], std[:, t:t + 1]))
                    then(nc.vector.scalar_tensor_tensor(out=h[:, t, :], in0=h[:, t, :], scalar=mean_var[:, t, 0:1],
                                                        in1=ln_gb[:, 0, :], op0=ALU.subtract, op1=ALU.mult))
                    nc.vector.scalar_tensor_tensor(out=h[:, t, :], in0=h[:, t, :], scalar=rstd[:, t:t + 1],
                                                   in1=ln_gb[:, 1, :], op0=ALU.mult, op1=ALU.add).then_inc(h_ready, 1)

            drain_xT(0)
            for u in range(AHEAD):
                split_lo(dve, u)
            drain_proj(U_RET_IN, RIN // BANK // 3, rows_flat)
            for g in range(1, 8, 2):
                dve.wait_ge(filled, FILLED_QK[0] + g + 1)
                nc.vector.tensor_copy(qkT[:, 4 * (g // 2):4 * (g // 2) + 4, P:2 * P],
                                      bank(XT_BANKS[g % 4], 4)).then_inc(dve_drained, 1)

            def decayed(head):
                dve.wait_ge(score_done, head + 1)
                if head == 0:
                    dve.wait_ge(decay_ready, 1)
                if head >= 2:
                    dve.wait_ge(ret_y, T * (head - 1))
                for a, b, c in ((0, SEQ, 0), (SEQ, SEQ + P, 0)):
                    nc.vector.scalar_tensor_tensor(out=attT[:, head % 2, a:b], in0=ps[:, head % 2, a:b],
                                                   scalar=256.0 ** -0.5, in1=decay[:, head, c:c + b - a],
                                                   op0=ALU.mult, op1=ALU.mult).then_inc(att_ready, 1)

            decayed(0)
            decayed(1)
            for head in range(RH + 1):
                if head < RH:
                    for t in range(T):
                        dve.wait_ge(ret_y, T * head + t + 1)
                        then(nc.vector.bn_stats(gstats[:, t, :], ps[:, 2 + 2 * (head % 2) + t, :]))
                        nc.vector.bn_aggr(gmv[:, t, :], gstats[:, t, :]).then_inc(gn_var, 1)
                    if head + 2 < RH:
                        decayed(head + 2)
                    dve.wait_ge(gn_std, head + 1)
                    then(nc.vector.reciprocal(grstd[:, :], gstd[:, :]))
                    dve.wait_ge(gn_landed[head], 32)
                    for t in range(T):
                        if head >= 1:
                            dve.wait_ge(z_ready, T * (head - 1) + t + 1)
                        nc.vector.scalar_tensor_tensor(out=normed[:, t, :], in0=ps[:, 2 + 2 * (head % 2) + t, :],
                                                       scalar=gmv[:, t, 0:1], in1=gn[:, head % 2, 0, :],
                                                       op0=ALU.subtract, op1=ALU.mult).then_inc(y_read, 1)
                        dve.wait_ge(y_read, T * head + t + 1)
                        nc.vector.scalar_tensor_tensor(out=normed[:, t, :], in0=normed[:, t, :],
                                                       scalar=grstd[:, t:t + 1], in1=gn[:, head % 2, 1, :],
                                                       op0=ALU.mult, op1=ALU.add).then_inc(norm_ready, 1)
                if head >= 1:
                    for t in range(T):
                        dve.wait_ge(zT_hi_done, T * (head - 1) + t + 1)
                        lo_of(zT_lo[:, 4 * (head - 1):4 * head, t * P:(t + 1) * P], bank(6 + t, 4),
                              zT_hi[:, 4 * (head - 1):4 * head, t * P:(t + 1) * P]).then_inc(zT_lo_done, 1)
            for u in range(U_RET_OUT, U_FFN):
                split_lo(dve, u + AHEAD)
            norm(0)
            drain_xT(1)

            def mul_block(b):
                dve.wait_ge(f_silu, b + 1)
                nc.vector.tensor_tensor(hid2[:, :, :], act2[:, :, :], ps[:, 0:2, FB:2 * FB], ALU.mult).then_inc(f_mul, 1)

            def drain_fT(b):
                dve.wait_ge(fT_hi_done, b + 1)
                lo_of(fT_lo[:, :, :], bank(6, 2), fT_hi[:, :, :]).then_inc(fT_lo_done, 1)

            split_lo(dve, U_FFN + AHEAD)
            mul_block(0)
            split_lo(dve, U_FFN + 1 + AHEAD)
            with dve.Fori(0, NFB // 2) as r:
                for half in range(2):
                    u = U_FFN + 2 + 3 * half + AHEAD
                    split_lo(dve, u, r)
                    drain_fT(2 * r + half)
                    split_lo(dve, u + 1, r)
                    mul_block(2 * r + half + 1)
                    split_lo(dve, u + 2, r)
            drain_fT(NFB - 1)
            split_lo(dve, U_KVQ - 1 + AHEAD)
            norm(1)
            drain_xT(2)
            drain_proj(U_KVQ, 2, kvq_flat)
            for g in range(1, 8, 2):
                dve.wait_ge(filled, FILLED_QK[1] + g + 1)
                nc.vector.tensor_scalar(kqT[:, 4 * (g // 2):4 * (g // 2) + 4, P:2 * P], bank(XT_BANKS[g % 4], 4),
                                        1.0 if g < 4 else P ** -0.5, None, ALU.mult).then_inc(dve_drained, 1)
            dve.wait_ge(tables, 5)
            for t in range(T):
                w = P * (t + 1)
                dve.wait_ge(s_done, t + 1)
                for head in range(AH):
                    s = ps[:, 2 + head // 4, (head % 4) * P:(head % 4 + 1) * P] if t == 0 else \
                        ps[:, 4 + head // 2, (head % 2) * SEQ:(head % 2 + 1) * SEQ]
                    ins = nc.vector.scalar_tensor_tensor(out=prob[:, t, head, 0:w], in0=past[:, t, 0:w],
                                                         scalar=-2.0 ** (-8.0 / AH * (head + 1)), in1=s,
                                                         op0=ALU.mult, op1=ALU.add)
                then(ins)
                nc.vector.tensor_reduce(neg_max[:, t, :], prob[:, t, :, 0:w], AX.X, ALU.max,
                                        negate=True).then_inc(max_ready, 1)
            for t in range(T):
                w = P * (t + 1)
                dve.wait_ge(p_exp, AH * (t + 1))
                then(nc.vector.reciprocal(inv_p[:, t, :], psum_p[:, t, :]))
                for head in range(AH):
                    nc.vector.tensor_scalar(prob[:, t, head, 0:w], prob[:, t, head, 0:w],
                                            inv_p[:, t, head:head + 1], None, ALU.mult).then_inc(p_ready, 1)
            for head in range(AH):
                if head % 2 == 1:
                    dve.wait_ge(pT_done, head + 1)
                    nc.vector.tensor_copy(pT[:, 1, :], ps[:, XT_BANKS[head % 4], 0:3 * P]).then_inc(pT_dve, 1)
                elif head >= 4:
                    dve.wait_ge(oT_hi_done, head // 2 - 1)
                    lo_of(xT_lo[:, head - 4:head - 2, :], bank(2 + (head - 4) // 2, 2),
                          xT_hi[:, head - 4:head - 2, :]).then_inc(oT_lo_done, 1)
            for pair in (AH // 2 - 2, AH // 2 - 1):
                dve.wait_ge(oT_hi_done, pair + 1)
                lo_of(xT_lo[:, 2 * pair:2 * pair + 2, :], bank(2 + pair, 2),
                      xT_hi[:, 2 * pair:2 * pair + 2, :]).then_inc(oT_lo_done, 1)
            for u in range(U_ATT_OUT, U_MOE):
                split_lo(dve, u + AHEAD)
            norm(2)
            dve.wait_ge(router_split, 1)
            nc.vector.tensor_tensor(router_lo[:, :, :], router[:, :, :], router_hi[:, :, :].bitcast(F32),
                                    ALU.subtract).then_inc(router_split, 1)
            drain_xT(3)
            dve.wait_ge(h_hi_done, 1)
            nc.vector.tensor_tensor(h_lo[:, :, :], h[:, :, :], h_hi[:, :, :].bitcast(F32),
                                    ALU.subtract).then_inc(h_split, 1)
            nc.vector.tensor_scalar(h[:, :, :], h[:, :, :], ALPHA, None, ALU.mult).then_inc(dve_step, 1)
            step[0] += 1
            nc.vector.memset(y_hi[:, :].bitcast(F32), 0.0).then_inc(dve_step, 1)
            nc.vector.memset(y_lo[:, :].bitcast(F32), 0.0).then_inc(y_lo_done, 1)
            nc.vector.memset(selT[:, :].bitcast(F32), 0.0).then_inc(selT_ready, 1)
            nc.vector.memset(gate_of[:, :, 0:1], 0.0).then_inc(dve_step, 1)
            nc.vector.memset(slot_of[:, :, 2 * EX:2 * EX + 1], -1.0).then_inc(dve_step, 1)
            step[0] += 3
            dve.wait_ge(logit_done, 1)
            then(nc.vector.tensor_copy(logits[:, :, :], ps[:, 2, 0:T * EX].rearrange("p (t e) -> p t e", t=T)))
            for t in range(T):
                then(nc.vector.max(top[:, t, :], logits[:, t, :]))
                then(nc.vector.max_index(top_i[:, t, :], top[:, t, :], logits[:, t, :]))
            nc.vector.tensor_tensor(two[:, 0, :], top[:, :, 1], top[:, :, 0], ALU.subtract).then_inc(gap_ready, 1)
            then(nc.vector.tensor_copy(top_f[:, :, :], top_i[:, :, 0:2]))
            for k in range(2):
                for t in range(T):
                    then(nc.vector.tensor_scalar(hot[:, k, t, :], iota_slot[:, 0:EX], top_f[:, t, k:k + 1], None,
                                                 ALU.is_equal))
            nc.vector.tensor_tensor(member[:, :, :], hot[:, 0, :, :], hot[:, 1, :, :], ALU.add).then_inc(member_ready, 1)
            dve.wait_ge(gap_exp, 1)
            then(nc.vector.tensor_scalar(two[:, 2, :], two[:, 1, :], 1.0, None, ALU.add))
            then(nc.vector.reciprocal(two[:, 2, :], two[:, 2, :]))
            then(nc.vector.tensor_tensor(two[:, 3, :], two[:, 1, :], two[:, 2, :], ALU.mult))
            for t in range(T):
                then(nc.vector.tensor_scalar(hot_w[:, t, :], hot[:, 1, t, :], two[:, 3, t:t + 1], None, ALU.mult))
                for k in range(2):
                    then(nc.vector.scalar_tensor_tensor(out=gate_of[:, t, 1 + k * EX:1 + (k + 1) * EX],
                                                        in0=hot[:, 0, t, :], scalar=two[:, 2, t:t + 1],
                                                        in1=hot_w[:, t, :], op0=ALU.mult, op1=ALU.add))
            dve.wait_ge(rank_done, 1)
            for t in range(T):
                then(nc.vector.scalar_tensor_tensor(out=slot_of[:, t, 0:EX], in0=ps[:, 6, t * EX:(t + 1) * EX],
                                                    scalar=1.0, in1=member[:, t, :], op0=ALU.add, op1=ALU.mult))
            then(nc.vector.tensor_scalar(slot_of[:, :, 0:EX], slot_of[:, :, 0:EX], -1.0, None, ALU.add))
            then(nc.vector.tensor_scalar(slot_of[:, :, EX:2 * EX], slot_of[:, :, 0:EX], -float(P), None, ALU.add))
            then(nc.vector.tensor_reduce(most[:, :], ps[:, 6, T * EX:(T + 1) * EX], AX.X, ALU.max))
            nc.vector.tensor_scalar(over[:, :], most[:, :], float(P), None, ALU.is_gt).then_inc(over_ready, 1)

            def select(j):
                for t in range(T):
                    ins = nc.vector.tensor_scalar(sel[:, t, :], iota_slot[:, :], slot_of[:, t, bass.ds(j, 1)], None,
                                                  ALU.is_equal)
                ins.then_inc(sel_ready, 1)

            def drain_xg(j):
                dve.wait_ge(gathered, j + 1)
                nc.vector.tensor_copy(xg_lo[:, :, :].rearrange("p k n -> p (k n)"),
                                      ps[:, 0:2, :].rearrange("p b n -> p (b n)")).then_inc(xg_lo_done, 1)

            def mul_e(n, u_up, r):
                unit_done(dve, u_up, r)
                dve.wait_ge(e_silu, n + 1)
                nc.vector.tensor_tensor(hid4[:, :], act4[:, :], ps[:, 1, :], ALU.mult).then_inc(e_mul, 1)

            def drain_gT(n):
                dve.wait_ge(gT_hi_done, n + 1)
                lo_of(gT_lo[:, :, :], bank(6, 4), gT_hi[:, :, :]).then_inc(gT_lo_done, 1)

            def add_scattered(j, t):
                dve.wait_ge(scattered, T * j + t + 1)
                nc.vector.scalar_tensor_tensor(out=h[:, t, :], in0=ps[:, 4:6, :].rearrange("p b n -> p (b n)"),
                                               scalar=gate_of[:, t, bass.ds(j, 1)], in1=h[:, t, :],
                                               op0=ALU.mult, op1=ALU.add).then_inc(summed, 1)

            def job(j):
                split_lo(dve, U_MOE + 3, NEB * j)
                add_scattered(j, 0)
                split_lo(dve, U_MOE + 4, NEB * j)
                split_lo(dve, U_MOE + 5, NEB * j)
                mul_e(NEB * j, U_MOE + 3, NEB * j)
                split_lo(dve, U_MOE + 6, NEB * j)
                add_scattered(j, 1)
                dve.wait_ge(selT_done, j + 1)
                select(j + 1)
                with dve.Fori(1, NEB) as b:
                    n = NEB * j + b
                    u = U_MOE - 2 + AHEAD
                    split_lo(dve, u, n)
                    split_lo(dve, u + 1, n)
                    drain_gT(n - 1)
                    split_lo(dve, u + 2, n)
                    mul_e(n, U_MOE + 1, n)
                    for k in range(3, 6):
                        split_lo(dve, u + k, n)
                drain_gT(NEB * j + NEB - 1)
                drain_xg(j + 1)
                split_lo(dve, U_MOE + JOB_UNITS - 2 + AHEAD, NEB * j)
                dve.wait_ge(y_hi_done, j + 1)
                lo_of(y_lo[:, :], ps[:, 2:4, :].rearrange("p b n -> p (b n)"), y_hi[:, :]).then_inc(y_lo_done, 1)
                split_lo(dve, U_MOE + JOB_UNITS - 1 + AHEAD, NEB * j)

            select(0)
            drain_xg(0)
            with dve.Fori(0, EX) as j:
                job(j)
            dve.wait_ge(over_ready, 1)
            more = dve.value_load(over[0:1, 0:1], min_val=0, max_val=1)
            with dve.If(more > 0):
                with dve.Fori(EX, 2 * EX) as j:
                    job(j)
            jobs = EX + EX * more
            for t in range(T):
                add_scattered(jobs, t)
                dve.wait_ge(summed, T * jobs + t + 1)
            norm(3)

        @block.tensor
        def _(pe):
            def passes(dst, a_hi, a_lo, b_hi, b_lo, start, stop):
                pe.matmul(dst, a_hi, b_hi, start=start, stop=False, skip_group_check=True)
                pe.matmul(dst, a_hi, b_lo, start=False, stop=False, skip_group_check=True)
                return pe.matmul(dst, a_lo, b_hi, start=False, stop=stop, skip_group_check=True)

            def unit_ready(u, r=0):
                pe.wait_ge(lo_done, number(u + 1, r))

            def transposes_x(n):
                for g in range(4):
                    t, c = g // 2, 4 * (g % 2)
                    if g % 2 == 0:
                        if n == 0:
                            pe.wait_ge(x_landed, 16 * T)
                            pe.wait_ge(tables, 1)
                        else:
                            pe.wait_ge(h_ready, T * (n - 1) + t + 1)
                    for k in range(4):
                        last = pe.transpose(ps[:, XT_BANKS[g], k * P:(k + 1) * P],
                                            h[:, t, (c + k) * P:(c + k + 1) * P], ident[:, :])
                    last.then_inc(filled, 1)
                pe.wait_ge(dve_drained, DR_XT[n] + 4)

            def project(n, u0, iters):
                with pe.Fori(0, iters) as r:
                    for m in range(3):
                        pe.wait_ge(act_drained, DR_PROJ[n] - 2 + m + 3 * r)
                        pe.wait_ge(dve_drained, DR_PROJ[n] - 2 + m + 3 * r)
                        for part in range(2):
                            u = u0 + 2 * m + part
                            unit_ready(u, r)
                            for c in range(4):
                                k = 4 * part + c
                                w = slice(c * BANK, (c + 1) * BANK)
                                for t in range(T):
                                    tok = slice(t * P, (t + 1) * P)
                                    last = passes(ps[:, PROJ_BANKS[m][t], :], xT_hi[:, k, tok], xT_lo[:, k, tok],
                                                  whi[:, u % SPLIT, w], wlo[:, u % SPLIT, w], k == 0, k == KD - 1)
                            last.then_inc(unit_used, 1)

            def transposes_qk(n, src, blocks):
                pe.wait_ge(act_drained, DR_QK[n])
                pe.wait_ge(dve_drained, DR_QK[n])
                for g in range(8):
                    if g >= 4:
                        pe.wait_ge((act_drained, dve_drained)[g % 2], DR_QK[n] + (g - 4) // 2 + 1)
                    for k in range(4):
                        last = pe.transpose(ps[:, XT_BANKS[g % 4], k * P:(k + 1) * P],
                                            src[:, blocks[g // 2], g % 2, k * P:(k + 1) * P], ident[:, :])
                    last.then_inc(filled, 1)
                pe.wait_ge(act_drained, DR_QK[n] + 4)
                pe.wait_ge(dve_drained, DR_QK[n] + 4)

            def out_product(u, r, a_hi, a_lo, first, last_k):
                unit_ready(u, r)
                for c in range(2):
                    for t in range(T):
                        tok = slice(t * P, (t + 1) * P)
                        for half in range(2):
                            w = slice((2 * c + half) * BANK, (2 * c + half + 1) * BANK)
                            last = passes(ps[:, 2 + 2 * t + half, :], a_hi[:, c, tok], a_lo[:, c, tok],
                                          whi[:, u % SPLIT, w], wlo[:, u % SPLIT, w],
                                          first and c == 0, last_k and c == 1)
                last.then_inc(unit_used, 1)

            transposes_x(0)
            project(0, U_RET_IN, RIN // BANK // 3)
            transposes_qk(0, rows, [0, 1, 2, 3])

            def ret_scores(head):
                if head >= 2:
                    pe.wait_ge(att_ready, 2 * (head - 1))
                q, k = 2 * head, KD + 2 * head
                for c in range(2):
                    pe.matmul(ps[:, head % 2, 0:SEQ], qkT[:, k + c, 0:P], qkT[:, q + c, :],
                              start=(c == 0), stop=(c == 1))
                for c in range(2):
                    last = pe.matmul(ps[:, head % 2, SEQ:SEQ + P], qkT[:, k + c, P:SEQ], qkT[:, q + c, P:SEQ],
                                     start=(c == 0), stop=(c == 1))
                last.then_inc(score_done, 1)

            def ret_values(head):
                pe.wait_ge(att_ready, 2 * (head + 1))
                if head >= 2:
                    pe.wait_ge(y_read, T * (head - 1))
                a = attT[:, head % 2]
                y = 2 + 2 * (head % 2)
                pe.matmul(ps[:, y, :], a[:, 0:P], vals[:, head, 0, :], start=True, stop=True).then_inc(ret_y, 1)
                pe.matmul(ps[:, y + 1, :], a[:, P:SEQ], vals[:, head, 0, :], start=True, stop=False)
                pe.matmul(ps[:, y + 1, :], a[:, SEQ:SEQ + P], vals[:, head, 1, :], start=False,
                          stop=True).then_inc(ret_y, 1)

            def transposes_z(head):
                for t in range(T):
                    pe.wait_ge(z_ready, T * head + t + 1)
                    if head >= 1:
                        pe.wait_ge(zT_lo_done, T * (head - 1) + t + 1)
                    for k in range(4):
                        last = pe.transpose(ps[:, 6 + t, k * P:(k + 1) * P],
                                            gated[:, head, t, k * P:(k + 1) * P], ident[:, :])
                    last.then_inc(zT_done, 1)

            ret_scores(0)
            ret_scores(1)
            for head in range(RH):
                ret_values(head)
                if head + 2 < RH:
                    ret_scores(head + 2)
                if head >= 1:
                    transposes_z(head - 1)
            transposes_z(RH - 1)
            pe.wait_ge(zT_lo_done, T * RH)
            for i in range(U_FFN - U_RET_OUT):
                out_product(U_RET_OUT + i, 0, zT_hi[:, 2 * i:2 * i + 2], zT_lo[:, 2 * i:2 * i + 2],
                            i == 0, i == U_FFN - U_RET_OUT - 1)

            transposes_x(1)

            def ffn_in_product(u, r, part):
                unit_ready(u, r)
                for k in range(KD):
                    w = slice(k * FB, (k + 1) * FB)
                    for t in range(T):
                        tok = slice(t * P, (t + 1) * P)
                        last = passes(ps[:, t, part * FB:(part + 1) * FB], xT_hi[:, k, tok], xT_lo[:, k, tok],
                                      whi[:, u % SPLIT, w], wlo[:, u % SPLIT, w], k == 0, k == KD - 1)
                last.then_inc(unit_used, 1)

            def transposes_f(b):
                pe.wait_ge(f_mul, b + 1)
                for c in range(2):
                    for t in range(T):
                        last = pe.transpose(ps[:, 6, (2 * c + t) * P:(2 * c + t + 1) * P],
                                            hid2[:, t, c * P:(c + 1) * P], ident[:, :])
                last.then_inc(fT_done, 1)

            def ffn_block(r, half, first):
                u, b = U_FFN + 2 + 3 * half, 2 * r + half + 1
                pe.wait_ge(f_mul, b)
                ffn_in_product(u, r, 0)
                transposes_f(b - 1)
                ffn_in_product(u + 1, r, 1)
                pe.wait_ge(fT_lo_done, b)
                out_product(u + 2, r, fT_hi, fT_lo, first, False)

            ffn_in_product(U_FFN, 0, 0)
            ffn_in_product(U_FFN + 1, 0, 1)
            ffn_block(0, 0, True)
            ffn_block(0, 1, False)
            with pe.Fori(1, NFB // 2) as r:
                ffn_block(r, 0, False)
                ffn_block(r, 1, False)
            transposes_f(NFB - 1)
            pe.wait_ge(fT_lo_done, NFB)
            out_product(U_KVQ - 1, 0, fT_hi, fT_lo, False, True)

            transposes_x(2)
            project(1, U_KVQ, 2)
            transposes_qk(1, kvq, [0, 1, 4, 5])
            for t in range(T):
                for head in range(AH):
                    s = ps[:, 2 + head // 4, (head % 4) * P:(head % 4 + 1) * P] if t == 0 else \
                        ps[:, 4 + head // 2, (head % 2) * SEQ:(head % 2 + 1) * SEQ]
                    last = pe.matmul(s, kqT[:, AH + head, t * P:(t + 1) * P], kqT[:, head, 0:P * (t + 1)],
                                     start=True, stop=True)
                last.then_inc(s_done, 1)

            def transposes_p(head):
                pe.wait_ge(p_ready, AH + head + 1)
                if head >= 4:
                    pe.wait_ge((pT_act, pT_dve)[head % 2], (head - 4) // 2 + 1)
                for c, piece in enumerate((prob[:, 0, head, 0:P], prob[:, 1, head, 0:P], prob[:, 1, head, P:SEQ])):
                    last = pe.transpose(ps[:, XT_BANKS[head % 4], c * P:(c + 1) * P], piece, ident[:, :])
                last.then_inc(pT_done, 1)

            transposes_p(0)
            for head in range(AH):
                if head + 1 < AH:
                    transposes_p(head + 1)
                pe.wait_ge((pT_act, pT_dve)[head % 2], head // 2 + 1)
                o = ps[:, 2 + head // 2, (head % 2) * SEQ:(head % 2 + 1) * SEQ]
                v = slice((head % 4) * P, (head % 4 + 1) * P)
                pe.matmul(o, kvq[:, 2 + head // 4, 0, v], pT[:, head % 2, 0:SEQ], start=True, stop=False,
                          skip_group_check=True)
                last = pe.matmul(o[:, P:SEQ], kvq[:, 2 + head // 4, 1, v], pT[:, head % 2, SEQ:SEQ + P],
                                 start=False, stop=True, skip_group_check=True)
                if head % 2 == 1:
                    last.then_inc(o_done, 1)
            pe.wait_ge(oT_lo_done, AH // 2)
            for i in range(KD // 2):
                out_product(U_ATT_OUT + i, 0, xT_hi[:, 2 * i:2 * i + 2], xT_lo[:, 2 * i:2 * i + 2],
                            i == 0, i == KD // 2 - 1)

            transposes_x(3)
            pe.wait_ge(router_split, 2)
            for t in range(T):
                tok = slice(t * P, (t + 1) * P)
                for k in range(KD):
                    last = passes(ps[:, 2, t * EX:(t + 1) * EX], xT_hi[:, k, tok], xT_lo[:, k, tok],
                                  router_hi[:, k, :], router_lo[:, k, :], k == 0, k == KD - 1)
            last.then_inc(logit_done, 1)
            pe.wait_ge(member_ready, 1)
            pe.wait_ge(tables, 5)
            pe.matmul(ps[:, 6, 0:EX], before[:, :], member[:, 0, :], start=True, stop=True)
            for c, second in enumerate((before, ones)):
                at = slice((c + 1) * EX, (c + 2) * EX)
                pe.matmul(ps[:, 6, at], ones[:, :], member[:, 0, :], start=True, stop=False)
                last = pe.matmul(ps[:, 6, at], second[:, :], member[:, 1, :], start=False, stop=True)
            last.then_inc(rank_done, 1)

            def gather(j):
                pe.wait_ge(sel_ready, j + 1)
                for b0, src in ((4, h_hi), (0, h_lo)):
                    for k in range(KD):
                        for t in range(T):
                            last = pe.matmul(ps[:, b0 + k // 4, (k % 4) * P:(k % 4 + 1) * P],
                                             src[:, t, k * P:(k + 1) * P], sel[:, t, :],
                                             start=(t == 0), stop=(t == T - 1))
                last.then_inc(gathered, 1)

            def scatter(j, t):
                for half in range(2):
                    n = slice(half * BANK, (half + 1) * BANK)
                    pe.matmul(ps[:, 4 + half, :], selT[:, t * P:(t + 1) * P], y_hi[:, n], start=True, stop=False)
                    last = pe.matmul(ps[:, 4 + half, :], selT[:, t * P:(t + 1) * P], y_lo[:, n],
                                     start=False, stop=True)
                last.then_inc(scattered, 1)

            def moe_in_product(u, r, part):
                for q in range(2):
                    unit_ready(u + q, r)
                    for c in range(4):
                        k = 4 * q + c
                        w = slice(c * BANK, (c + 1) * BANK)
                        last = passes(ps[:, part, :], xg_hi[:, k, :], xg_lo[:, k, :],
                                      whi[:, (u + q) % SPLIT, w], wlo[:, (u + q) % SPLIT, w], k == 0, k == KD - 1)
                    last.then_inc(unit_used, 1)

            def moe_out_product(u, r, first, last_k):
                for q in range(2):
                    unit_ready(u + q, r)
                    for c in range(2):
                        for half in range(2):
                            w = slice((2 * c + half) * BANK, (2 * c + half + 1) * BANK)
                            last = passes(ps[:, 2 + half, :], gT_hi[:, 2 * q + c, :], gT_lo[:, 2 * q + c, :],
                                          whi[:, (u + q) % SPLIT, w], wlo[:, (u + q) % SPLIT, w],
                                          first and q == 0 and c == 0, last_k and q == 1 and c == 1)
                    last.then_inc(unit_used, 1)

            def transposes_g(n):
                pe.wait_ge(e_mul, n + 1)
                for k in range(4):
                    last = pe.transpose(ps[:, 6, k * P:(k + 1) * P], hid4[:, k * P:(k + 1) * P], ident[:, :])
                last.then_inc(gT_done, 1)

            def moe_block(j, b, first):
                n = NEB * j + b
                pe.wait_ge(e_silu, n)
                moe_in_product(U_MOE - 2, n, 0)
                transposes_g(n - 1)
                moe_in_product(U_MOE, n, 1)
                pe.wait_ge(gT_lo_done, n)
                moe_out_product(U_MOE + 2, n, first, False)

            def job(j):
                pe.wait_ge(xg_hi_done, j + 1)
                pe.wait_ge(xg_lo_done, j + 1)
                moe_in_product(U_MOE, NEB * j, 0)
                pe.wait_ge(y_lo_done, j + 1)
                pe.wait_ge(selT_ready, j + 1)
                scatter(j, 0)
                moe_in_product(U_MOE + 2, NEB * j, 1)
                pe.wait_ge(summed, T * j + 1)
                scatter(j, 1)
                for t in range(T):
                    last = pe.transpose(ps[:, 7, t * P:(t + 1) * P], sel[:, t, :].bitcast(F32), ident[:, :])
                last.then_inc(selT_done, 1)
                moe_block(j, 1, True)
                with pe.Fori(2, NEB) as b:
                    moe_block(j, b, False)
                transposes_g(NEB * j + NEB - 1)
                pe.wait_ge(summed, T * j + T)
                gather(j + 1)
                pe.wait_ge(gT_lo_done, NEB * j + NEB)
                moe_out_product(U_MOE + JOB_UNITS - 2, NEB * j, False, True)

            pe.wait_ge(h_split, 1)
            gather(0)
            with pe.Fori(0, EX) as j:
                job(j)
            pe.wait_ge(over_ready, 1)
            more = pe.value_load(over[0:1, 0:1], min_val=0, max_val=1)
            with pe.If(more > 0):
                with pe.Fori(EX, 2 * EX) as j:
                    job(j)
            jobs = EX + EX * more
            pe.wait_ge(xg_hi_done, jobs + 1)
            pe.wait_ge(y_lo_done, jobs + 1)
            pe.wait_ge(selT_ready, jobs + 1)
            scatter(jobs, 0)
            pe.wait_ge(summed, T * jobs + 1)
            scatter(jobs, 1)


_INS = ['x', 'ln_g', 'ln_b', 'ret_w_in', 'ret_gn_g', 'ret_gn_b', 'ret_w_out', 'kv_w', 'moba_w_q', 'moba_w_out',
        'ffn_w_in', 'ffn_w_out', 'moe_router', 'moe_w_in', 'moe_w_out']


def kernel(**inputs):
    import numpy as np
    import concourse.bacc as bacc
    from concourse.bass_utils import run_bass_kernel_spmd

    nc = bacc.Bacc("TRN2", target_bir_lowering=False, num_devices=1)
    arrays, args = {}, []
    for name in _INS:
        a = np.ascontiguousarray(inputs[name])
        arrays[f"in_{name}"] = a
        args.append(nc.dram_tensor(f"in_{name}", a.shape, mybir.dt.from_np(a.dtype), kind="ExternalInput").ap())
    args.append(nc.dram_tensor("out_h", inputs["x"].shape, F32, kind="ExternalOutput").ap())
    build(nc, *args)
    r = run_bass_kernel_spmd(nc, [arrays], core_ids=[0])
    return r.results[0]["out_h"]
```

```python
import math
from contextlib import ExitStack

import concourse.bass as bass
import concourse.mybir as mybir

ALU = mybir.AluOpType
ACT = mybir.ActivationFunctionType
AX = mybir.AxisListType
F32 = mybir.dt.float32
F32R = mybir.dt.float32r
U32 = mybir.dt.uint32
I32 = mybir.dt.int32

P = 128
BANK = 512
RAW = 6
SPLIT = 3
AHEAD = 3
UNIT = 2048

LN_EPS, GN_EPS = 1e-5, 1e-6
NEVER = 3e38


def build(nc, x, ln_g, ln_b, ret_w_in, ret_gn_g, ret_gn_b, ret_w_out, kv_w, moba_w_q, moba_w_out,
          ffn_w_in, ffn_w_out, moe_router, moe_w_in, moe_w_out, out):
    _, SEQ, D = x.shape
    T = SEQ // P
    KD = D // P
    DEPTH = ln_g.shape[0]
    ALPHA = (2 * DEPTH) ** 0.25
    RH = D // 256
    VW = ret_w_out.shape[1]
    DV = VW // RH
    RIN = ret_w_in.shape[2]
    AH = D // P
    FF = ffn_w_out.shape[1]
    FB = 256
    NFB = FF // FB
    EX = moe_router.shape[2]
    EFF = moe_w_out.shape[2]
    NEB = EFF // BANK
    assert T == 2 and KD == 8 and DV == BANK and NFB % 2 == 1 and EX == 8

    U_RET_IN = 0
    U_RET_OUT = U_RET_IN + RIN // BANK * 2
    U_FFN = U_RET_OUT + VW // P // 2
    U_KVQ = U_FFN + 3 * NFB
    U_ATT_OUT = U_KVQ + 3 * D // BANK * 2
    U_MOE = U_ATT_OUT + KD // 2
    JOB_UNITS = 6 * NEB
    assert JOB_UNITS % RAW == 0 and RAW % SPLIT == 0

    DR_XT = [0, 16, 20, 34]
    DR_PROJ = [4, 24]
    DR_QK = [10, 28]

    ret_in = ret_w_in.rearrange("a (k p) n -> p (a k) n", p=P)
    ret_out = ret_w_out.rearrange("a (k p) n -> p (a k) n", p=P)
    kv_in = kv_w.rearrange("(k p) n -> p k n", p=P)
    q_in = moba_w_q.rearrange("a (k p) n -> p (a k) n", p=P)
    att_out = moba_w_out.rearrange("a (k p) n -> p (a k) n", p=P)
    ffn_in = ffn_w_in.rearrange("a (k p) n -> p (a k) n", p=P)
    ffn_out = ffn_w_out.rearrange("a (k p) n -> p (a k) n", p=P)
    moe_in = moe_w_in.rearrange("a e (k p) n -> p (a e k) n", p=P)
    moe_out = moe_w_out.rearrange("a e (k p) n -> p (a e k) n", p=P)
    router_in = moe_router.rearrange("a (k p) n -> p (a k) n", p=P)
    x_rows = x.rearrange("b (t p) d -> p (b t) d", p=P)
    out_rows = out.rearrange("b (t p) d -> p (b t) d", p=P)

    T_BANKS = [6, 7, 0, 1]
    PROJ_BANKS = [(2, 3), (4, 5), (0, 1)]
    FILLED_XT = [0, 12, 16, 28]
    FILLED_QK = [4, 20]
    LAST_SUM = [U_FFN - 1, U_KVQ - 1, U_MOE - 1]
    QKV = RH + RH
    QK_GROUP_DRAINED = [11, 28]
    KVQ_BLOCK_DRAINED = [25, 26, 27, 30, 33, 34]
    LOOPED = 6

    ctx = ExitStack()
    with ctx:
        def sem(name):
            return ctx.enter_context(nc.semaphore(name))

        map_at = [(nc.sbuf_base + 31) // 32 * 32]

        def place(name, shape, dt=F32, at=None):
            start = map_at[0] if at is None else at
            size = (math.prod(shape[1:]) * 4 + 31) // 32 * 32
            assert start + size <= nc.sbuf_usable_end, name
            if at is None:
                map_at[0] = start + size
            return nc.alloc_sbuf_tensor_at(name, shape, dt, offset=start), start

        raw, _ = place("raw", [P, RAW, UNIT])
        whi, _ = place("whi", [P, SPLIT, UNIT], F32R)
        wlo, _ = place("wlo", [P, SPLIT, UNIT], F32R)
        h, _ = place("h", [P, T, D])
        xT_hi, _ = place("xT_hi", [P, KD, SEQ], F32R)
        xT_lo, _ = place("xT_lo", [P, KD, SEQ], F32R)
        ident, _ = place("ident", [P, P])
        eps, _ = place("eps", [P, 2])
        row_sum, _ = place("row_sum", [P, T])
        neg_mean, _ = place("neg_mean", [P, T])
        square_sum, _ = place("square_sum", [P, T])
        std, _ = place("std", [P, T])
        rstd, _ = place("rstd", [P, T])

        router, _ = place("router", [P, KD, EX])
        router_hi, _ = place("router_hi", [P, KD, EX], F32R)
        router_lo, _ = place("router_lo", [P, KD, EX], F32R)

        area = map_at[0]
        qkT, _ = place("qkT", [P, 2 * KD, SEQ])
        rows, rows_at = place("rows", [P, RIN // BANK, T, BANK])
        rows_flat = rows.rearrange("p c t n -> p (c t n)")
        vals = rows[:, RH:2 * RH]
        gated = rows[:, 2 * RH:3 * RH]
        decay, _ = place("decay", [P, RH, SEQ])
        attT, _ = place("attT", [P, 2, 3 * P])
        gn, _ = place("gn", [P, 2, 2, DV])
        normed, _ = place("normed", [P, T, DV])
        gstats, _ = place("gstats", [P, T, 6])
        gmv, _ = place("gmv", [P, T, 2])
        gstd, _ = place("gstd", [P, T])
        grstd, _ = place("grstd", [P, T])
        zT_hi, _ = place("zT_hi", [P, VW // P, SEQ], F32R, at=rows_at)
        zT_lo, _ = place("zT_lo", [P, VW // P, SEQ], F32R, at=rows_at + VW * T * 4)

        map_at[0] = area
        ln_gb, _ = place("ln_gb", [P, 2, D])
        ones, _ = place("ones", [P, P])
        before, _ = place("before", [P, P])
        iota_slot, _ = place("iota_slot", [P, P])
        past, _ = place("past", [P, T, SEQ])
        assert map_at[0] <= rows_at
        shared = map_at[0]
        act2, _ = place("act2", [P, T, FB])
        hid2, _ = place("hid2", [P, T, FB])
        fT_hi, _ = place("fT_hi", [P, 2, SEQ], F32R)
        fT_lo, _ = place("fT_lo", [P, 2, SEQ], F32R)
        kvq, _ = place("kvq", [P, 3 * D // BANK, T, BANK])
        kvq_flat = kvq.rearrange("p c t n -> p (c t n)")
        kqT, _ = place("kqT", [P, 2 * KD, SEQ])
        prob, _ = place("prob", [P, T, AH, SEQ])
        pT, _ = place("pT", [P, 2, 3 * P])
        neg_max, _ = place("neg_max", [P, T, AH])
        psum_p, _ = place("psum_p", [P, T, AH])
        inv_p, _ = place("inv_p", [P, T, AH])

        map_at[0] = shared
        h_hi, _ = place("h_hi", [P, T, D], F32R)
        h_lo, _ = place("h_lo", [P, T, D], F32R)
        xg_hi, _ = place("xg_hi", [P, KD, P], F32R)
        xg_lo, _ = place("xg_lo", [P, KD, P], F32R)
        act4, _ = place("act4", [P, BANK])
        hid4, _ = place("hid4", [P, BANK])
        gT_hi, _ = place("gT_hi", [P, 4, P], F32R)
        gT_lo, _ = place("gT_lo", [P, 4, P], F32R)
        y_hi, _ = place("y_hi", [P, D], F32R)
        y_lo, _ = place("y_lo", [P, D], F32R)
        sel, _ = place("sel", [P, T, P], F32R)
        selT, _ = place("selT", [P, T * P], F32R)
        logits, _ = place("logits", [P, T, EX])
        top, _ = place("top", [P, T, 8])
        top_i, _ = place("top_i", [P, T, 8], U32)
        top_f, _ = place("top_f", [P, T, 2])
        hot, _ = place("hot", [P, 2, T, EX])
        hot_w, _ = place("hot_w", [P, T, EX])
        member, _ = place("member", [P, T, EX])
        two, _ = place("two", [P, 4, T])
        slot_of, _ = place("slot_of", [P, T, 2 * EX + 1])
        gate_of, _ = place("gate_of", [P, T, 2 * EX + 1])
        most, _ = place("most", [P, 1])
        over, _ = place("over", [P, 1], I32)

        ps = ctx.enter_context(nc.psum_tensor("ps", [P, 8, BANK], F32))

        landed = [sem(f"landed{i}") for i in range(RAW)]
        hi_done = sem("hi_done")
        lo_done = sem("lo_done")
        unit_used = sem("unit_used")
        x_landed = sem("x_landed")
        gn_landed = [sem(f"gn_landed{i}") for i in range(RH)]
        ln_landed = [sem(f"ln_landed{i}") for i in range(4)]
        router_landed = sem("router_landed")
        stored = sem("stored")
        zeroed = sem("zeroed")
        tables = sem("tables")
        rel_ready = sem("rel_ready")
        decay_exp = sem("decay_exp")
        decay_ready = sem("decay_ready")
        filled = sem("filled")
        act_drained = sem("act_drained")
        dve_drained = sem("dve_drained")
        score_done = sem("score_done")
        att_ready = sem("att_ready")
        silu_g = sem("silu_g")
        ret_y = sem("ret_y")
        gn_var = sem("gn_var")
        gn_std = sem("gn_std")
        y_read = sem("y_read")
        norm_ready = sem("norm_ready")
        z_ready = sem("z_ready")
        zT_done = sem("zT_done")
        zT_hi_done = sem("zT_hi_done")
        zT_lo_done = sem("zT_lo_done")
        tile0_summed = sem("tile0_summed")
        ln_mean = sem("ln_mean")
        ln_square = sem("ln_square")
        ln_std = sem("ln_std")
        h_ready = sem("h_ready")
        f_silu = sem("f_silu")
        f_mul = sem("f_mul")
        fT_done = sem("fT_done")
        fT_hi_done = sem("fT_hi_done")
        fT_lo_done = sem("fT_lo_done")
        s_done = sem("s_done")
        max_ready = sem("max_ready")
        p_exp = sem("p_exp")
        p_ready = sem("p_ready")
        pT_done = sem("pT_done")
        scores_read = sem("scores_read")
        pT_act = sem("pT_act")
        pT_dve = sem("pT_dve")
        o_done = sem("o_done")
        oT_hi_done = sem("oT_hi_done")
        oT_lo_done = sem("oT_lo_done")
        router_split = sem("router_split")
        logit_done = sem("logit_done")
        gap_ready = sem("gap_ready")
        gap_exp = sem("gap_exp")
        member_ready = sem("member_ready")
        rank_done = sem("rank_done")
        over_ready = sem("over_ready")
        h_hi_done = sem("h_hi_done")
        h_split = sem("h_split")
        sel_ready = sem("sel_ready")
        gathered = sem("gathered")
        xg_hi_done = sem("xg_hi_done")
        xg_lo_done = sem("xg_lo_done")
        e_silu = sem("e_silu")
        e_mul = sem("e_mul")
        gT_done = sem("gT_done")
        gT_hi_done = sem("gT_hi_done")
        gT_lo_done = sem("gT_lo_done")
        y_hi_done = sem("y_hi_done")
        y_lo_done = sem("y_lo_done")
        selT_done = sem("selT_done")
        selT_ready = sem("selT_ready")
        scattered = sem("scattered")
        summed = sem("summed")
        dve_step = sem("dve_step")

        def number(u, r):
            return u + RAW * r

        def unit_done(eng, u, r):
            eng.wait_ge(unit_used, number(u + 1, r))

        def bank(n, k):
            return ps[:, n, :].rearrange("p (k n) -> p k n", k=k)

        def score_at(t, head):
            if t == 0:
                return ps[:, 6 + head // 4, (head % 4) * P:(head % 4 + 1) * P]
            return ps[:, T_BANKS[head // 2], (head % 2) * SEQ:(head % 2 + 1) * SEQ]

        def load_unit(sp, u, r, src, rows):
            if u >= RAW or not isinstance(r, int):
                sp.wait_ge(lo_done, number(u - RAW + 1, r))
            dst = raw[:, u % RAW, :].rearrange("p (k n) -> p k n", k=rows)
            sp.dma_start(dst, src).then_inc(landed[u % RAW], 16)

        def split_hi(act, u, r=0):
            act.wait_ge(landed[u % RAW], 16 * (u // RAW + 1) + 16 * r)
            if u >= SPLIT:
                act.wait_ge(unit_used, number(u - SPLIT + 1, r))
            nc.scalar.activation(whi[:, u % SPLIT, :], raw[:, u % RAW, :], ACT.Copy).then_inc(hi_done, 1)

        def split_lo(dve, u, r=0):
            dve.wait_ge(hi_done, number(u + 1, r))
            nc.vector.tensor_tensor(wlo[:, u % SPLIT, :], raw[:, u % RAW, :],
                                    whi[:, u % SPLIT, :].bitcast(F32), ALU.subtract).then_inc(lo_done, 1)

        def moe_source(i, e, b):
            if i < 4:
                b, part = 0, i
            elif i < JOB_UNITS - 2:
                part = (i - 4) % 6
            else:
                b, part = NEB, i - (JOB_UNITS - 2) + 4
            if part < 4:
                col = (part // 2) * EFF
                return moe_in[:, bass.ds(e * KD + 4 * (part % 2), 4), bass.ds(col + b * BANK, BANK)], 4
            return moe_out[:, bass.ds(e * (EFF // P) + (b - 1) * 4 + 2 * (part - 4), 2), :], 2

        block = ctx.enter_context(nc.Block())

        @block.sync
        def _(sp):
            for t in range(T):
                sp.dma_start(h[:, t, :], x_rows[:, t, :]).then_inc(x_landed, 16)

            def ret_in_units(r):
                for m in range(3):
                    for part in range(2):
                        load_unit(sp, U_RET_IN + 2 * m + part, r,
                                  ret_in[:, 4 * part:4 * part + 4, bass.ds((3 * r + m) * BANK, BANK)], 4)

            ret_in_units(0)
            with sp.Fori(1, RIN // BANK // 3) as r:
                ret_in_units(r)
            for i in range(VW // P // 2):
                load_unit(sp, U_RET_OUT + i, 0, ret_out[:, 2 * i:2 * i + 2, :], 2)

            def ffn_unit(u, r, part, b):
                if part < 2:
                    src, rows = ffn_in[:, 0:KD, bass.ds(part * FF + b * FB, FB)], KD
                else:
                    src, rows = ffn_out[:, bass.ds(2 * b, 2), :], 2
                load_unit(sp, u, r, src, rows)

            ffn_unit(U_FFN, 0, 0, 0)
            ffn_unit(U_FFN + 1, 0, 1, 0)
            with sp.Fori(0, NFB // 2) as r:
                for half in range(2):
                    u = U_FFN + 2 + 3 * half
                    ffn_unit(u, r, 0, 2 * r + 1 + half)
                    ffn_unit(u + 1, r, 1, 2 * r + 1 + half)
                    ffn_unit(u + 2, r, 2, 2 * r + half)
            ffn_unit(U_FFN + 3 * NFB - 1, 0, 2, NFB - 1)
            for m in range(6):
                for part in range(2):
                    w, col = ((kv_in, m * BANK), (q_in, (m - 2) * BANK), (kv_in, (m - 2) * BANK))[m // 2]
                    load_unit(sp, U_KVQ + 2 * m + part, 0, w[:, 4 * part:4 * part + 4, col:col + BANK], 4)
            for i in range(KD // 2):
                load_unit(sp, U_ATT_OUT + i, 0, att_out[:, 2 * i:2 * i + 2, :], 2)

            for i in range(AHEAD):
                load_unit(sp, U_MOE + i, 0, *moe_source(i, 0, 0))

            def job_loads(e, e_next, j):
                load_unit(sp, U_MOE + 3, NEB * j, *moe_source(3, e, 0))
                with sp.Fori(1, NEB) as b:
                    for i in range(4, 10):
                        load_unit(sp, U_MOE + i - 6, NEB * j + b, *moe_source(i, e, b))
                for i in (JOB_UNITS - 2, JOB_UNITS - 1):
                    load_unit(sp, U_MOE + i, NEB * j, *moe_source(i, e, 0))
                for i in range(AHEAD):
                    load_unit(sp, U_MOE + JOB_UNITS + i, NEB * j, *moe_source(i, e_next, 0))

            def pass_loads(first):
                with sp.Fori(0, EX - 1) as e:
                    job_loads(e, e + 1, e + first)
                job_loads(EX - 1, 0, EX - 1 + first)

            pass_loads(0)
            sp.wait_ge(over_ready, 1)
            more = sp.value_load(over[0:1, 0:1], min_val=0, max_val=1)
            with sp.If(more > 0):
                pass_loads(EX)
            for t in range(T):
                sp.wait_ge(h_ready, 6 + t + 1)
                sp.dma_start(out_rows[:, t, :], h[:, t, :]).then_inc(stored, 16)
            sp.wait_ge(stored, 16 * T)

        @block.gpsimd
        def _(pool):
            def load_gn(head):
                cols = slice(head * DV, (head + 1) * DV)
                for n, w in enumerate((ret_gn_g, ret_gn_b)):
                    pool.dma_start(gn[:, head % 2, n, :], w[0:1, cols].partition_broadcast(P)
                                   ).then_inc(gn_landed[head], 16)

            def load_ln(n):
                for k, w in enumerate((ln_g, ln_b)):
                    pool.dma_start(ln_gb[:, k, :], w[n // 2:n // 2 + 1, n % 2, :].partition_broadcast(P)
                                   ).then_inc(ln_landed[n], 16)

            pool.memset(ident[:, :], 0.0).then_inc(zeroed, 1)
            pool.memset(eps[:, 0:1], LN_EPS).then_inc(zeroed, 1)
            pool.memset(eps[:, 1:2], GN_EPS).then_inc(zeroed, 1)
            pool.wait_ge(zeroed, 3)
            pool.affine_select(out=ident[:, :], in_=ident[:, :], compare_op=ALU.not_equal, fill=1.0, base=0,
                               pattern=[[-1, P]], channel_multiplier=1).then_inc(tables, 1)
            pool.iota(decay[:, :, :], pattern=[[0, RH], [1, SEQ]], base=0, channel_multiplier=-1,
                      allow_small_or_imprecise_dtypes=True).then_inc(rel_ready, 1)
            pool.dma_start(router[:, :, :], router_in).then_inc(router_landed, 16)
            load_gn(0)
            load_gn(1)
            pool.wait_ge(decay_exp, RH)
            pool.affine_select(out=decay[:, :, :], in_=decay[:, :, :], compare_op=ALU.is_ge, fill=0.0, base=0,
                               pattern=[[0, RH], [1, SEQ]], channel_multiplier=-1).then_inc(decay_ready, 1)
            for head in range(RH):
                for t in range(T):
                    pool.wait_ge(norm_ready, T * head + t + 1)
                    pool.wait_ge(silu_g, head + 1)
                    g = gated[:, head, t, :]
                    pool.tensor_tensor(g, g, normed[:, t, :], ALU.mult).then_inc(z_ready, 1)
                if head + 2 < RH:
                    load_gn(head + 2)
            pool.wait_ge(score_done, RH)
            load_ln(0)
            pool.memset(ones[:, :], 1.0).then_inc(zeroed, 1)
            pool.wait_ge(zeroed, 4)
            pool.affine_select(out=before[:, :], in_=ones[:, :], compare_op=ALU.is_gt, fill=0.0, base=0,
                               pattern=[[1, P]], channel_multiplier=-1).then_inc(tables, 1)
            pool.iota(iota_slot[:, :], pattern=[[1, P]], base=0, channel_multiplier=0,
                      allow_small_or_imprecise_dtypes=True).then_inc(tables, 1)
            for t in range(T):
                pool.iota(past[:, t, :], pattern=[[-1, SEQ]], base=t * P, channel_multiplier=1,
                          allow_small_or_imprecise_dtypes=True).then_inc(zeroed, 1)
            pool.wait_ge(zeroed, 6)
            for t in range(T):
                pool.affine_select(out=past[:, t, :], in_=past[:, t, :], compare_op=ALU.is_ge, fill=NEVER,
                                   base=t * P, pattern=[[-1, SEQ]], channel_multiplier=1).then_inc(tables, 1)
            for n in (1, 2, 3):
                pool.wait_ge(h_ready, T * n)
                load_ln(n)

        @block.scalar
        def _(act):
            def drain_xT(n, t):
                for g in (2 * t, 2 * t + 1):
                    c = 4 * (g % 2)
                    act.wait_ge(filled, FILLED_XT[n] + g + 1)
                    nc.scalar.activation(xT_hi[:, c:c + 4, t * P:(t + 1) * P], bank(6 + g % 2, 4),
                                         ACT.Copy).then_inc(act_drained, 1)

            def drain_block(u, r, dst, at):
                unit_done(act, u, r)
                nc.scalar.activation(dst, ps[:, at, :], ACT.Copy).then_inc(act_drained, 1)

            def drain_qk(n, groups, dst, scale):
                for g in groups:
                    act.wait_ge(filled, FILLED_QK[n] + g + 1)
                    nc.scalar.activation(dst[:, 4 * (g // 2):4 * (g // 2) + 4, 0:P], bank(T_BANKS[g % 4], 4),
                                         ACT.Copy, scale=scale).then_inc(act_drained, 1)

            def drain_zT_hi(n):
                head, t = n // T, n % T
                act.wait_ge(zT_done, n + 1)
                nc.scalar.activation(zT_hi[:, 4 * head:4 * head + 4, t * P:(t + 1) * P], bank(7, 4),
                                     ACT.Copy).then_inc(zT_hi_done, 1)

            def norm_std(n, t):
                act.wait_ge(ln_mean, T * n + t + 1)
                nc.scalar.activation(ps[:, 2 + 2 * t:4 + 2 * t, :].rearrange("p b n -> p (b n)"), h[:, t, :],
                                     ACT.Square, bias=neg_mean[:, t:t + 1],
                                     accum_out=square_sum[:, t:t + 1]).then_inc(ln_square, 1)
                act.wait_ge(ln_square, T * n + t + 1)
                nc.scalar.activation(std[:, t:t + 1], square_sum[:, t:t + 1], ACT.Sqrt, scale=1.0 / D,
                                     bias=eps[:, 0:1]).then_inc(ln_std, 1)

            def norm_between(n, u):
                norm_std(n, 0)
                if n != 1:
                    split_hi(act, u)
                    split_hi(act, u + 1)
                norm_std(n, 1)
                drain_xT(n + 1, 0)
                split_hi(act, u + 2)
                drain_xT(n + 1, 1)

            def exps(t):
                act.wait_ge(max_ready, T - t)
                w = P * (t + 1)
                for head in range(AH):
                    nc.scalar.activation(prob[:, t, head, 0:w], prob[:, t, head, 0:w], ACT.Exp,
                                         bias=neg_max[:, t, head:head + 1],
                                         accum_out=psum_p[:, t, head:head + 1]).then_inc(p_exp, 1)

            act.wait_ge(rel_ready, 1)
            for head in range(RH):
                nc.scalar.activation(decay[:, head, :], decay[:, head, :], ACT.Exp,
                                     scale=math.log1p(-2.0 ** (-5 - head))).then_inc(decay_exp, 1)
            split_hi(act, 0)
            drain_xT(0, 0)
            drain_xT(0, 1)
            for u in range(1, AHEAD):
                split_hi(act, u)
            act.wait_ge(router_landed, 16)
            nc.scalar.activation(router_hi[:, :, :], router[:, :, :], ACT.Copy).then_inc(router_split, 1)
            with act.Fori(0, LOOPED // 3) as r:
                for m in range(3):
                    u = U_RET_IN + 2 * m
                    split_hi(act, u + AHEAD, r)
                    drain_block(u + 1, r, rows_flat[:, bass.ds((3 * r + m) * T * BANK, BANK)], PROJ_BANKS[m][0])
                    split_hi(act, u + 1 + AHEAD, r)
            drain_qk(0, (0, 2), qkT, 1.0)
            for s in range(2 * (3 * RH - LOOPED)):
                u, c = U_RET_IN + 2 * LOOPED + s, LOOPED + s // 2
                if s % 2 == 1 and c < QKV:
                    drain_block(u, 0, rows[:, c, 0, :], 2 + 2 * (c % 2))
                elif s % 2 == 1:
                    unit_done(act, u, 0)
                    nc.scalar.activation(gated[:, c - QKV, :, :], ps[:, 2 + 2 * (c % 2):4 + 2 * (c % 2), :],
                                         ACT.Silu).then_inc(silu_g, 1)
                if s >= 6:
                    drain_zT_hi(s - 6)
                split_hi(act, u + AHEAD)
                if s == 0:
                    drain_qk(0, (4, 6), qkT, 1.0)
                if s >= 2 and s % 2 == 0 and (s - 2) // 2 < RH:
                    act.wait_ge(gn_var, T * ((s - 2) // 2 + 1))
                    nc.scalar.activation(gstd[:, :], gmv[:, :, 1], ACT.Sqrt, bias=eps[:, 1:2]).then_inc(gn_std, 1)
            for u in range(U_RET_OUT, U_FFN - AHEAD):
                if u < U_RET_OUT + T:
                    drain_zT_hi(T * (RH - 1) + u - U_RET_OUT)
                split_hi(act, u + AHEAD)
            norm_between(0, U_FFN)

            def silu_block(*u_up):
                unit_done(act, *u_up)
                nc.scalar.activation(act2[:, :, :], ps[:, 0:2, 0:FB], ACT.Silu).then_inc(f_silu, 1)

            def drain_fT(b):
                act.wait_ge(fT_done, b + 1)
                nc.scalar.activation(fT_hi[:, :, :], bank(6, 2), ACT.Copy).then_inc(fT_hi_done, 1)

            split_hi(act, U_FFN + AHEAD)
            silu_block(U_FFN + 1, 0)
            split_hi(act, U_FFN + 1 + AHEAD)
            with act.Fori(0, NFB // 2) as r:
                for half in range(2):
                    u = U_FFN + 2 + 3 * half + AHEAD
                    split_hi(act, u, r)
                    drain_fT(2 * r + half)
                    split_hi(act, u + 1, r)
                    silu_block(U_FFN + 3 + 3 * half, r)
                    split_hi(act, u + 2, r)
            drain_fT(NFB - 1)
            norm_between(1, U_KVQ)
            for s in range(12):
                u, c = U_KVQ + s, s // 2
                if s % 2 == 1:
                    drain_block(u, 0, kvq[:, c, 0, :], 2 + 2 * (c % 2))
                if s == 5:
                    drain_qk(1, (0, 2), kqT, 1.0)
                split_hi(act, u + AHEAD)
                if s == 8:
                    drain_qk(1, (4, 6), kqT, P ** -0.5)
                if s == 10:
                    exps(1)
            exps(0)
            for head in range(AH):
                if head % 2 == 0:
                    act.wait_ge(pT_done, head + 1)
                    nc.scalar.activation(pT[:, 0, :], ps[:, 6, 0:3 * P], ACT.Copy).then_inc(pT_act, 1)
                else:
                    pair = head // 2
                    act.wait_ge(o_done, pair + 1)
                    nc.scalar.activation(xT_hi[:, head - 1:head + 1, :], bank(pair % 2, 2),
                                         ACT.Copy).then_inc(oT_hi_done, 1)
                if head == 4:
                    split_hi(act, U_ATT_OUT + AHEAD)
            norm_between(2, U_MOE)
            act.wait_ge(h_ready, T * 3)
            nc.scalar.activation(h_hi[:, :, :], h[:, :, :], ACT.Copy).then_inc(h_hi_done, 1)
            act.wait_ge(gap_ready, 1)
            nc.scalar.activation(two[:, 1, :], two[:, 0, :], ACT.Exp).then_inc(gap_exp, 1)

            def drain_xg(j):
                act.wait_ge(gathered, j + 1)
                nc.scalar.activation(xg_hi[:, :, :].rearrange("p k n -> p (k n)"),
                                     ps[:, 4:6, :].rearrange("p b n -> p (b n)"), ACT.Copy).then_inc(xg_hi_done, 1)

            def silu_e(u_gate, r):
                unit_done(act, u_gate, r)
                nc.scalar.activation(act4[:, :], ps[:, 0, :], ACT.Silu).then_inc(e_silu, 1)

            def drain_gT(n):
                act.wait_ge(gT_done, n + 1)
                nc.scalar.activation(gT_hi[:, :, :], bank(6, 4), ACT.Copy).then_inc(gT_hi_done, 1)

            def job(j):
                split_hi(act, U_MOE + 3, NEB * j)
                silu_e(U_MOE + 1, NEB * j)
                split_hi(act, U_MOE + 4, NEB * j)
                split_hi(act, U_MOE + 5, NEB * j)
                split_hi(act, U_MOE + 6, NEB * j)
                act.wait_ge(selT_done, j + 1)
                nc.scalar.activation(selT[:, :], ps[:, 7, 0:T * P], ACT.Copy).then_inc(selT_ready, 1)
                with act.Fori(1, NEB) as b:
                    n = NEB * j + b
                    u = U_MOE - 2 + AHEAD
                    split_hi(act, u, n)
                    act.wait_ge(e_mul, n)
                    silu_e(U_MOE - 1, n)
                    drain_gT(n - 1)
                    for k in range(1, 6):
                        split_hi(act, u + k, n)
                drain_gT(NEB * j + NEB - 1)
                drain_xg(j + 1)
                split_hi(act, U_MOE + JOB_UNITS - 2 + AHEAD, NEB * j)
                unit_done(act, U_MOE + JOB_UNITS - 1, NEB * j)
                nc.scalar.activation(y_hi[:, :], ps[:, 2:4, :].rearrange("p b n -> p (b n)"), ACT.Copy).then_inc(y_hi_done, 1)
                split_hi(act, U_MOE + JOB_UNITS - 1 + AHEAD, NEB * j)

            drain_xg(0)
            with act.Fori(0, EX) as j:
                job(j)
            act.wait_ge(over_ready, 1)
            more = act.value_load(over[0:1, 0:1], min_val=0, max_val=1)
            with act.If(more > 0):
                with act.Fori(EX, 2 * EX) as j:
                    job(j)
            for t in range(T):
                norm_std(3, t)

        @block.vector
        def _(dve):
            step = [0]

            def then(ins):
                step[0] += 1
                ins.then_inc(dve_step, 1)
                dve.wait_ge(dve_step, step[0])

            def lo_of(dst, src, hi):
                return nc.vector.tensor_tensor(dst, src, hi.bitcast(F32), ALU.subtract)

            def drain_xT(n, t):
                for g in (2 * t, 2 * t + 1):
                    c = 4 * (g % 2)
                    dve.wait_ge(act_drained, DR_XT[n] + g + 1)
                    lo_of(xT_lo[:, c:c + 4, t * P:(t + 1) * P], bank(6 + g % 2, 4),
                          xT_hi[:, c:c + 4, t * P:(t + 1) * P]).then_inc(dve_drained, 1)

            def drain_block(u, r, dst, at):
                unit_done(dve, u, r)
                nc.vector.tensor_copy(dst, ps[:, at, :]).then_inc(dve_drained, 1)

            def drain_qk(n, groups, dst, scale):
                for g in groups:
                    dve.wait_ge(filled, FILLED_QK[n] + g + 1)
                    nc.vector.tensor_scalar(dst[:, 4 * (g // 2):4 * (g // 2) + 4, P:2 * P],
                                            bank(T_BANKS[g % 4], 4), scale, None, ALU.mult).then_inc(dve_drained, 1)

            def norm_mean(n, t):
                if n < 3:
                    if t == 0:
                        dve.wait_ge(tile0_summed, n + 1)
                    else:
                        unit_done(dve, LAST_SUM[n], 0)
                    then(nc.vector.scalar_tensor_tensor(out=h[:, t, :], in0=h[:, t, :], scalar=ALPHA,
                                                        in1=ps[:, 2 + 2 * t:4 + 2 * t, :].rearrange("p b n -> p (b n)"),
                                                        op0=ALU.mult, op1=ALU.add, accum_out=row_sum[:, t:t + 1]))
                nc.vector.tensor_scalar(neg_mean[:, t:t + 1], row_sum[:, t:t + 1], -1.0 / D, None,
                                        ALU.mult).then_inc(ln_mean, 1)

            def norm_end(n, t):
                if t == 0:
                    dve.wait_ge(ln_landed[n], 32)
                dve.wait_ge(ln_std, T * n + t + 1)
                then(nc.vector.reciprocal(rstd[:, t:t + 1], std[:, t:t + 1]))
                then(nc.vector.scalar_tensor_tensor(out=h[:, t, :], in0=h[:, t, :], scalar=neg_mean[:, t:t + 1],
                                                    in1=ln_gb[:, 0, :], op0=ALU.add, op1=ALU.mult))
                nc.vector.scalar_tensor_tensor(out=h[:, t, :], in0=h[:, t, :], scalar=rstd[:, t:t + 1],
                                               in1=ln_gb[:, 1, :], op0=ALU.mult, op1=ALU.add).then_inc(h_ready, 1)

            def norm_between(n, u):
                norm_mean(n, 0)
                norm_end(n, 0)
                if n != 1:
                    split_lo(dve, u)
                norm_mean(n, 1)
                drain_xT(n + 1, 0)
                if n != 1:
                    split_lo(dve, u + 1)
                norm_end(n, 1)
                split_lo(dve, u + 2)
                drain_xT(n + 1, 1)

            split_lo(dve, 0)
            drain_xT(0, 0)
            drain_xT(0, 1)
            for u in range(1, AHEAD):
                split_lo(dve, u)
            dve.wait_ge(router_split, 1)
            nc.vector.tensor_tensor(router_lo[:, :, :], router[:, :, :], router_hi[:, :, :].bitcast(F32),
                                    ALU.subtract).then_inc(router_split, 1)
            with dve.Fori(0, LOOPED // 3) as r:
                for m in range(3):
                    u = U_RET_IN + 2 * m
                    split_lo(dve, u + AHEAD, r)
                    drain_block(u + 1, r, rows_flat[:, bass.ds((3 * r + m) * T * BANK + BANK, BANK)],
                                PROJ_BANKS[m][1])
                    split_lo(dve, u + 1 + AHEAD, r)

            def decayed(head):
                dve.wait_ge(score_done, head + 1)
                if head == 0:
                    dve.wait_ge(decay_ready, 1)
                if head >= 1:
                    dve.wait_ge(ret_y, T * head)
                for a, b, c in ((0, SEQ, 0), (SEQ, SEQ + P, 0)):
                    nc.vector.scalar_tensor_tensor(out=attT[:, head % 2, a:b], in0=ps[:, 6, a:b],
                                                   scalar=256.0 ** -0.5, in1=decay[:, head, c:c + b - a],
                                                   op0=ALU.mult, op1=ALU.mult).then_inc(att_ready, 1)

            def group_stats(head):
                for t in range(T):
                    dve.wait_ge(ret_y, T * head + t + 1)
                    then(nc.vector.bn_stats(gstats[:, t, :], ps[:, t, :]))
                    nc.vector.bn_aggr(gmv[:, t, :], gstats[:, t, :]).then_inc(gn_var, 1)

            def group_norm(head):
                dve.wait_ge(gn_std, head + 1)
                then(nc.vector.reciprocal(grstd[:, :], gstd[:, :]))
                dve.wait_ge(gn_landed[head], 32)
                for t in range(T):
                    if head >= 1:
                        dve.wait_ge(z_ready, T * (head - 1) + t + 1)
                    nc.vector.scalar_tensor_tensor(out=normed[:, t, :], in0=ps[:, t, :],
                                                   scalar=gmv[:, t, 0:1], in1=gn[:, head % 2, 0, :],
                                                   op0=ALU.subtract, op1=ALU.mult).then_inc(y_read, 1)
                    dve.wait_ge(y_read, T * head + t + 1)
                    nc.vector.scalar_tensor_tensor(out=normed[:, t, :], in0=normed[:, t, :],
                                                   scalar=grstd[:, t:t + 1], in1=gn[:, head % 2, 1, :],
                                                   op0=ALU.mult, op1=ALU.add).then_inc(norm_ready, 1)

            def drain_zT_lo(n):
                head, t = n // T, n % T
                dve.wait_ge(zT_hi_done, n + 1)
                lo_of(zT_lo[:, 4 * head:4 * head + 4, t * P:(t + 1) * P], bank(7, 4),
                      zT_hi[:, 4 * head:4 * head + 4, t * P:(t + 1) * P]).then_inc(zT_lo_done, 1)

            drain_qk(0, (1, 3), qkT, 1.0)
            for s in range(2 * (3 * RH - LOOPED)):
                u, c = U_RET_IN + 2 * LOOPED + s, LOOPED + s // 2
                head = (s - 2) // 2
                if s % 2 == 1 and c < QKV:
                    drain_block(u, 0, rows[:, c, 1, :], 3 + 2 * (c % 2))
                if s == 1:
                    decayed(0)
                if s >= 2 and s % 2 == 0 and head < RH:
                    group_stats(head)
                    if head + 1 < RH:
                        decayed(head + 1)
                if s >= 6:
                    drain_zT_lo(s - 6)
                split_lo(dve, u + AHEAD)
                if s == 0:
                    drain_qk(0, (5, 7), qkT, 1.0)
                if s >= 2 and s % 2 == 0 and head < RH:
                    group_norm(head)
            for u in range(U_RET_OUT, U_FFN - AHEAD):
                if u < U_RET_OUT + T:
                    drain_zT_lo(T * (RH - 1) + u - U_RET_OUT)
                split_lo(dve, u + AHEAD)
            norm_between(0, U_FFN)

            def mul_block(b):
                dve.wait_ge(f_silu, b + 1)
                nc.vector.tensor_tensor(hid2[:, :, :], act2[:, :, :], ps[:, 0:2, FB:2 * FB], ALU.mult).then_inc(f_mul, 1)

            def drain_fT(b):
                dve.wait_ge(fT_hi_done, b + 1)
                lo_of(fT_lo[:, :, :], bank(6, 2), fT_hi[:, :, :]).then_inc(fT_lo_done, 1)

            split_lo(dve, U_FFN + AHEAD)
            mul_block(0)
            split_lo(dve, U_FFN + 1 + AHEAD)
            with dve.Fori(0, NFB // 2) as r:
                for half in range(2):
                    u = U_FFN + 2 + 3 * half + AHEAD
                    split_lo(dve, u, r)
                    drain_fT(2 * r + half)
                    split_lo(dve, u + 1, r)
                    mul_block(2 * r + half + 1)
                    split_lo(dve, u + 2, r)
            drain_fT(NFB - 1)
            norm_between(1, U_KVQ)

            def scores(t):
                w = P * (t + 1)
                dve.wait_ge(s_done, T - t)
                for head in range(AH):
                    ins = nc.vector.scalar_tensor_tensor(out=prob[:, t, head, 0:w], in0=past[:, t, 0:w],
                                                         scalar=-2.0 ** (-8.0 / AH * (head + 1)),
                                                         in1=score_at(t, head), op0=ALU.mult, op1=ALU.add)
                ins.then_inc(scores_read, 1)
                dve.wait_ge(scores_read, T - t)
                nc.vector.tensor_reduce(neg_max[:, t, :], prob[:, t, :, 0:w], AX.X, ALU.max,
                                        negate=True).then_inc(max_ready, 1)

            def probabilities(t):
                w = P * (t + 1)
                dve.wait_ge(p_exp, AH * (T - t))
                then(nc.vector.reciprocal(inv_p[:, t, :], psum_p[:, t, :]))
                for head in range(AH):
                    nc.vector.tensor_scalar(prob[:, t, head, 0:w], prob[:, t, head, 0:w],
                                            inv_p[:, t, head:head + 1], None, ALU.mult).then_inc(p_ready, 1)

            dve.wait_ge(tables, 5)
            for s in range(12):
                u, c = U_KVQ + s, s // 2
                if s % 2 == 1:
                    drain_block(u, 0, kvq[:, c, 1, :], 3 + 2 * (c % 2))
                if s == 5:
                    drain_qk(1, (1, 3), kqT, 1.0)
                split_lo(dve, u + AHEAD)
                if s == 8:
                    drain_qk(1, (5, 7), kqT, P ** -0.5)
                if s == 9:
                    scores(1)
                if s == 10:
                    scores(0)
                    probabilities(1)
            probabilities(0)
            for head in range(AH):
                if head % 2 == 1:
                    pair = head // 2
                    dve.wait_ge(pT_done, head + 1)
                    nc.vector.tensor_copy(pT[:, 1, :], ps[:, 7, 0:3 * P]).then_inc(pT_dve, 1)
                    dve.wait_ge(oT_hi_done, pair + 1)
                    lo_of(xT_lo[:, head - 1:head + 1, :], bank(pair % 2, 2),
                          xT_hi[:, head - 1:head + 1, :]).then_inc(oT_lo_done, 1)
                elif head == 4:
                    split_lo(dve, U_ATT_OUT + AHEAD)
            norm_between(2, U_MOE)
            dve.wait_ge(h_hi_done, 1)
            nc.vector.tensor_tensor(h_lo[:, :, :], h[:, :, :], h_hi[:, :, :].bitcast(F32),
                                    ALU.subtract).then_inc(h_split, 1)
            nc.vector.tensor_scalar(h[:, :, :], h[:, :, :], ALPHA, None, ALU.mult).then_inc(dve_step, 1)
            step[0] += 1
            nc.vector.memset(y_hi[:, :].bitcast(F32), 0.0).then_inc(dve_step, 1)
            nc.vector.memset(y_lo[:, :].bitcast(F32), 0.0).then_inc(y_lo_done, 1)
            nc.vector.memset(selT[:, :].bitcast(F32), 0.0).then_inc(selT_ready, 1)
            nc.vector.memset(gate_of[:, :, 0:1], 0.0).then_inc(dve_step, 1)
            nc.vector.memset(slot_of[:, :, 2 * EX:2 * EX + 1], -1.0).then_inc(dve_step, 1)
            step[0] += 3
            dve.wait_ge(logit_done, 1)
            then(nc.vector.tensor_copy(logits[:, :, :], ps[:, 0, 0:T * EX].rearrange("p (t e) -> p t e", t=T)))
            for t in range(T):
                then(nc.vector.max(top[:, t, :], logits[:, t, :]))
                then(nc.vector.max_index(top_i[:, t, :], top[:, t, :], logits[:, t, :]))
            nc.vector.tensor_tensor(two[:, 0, :], top[:, :, 1], top[:, :, 0], ALU.subtract).then_inc(gap_ready, 1)
            then(nc.vector.tensor_copy(top_f[:, :, :], top_i[:, :, 0:2]))
            for k in range(2):
                for t in range(T):
                    then(nc.vector.tensor_scalar(hot[:, k, t, :], iota_slot[:, 0:EX], top_f[:, t, k:k + 1], None,
                                                 ALU.is_equal))
            nc.vector.tensor_tensor(member[:, :, :], hot[:, 0, :, :], hot[:, 1, :, :], ALU.add).then_inc(member_ready, 1)
            dve.wait_ge(gap_exp, 1)
            then(nc.vector.tensor_scalar(two[:, 2, :], two[:, 1, :], 1.0, None, ALU.add))
            then(nc.vector.reciprocal(two[:, 2, :], two[:, 2, :]))
            then(nc.vector.tensor_tensor(two[:, 3, :], two[:, 1, :], two[:, 2, :], ALU.mult))
            for t in range(T):
                then(nc.vector.tensor_scalar(hot_w[:, t, :], hot[:, 1, t, :], two[:, 3, t:t + 1], None, ALU.mult))
                for k in range(2):
                    then(nc.vector.scalar_tensor_tensor(out=gate_of[:, t, 1 + k * EX:1 + (k + 1) * EX],
                                                        in0=hot[:, 0, t, :], scalar=two[:, 2, t:t + 1],
                                                        in1=hot_w[:, t, :], op0=ALU.mult, op1=ALU.add))
            dve.wait_ge(rank_done, 1)
            for t in range(T):
                then(nc.vector.scalar_tensor_tensor(out=slot_of[:, t, 0:EX], in0=ps[:, 6, t * EX:(t + 1) * EX],
                                                    scalar=1.0, in1=member[:, t, :], op0=ALU.add, op1=ALU.mult))
            then(nc.vector.tensor_scalar(slot_of[:, :, 0:EX], slot_of[:, :, 0:EX], -1.0, None, ALU.add))
            then(nc.vector.tensor_scalar(slot_of[:, :, EX:2 * EX], slot_of[:, :, 0:EX], -float(P), None, ALU.add))
            then(nc.vector.tensor_reduce(most[:, :], ps[:, 6, T * EX:(T + 1) * EX], AX.X, ALU.max))
            nc.vector.tensor_scalar(over[:, :], most[:, :], float(P), None, ALU.is_gt).then_inc(over_ready, 1)

            def select(j):
                for t in range(T):
                    ins = nc.vector.tensor_scalar(sel[:, t, :], iota_slot[:, :], slot_of[:, t, bass.ds(j, 1)], None,
                                                  ALU.is_equal)
                ins.then_inc(sel_ready, 1)

            def drain_xg(j):
                dve.wait_ge(gathered, j + 1)
                nc.vector.tensor_copy(xg_lo[:, :, :].rearrange("p k n -> p (k n)"),
                                      ps[:, 0:2, :].rearrange("p b n -> p (b n)")).then_inc(xg_lo_done, 1)

            def mul_e(n, u_up, r):
                unit_done(dve, u_up, r)
                dve.wait_ge(e_silu, n + 1)
                nc.vector.tensor_tensor(hid4[:, :], act4[:, :], ps[:, 1, :], ALU.mult).then_inc(e_mul, 1)

            def drain_gT(n):
                dve.wait_ge(gT_hi_done, n + 1)
                lo_of(gT_lo[:, :, :], bank(6, 4), gT_hi[:, :, :]).then_inc(gT_lo_done, 1)

            def add_scattered(j, t, row_sums=None):
                dve.wait_ge(scattered, T * j + t + 1)
                nc.vector.scalar_tensor_tensor(out=h[:, t, :], in0=ps[:, 4:6, :].rearrange("p b n -> p (b n)"),
                                               scalar=gate_of[:, t, bass.ds(j, 1)], in1=h[:, t, :],
                                               op0=ALU.mult, op1=ALU.add, accum_out=row_sums).then_inc(summed, 1)

            def job(j):
                split_lo(dve, U_MOE + 3, NEB * j)
                add_scattered(j, 0)
                split_lo(dve, U_MOE + 4, NEB * j)
                split_lo(dve, U_MOE + 5, NEB * j)
                mul_e(NEB * j, U_MOE + 3, NEB * j)
                split_lo(dve, U_MOE + 6, NEB * j)
                add_scattered(j, 1)
                dve.wait_ge(selT_done, j + 1)
                select(j + 1)
                with dve.Fori(1, NEB) as b:
                    n = NEB * j + b
                    u = U_MOE - 2 + AHEAD
                    split_lo(dve, u, n)
                    split_lo(dve, u + 1, n)
                    drain_gT(n - 1)
                    split_lo(dve, u + 2, n)
                    mul_e(n, U_MOE + 1, n)
                    for k in range(3, 6):
                        split_lo(dve, u + k, n)
                drain_gT(NEB * j + NEB - 1)
                drain_xg(j + 1)
                split_lo(dve, U_MOE + JOB_UNITS - 2 + AHEAD, NEB * j)
                dve.wait_ge(y_hi_done, j + 1)
                lo_of(y_lo[:, :], ps[:, 2:4, :].rearrange("p b n -> p (b n)"), y_hi[:, :]).then_inc(y_lo_done, 1)
                split_lo(dve, U_MOE + JOB_UNITS - 1 + AHEAD, NEB * j)

            select(0)
            drain_xg(0)
            with dve.Fori(0, EX) as j:
                job(j)
            dve.wait_ge(over_ready, 1)
            more = dve.value_load(over[0:1, 0:1], min_val=0, max_val=1)
            with dve.If(more > 0):
                with dve.Fori(EX, 2 * EX) as j:
                    job(j)
            jobs = EX + EX * more
            for t in range(T):
                add_scattered(jobs, t, row_sum[:, t:t + 1])
                dve.wait_ge(summed, T * jobs + t + 1)
                norm_mean(3, t)
            for t in range(T):
                norm_end(3, t)

        @block.tensor
        def _(pe):
            def passes(dst, a_hi, a_lo, b_hi, b_lo, start, stop):
                pe.matmul(dst, a_hi, b_hi, start=start, stop=False, skip_group_check=True)
                pe.matmul(dst, a_hi, b_lo, start=False, stop=False, skip_group_check=True)
                return pe.matmul(dst, a_lo, b_hi, start=False, stop=stop, skip_group_check=True)

            def unit_ready(u, r=0):
                pe.wait_ge(lo_done, number(u + 1, r))

            def transposes_x(n, t):
                if n == 0:
                    pe.wait_ge(x_landed, 16 * T)
                    pe.wait_ge(tables, 1)
                else:
                    pe.wait_ge(h_ready, T * (n - 1) + t + 1)
                if t == 1:
                    pe.wait_ge(dve_drained, DR_XT[n] + 2)
                for g in range(2):
                    for k in range(4):
                        last = pe.transpose(ps[:, 6 + g, k * P:(k + 1) * P],
                                            h[:, t, (4 * g + k) * P:(4 * g + k + 1) * P], ident[:, :])
                    last.then_inc(filled, 1)

            def xT_ready(n, t):
                pe.wait_ge(dve_drained, DR_XT[n] + 2 * t + 2)

            def project_tile(u, part, t, at):
                tok = slice(t * P, (t + 1) * P)
                for c in range(4):
                    k = 4 * part + c
                    w = slice(c * BANK, (c + 1) * BANK)
                    last = passes(ps[:, at, :], xT_hi[:, k, tok], xT_lo[:, k, tok],
                                  whi[:, u % SPLIT, w], wlo[:, u % SPLIT, w], k == 0, k == KD - 1)
                return last

            def project_unit(u, r, part, banks):
                unit_ready(u, r)
                project_tile(u, part, 0, banks[0])
                project_tile(u, part, 1, banks[1]).then_inc(unit_used, 1)

            def transposes_qk(n, src, blocks, groups):
                for g in groups:
                    if g >= 4:
                        pe.wait_ge((act_drained, dve_drained)[g % 2], QK_GROUP_DRAINED[n] + (g - 4) // 2)
                    for k in range(4):
                        last = pe.transpose(ps[:, T_BANKS[g % 4], k * P:(k + 1) * P],
                                            src[:, blocks[g // 2], g % 2, k * P:(k + 1) * P], ident[:, :])
                    last.then_inc(filled, 1)

            def drained(n):
                pe.wait_ge(act_drained, n)
                pe.wait_ge(dve_drained, n)

            def out_product(u, r, a_hi, a_lo, first, last_k):
                unit_ready(u, r)
                for t in range(T):
                    last = out_product_tile(u, t, a_hi, a_lo, first, last_k)
                last.then_inc(unit_used, 1)

            def out_product_tile(u, t, a_hi, a_lo, first, last_k):
                tok = slice(t * P, (t + 1) * P)
                for c in range(2):
                    for half in range(2):
                        w = slice((2 * c + half) * BANK, (2 * c + half + 1) * BANK)
                        last = passes(ps[:, 2 + 2 * t + half, :], a_hi[:, c, tok], a_lo[:, c, tok],
                                      whi[:, u % SPLIT, w], wlo[:, u % SPLIT, w],
                                      first and c == 0, last_k and c == 1)
                return last

            def out_product_end(units, chunks):
                for t in range(T):
                    for u, (a_hi, a_lo) in zip(units, chunks):
                        if t == 0:
                            unit_ready(u)
                        last = out_product_tile(u, t, a_hi, a_lo, False, u == units[-1])
                        if t == 1:
                            last.then_inc(unit_used, 1)
                    if t == 0:
                        last.then_inc(tile0_summed, 1)

            for t in range(T):
                transposes_x(0, t)
                xT_ready(0, t)
            with pe.Fori(0, LOOPED // 3) as r:
                for m in range(3):
                    pe.wait_ge(act_drained, DR_PROJ[0] - 2 + m + 3 * r)
                    pe.wait_ge(dve_drained, DR_PROJ[0] - 2 + m + 3 * r)
                    for part in range(2):
                        project_unit(U_RET_IN + 2 * m + part, r, part, PROJ_BANKS[m])

            def ret_scores(head):
                q, k = 2 * head, KD + 2 * head
                for c in range(2):
                    pe.matmul(ps[:, 6, 0:SEQ], qkT[:, k + c, 0:P], qkT[:, q + c, :],
                              start=(c == 0), stop=(c == 1))
                for c in range(2):
                    last = pe.matmul(ps[:, 6, SEQ:SEQ + P], qkT[:, k + c, P:SEQ], qkT[:, q + c, P:SEQ],
                                     start=(c == 0), stop=(c == 1))
                last.then_inc(score_done, 1)

            def ret_values(head):
                pe.wait_ge(att_ready, 2 * (head + 1))
                if head >= 1:
                    pe.wait_ge(y_read, T * head)
                a = attT[:, head % 2]
                pe.matmul(ps[:, 0, :], a[:, 0:P], vals[:, head, 0, :], start=True, stop=True).then_inc(ret_y, 1)
                pe.matmul(ps[:, 1, :], a[:, P:SEQ], vals[:, head, 0, :], start=True, stop=False)
                pe.matmul(ps[:, 1, :], a[:, SEQ:SEQ + P], vals[:, head, 1, :], start=False,
                          stop=True).then_inc(ret_y, 1)

            def transposes_z(n):
                head, t = n // T, n % T
                pe.wait_ge(z_ready, n + 1)
                if n >= 1:
                    pe.wait_ge(zT_lo_done, n)
                for k in range(4):
                    last = pe.transpose(ps[:, 7, k * P:(k + 1) * P], gated[:, head, t, k * P:(k + 1) * P],
                                        ident[:, :])
                last.then_inc(zT_done, 1)

            drained(DR_QK[0])
            for s in range(2 * (3 * RH - LOOPED)):
                c = LOOPED + s // 2
                if s < 2:
                    transposes_qk(0, rows, [0, 1, 2, 3], range(4 * s, 4 * s + 4))
                if s % 2 == 0 and c >= QKV:
                    if c < QKV + 2:
                        drained(DR_QK[0] + 4 + c - QKV + 1)
                    else:
                        pe.wait_ge(silu_g, c - QKV - 1)
                project_unit(U_RET_IN + 2 * c + s % 2, 0, s % 2, (2 + 2 * (c % 2), 3 + 2 * (c % 2)))
                if s == 1:
                    drained(DR_QK[0] + 4)
                    ret_scores(0)
                if s >= 2 and s % 2 == 0 and (s - 2) // 2 < RH:
                    ret_values((s - 2) // 2)
                    if s // 2 < RH:
                        ret_scores(s // 2)
                if s >= 6:
                    transposes_z(s - 6)

            def zT_chunks(i):
                return zT_hi[:, 2 * i:2 * i + 2], zT_lo[:, 2 * i:2 * i + 2]

            pe.wait_ge(silu_g, RH)
            for i in range(U_FFN - U_RET_OUT - 3):
                pe.wait_ge(zT_lo_done, T * (i // 2 + 1))
                out_product(U_RET_OUT + i, 0, *zT_chunks(i), i == 0, False)
                if i < T:
                    transposes_z(T * (RH - 1) + i)
            pe.wait_ge(zT_lo_done, T * RH)
            out_product_end(range(U_FFN - 3, U_FFN), [zT_chunks(U_FFN - U_RET_OUT - 3 + i) for i in range(3)])

            def ffn_in_tile(u, part, t):
                tok = slice(t * P, (t + 1) * P)
                for k in range(KD):
                    w = slice(k * FB, (k + 1) * FB)
                    last = passes(ps[:, t, part * FB:(part + 1) * FB], xT_hi[:, k, tok], xT_lo[:, k, tok],
                                  whi[:, u % SPLIT, w], wlo[:, u % SPLIT, w], k == 0, k == KD - 1)
                return last

            def ffn_in_product(u, r, part):
                unit_ready(u, r)
                ffn_in_tile(u, part, 0)
                ffn_in_tile(u, part, 1).then_inc(unit_used, 1)

            def first_block(n, u, tile_of):
                for t in range(T):
                    transposes_x(n, t)
                    xT_ready(n, t)
                    for part in range(2):
                        if t == 0:
                            unit_ready(u + part)
                        last = tile_of(u + part, part, t)
                        if t == 1:
                            last.then_inc(unit_used, 1)

            def transposes_f(b):
                pe.wait_ge(f_mul, b + 1)
                for c in range(2):
                    for t in range(T):
                        last = pe.transpose(ps[:, 6, (2 * c + t) * P:(2 * c + t + 1) * P],
                                            hid2[:, t, c * P:(c + 1) * P], ident[:, :])
                last.then_inc(fT_done, 1)

            def ffn_block(r, half, first, out=True):
                u, b = U_FFN + 2 + 3 * half, 2 * r + half + 1
                pe.wait_ge(f_mul, b)
                ffn_in_product(u, r, 0)
                transposes_f(b - 1)
                ffn_in_product(u + 1, r, 1)
                pe.wait_ge(fT_lo_done, b)
                if out:
                    out_product(u + 2, r, fT_hi, fT_lo, first, False)

            first_block(1, U_FFN, ffn_in_tile)
            ffn_block(0, 0, True)
            ffn_block(0, 1, False)
            with pe.Fori(1, NFB // 2) as r:
                ffn_block(r, 0, False)
                ffn_block(r, 1, False)
            transposes_f(NFB - 1)
            pe.wait_ge(fT_lo_done, NFB)
            out_product_end([U_KVQ - 1], [(fT_hi, fT_lo)])

            first_block(2, U_KVQ, lambda u, part, t: project_tile(u, part, t, 2 + t))
            for s in range(2, 12):
                c = s // 2
                if s % 2 == 0 and c >= 2:
                    drained(KVQ_BLOCK_DRAINED[c - 2])
                project_unit(U_KVQ + s, 0, s % 2, (2 + 2 * (c % 2), 3 + 2 * (c % 2)))
                if s == 5:
                    drained(KVQ_BLOCK_DRAINED[1])
                    transposes_qk(1, kvq, [0, 1, 2, 3], range(0, 4))
                if s == 8:
                    drained(KVQ_BLOCK_DRAINED[3])
                    transposes_qk(1, kvq, [0, 1, 2, 3], range(4, 8))
                if s in (9, 10):
                    t = 10 - s
                    if t == 1:
                        drained(KVQ_BLOCK_DRAINED[3] + 2)
                    else:
                        pe.wait_ge(scores_read, 1)
                    for head in range(AH):
                        last = pe.matmul(score_at(t, head), kqT[:, AH + head, t * P:(t + 1) * P],
                                         kqT[:, head, 0:P * (t + 1)], start=True, stop=True)
                    last.then_inc(s_done, 1)

            def transposes_p(head):
                pe.wait_ge(p_ready, AH + head + 1)
                if head >= 2:
                    pe.wait_ge((pT_act, pT_dve)[head % 2], head // 2)
                for c, piece in enumerate((prob[:, 0, head, 0:P], prob[:, 1, head, 0:P], prob[:, 1, head, P:SEQ])):
                    last = pe.transpose(ps[:, 6 + head % 2, c * P:(c + 1) * P], piece, ident[:, :])
                last.then_inc(pT_done, 1)

            def oT_chunks(i):
                return xT_hi[:, 2 * i:2 * i + 2], xT_lo[:, 2 * i:2 * i + 2]

            drained(KVQ_BLOCK_DRAINED[5])
            transposes_p(0)
            for head in range(AH):
                if head + 1 < AH:
                    transposes_p(head + 1)
                pe.wait_ge((pT_act, pT_dve)[head % 2], head // 2 + 1)
                pair = head // 2
                if head % 2 == 0 and pair >= 2:
                    pe.wait_ge(oT_lo_done, pair - 1)
                o = ps[:, pair % 2, (head % 2) * SEQ:(head % 2 + 1) * SEQ]
                v = slice((head % 4) * P, (head % 4 + 1) * P)
                pe.matmul(o, kvq[:, 4 + head // 4, 0, v], pT[:, head % 2, 0:SEQ], start=True, stop=False,
                          skip_group_check=True)
                last = pe.matmul(o[:, P:SEQ], kvq[:, 4 + head // 4, 1, v], pT[:, head % 2, SEQ:SEQ + P],
                                 start=False, stop=True, skip_group_check=True)
                if head % 2 == 1:
                    last.then_inc(o_done, 1)
                if head == 3:
                    pe.wait_ge(oT_lo_done, 1)
                    out_product(U_ATT_OUT, 0, *oT_chunks(0), True, False)
            pe.wait_ge(oT_lo_done, AH // 2)
            out_product_end(range(U_ATT_OUT + 1, U_MOE), [oT_chunks(i) for i in range(1, KD // 2)])

            pe.wait_ge(router_split, 2)
            for t in range(T):
                tok = slice(t * P, (t + 1) * P)
                transposes_x(3, t)
                xT_ready(3, t)
                for k in range(KD):
                    last = passes(ps[:, 0, t * EX:(t + 1) * EX], xT_hi[:, k, tok], xT_lo[:, k, tok],
                                  router_hi[:, k, :], router_lo[:, k, :], k == 0, k == KD - 1)
            last.then_inc(logit_done, 1)
            pe.wait_ge(member_ready, 1)
            pe.wait_ge(tables, 5)
            pe.matmul(ps[:, 6, 0:EX], before[:, :], member[:, 0, :], start=True, stop=True)
            for c, second in enumerate((before, ones)):
                at = slice((c + 1) * EX, (c + 2) * EX)
                pe.matmul(ps[:, 6, at], ones[:, :], member[:, 0, :], start=True, stop=False)
                last = pe.matmul(ps[:, 6, at], second[:, :], member[:, 1, :], start=False, stop=True)
            last.then_inc(rank_done, 1)

            def gather(j):
                pe.wait_ge(sel_ready, j + 1)
                for b0, src in ((4, h_hi), (0, h_lo)):
                    for k in range(KD):
                        for t in range(T):
                            last = pe.matmul(ps[:, b0 + k // 4, (k % 4) * P:(k % 4 + 1) * P],
                                             src[:, t, k * P:(k + 1) * P], sel[:, t, :],
                                             start=(t == 0), stop=(t == T - 1))
                last.then_inc(gathered, 1)

            def scatter(j, t):
                for half in range(2):
                    n = slice(half * BANK, (half + 1) * BANK)
                    pe.matmul(ps[:, 4 + half, :], selT[:, t * P:(t + 1) * P], y_hi[:, n], start=True, stop=False)
                    last = pe.matmul(ps[:, 4 + half, :], selT[:, t * P:(t + 1) * P], y_lo[:, n],
                                     start=False, stop=True)
                last.then_inc(scattered, 1)

            def moe_in_product(u, r, part):
                for q in range(2):
                    unit_ready(u + q, r)
                    for c in range(4):
                        k = 4 * q + c
                        w = slice(c * BANK, (c + 1) * BANK)
                        last = passes(ps[:, part, :], xg_hi[:, k, :], xg_lo[:, k, :],
                                      whi[:, (u + q) % SPLIT, w], wlo[:, (u + q) % SPLIT, w], k == 0, k == KD - 1)
                    last.then_inc(unit_used, 1)

            def moe_out_product(u, r, first, last_k):
                for q in range(2):
                    unit_ready(u + q, r)
                    for c in range(2):
                        for half in range(2):
                            w = slice((2 * c + half) * BANK, (2 * c + half + 1) * BANK)
                            last = passes(ps[:, 2 + half, :], gT_hi[:, 2 * q + c, :], gT_lo[:, 2 * q + c, :],
                                          whi[:, (u + q) % SPLIT, w], wlo[:, (u + q) % SPLIT, w],
                                          first and q == 0 and c == 0, last_k and q == 1 and c == 1)
                    last.then_inc(unit_used, 1)

            def transposes_g(n):
                pe.wait_ge(e_mul, n + 1)
                for k in range(4):
                    last = pe.transpose(ps[:, 6, k * P:(k + 1) * P], hid4[:, k * P:(k + 1) * P], ident[:, :])
                last.then_inc(gT_done, 1)

            def moe_block(j, b, first):
                n = NEB * j + b
                pe.wait_ge(e_silu, n)
                moe_in_product(U_MOE - 2, n, 0)
                transposes_g(n - 1)
                moe_in_product(U_MOE, n, 1)
                pe.wait_ge(gT_lo_done, n)
                moe_out_product(U_MOE + 2, n, first, False)

            def job(j):
                pe.wait_ge(xg_hi_done, j + 1)
                pe.wait_ge(xg_lo_done, j + 1)
                moe_in_product(U_MOE, NEB * j, 0)
                pe.wait_ge(y_lo_done, j + 1)
                pe.wait_ge(selT_ready, j + 1)
                scatter(j, 0)
                moe_in_product(U_MOE + 2, NEB * j, 1)
                pe.wait_ge(summed, T * j + 1)
                scatter(j, 1)
                for t in range(T):
                    last = pe.transpose(ps[:, 7, t * P:(t + 1) * P], sel[:, t, :].bitcast(F32), ident[:, :])
                last.then_inc(selT_done, 1)
                moe_block(j, 1, True)
                with pe.Fori(2, NEB) as b:
                    moe_block(j, b, False)
                transposes_g(NEB * j + NEB - 1)
                pe.wait_ge(summed, T * j + T)
                gather(j + 1)
                pe.wait_ge(gT_lo_done, NEB * j + NEB)
                moe_out_product(U_MOE + JOB_UNITS - 2, NEB * j, False, True)

            pe.wait_ge(h_split, 1)
            gather(0)
            with pe.Fori(0, EX) as j:
                job(j)
            pe.wait_ge(over_ready, 1)
            more = pe.value_load(over[0:1, 0:1], min_val=0, max_val=1)
            with pe.If(more > 0):
                with pe.Fori(EX, 2 * EX) as j:
                    job(j)
            jobs = EX + EX * more
            pe.wait_ge(xg_hi_done, jobs + 1)
            pe.wait_ge(y_lo_done, jobs + 1)
            pe.wait_ge(selT_ready, jobs + 1)
            scatter(jobs, 0)
            pe.wait_ge(summed, T * jobs + 1)
            scatter(jobs, 1)


_INS = ['x', 'ln_g', 'ln_b', 'ret_w_in', 'ret_gn_g', 'ret_gn_b', 'ret_w_out', 'kv_w', 'moba_w_q', 'moba_w_out',
        'ffn_w_in', 'ffn_w_out', 'moe_router', 'moe_w_in', 'moe_w_out']


def kernel(**inputs):
    import numpy as np
    import concourse.bacc as bacc
    from concourse.bass_utils import run_bass_kernel_spmd

    nc = bacc.Bacc("TRN2", target_bir_lowering=False, num_devices=1)
    arrays, args = {}, []
    for name in _INS:
        a = np.ascontiguousarray(inputs[name])
        arrays[f"in_{name}"] = a
        args.append(nc.dram_tensor(f"in_{name}", a.shape, mybir.dt.from_np(a.dtype), kind="ExternalInput").ap())
    args.append(nc.dram_tensor("out_h", inputs["x"].shape, F32, kind="ExternalOutput").ap())
    build(nc, *args)
    r = run_bass_kernel_spmd(nc, [arrays], core_ids=[0])
    return r.results[0]["out_h"]
```

```python
import math
from contextlib import ExitStack

import concourse.bass as bass
import concourse.mybir as mybir

ALU = mybir.AluOpType
ACT = mybir.ActivationFunctionType
AX = mybir.AxisListType
F32 = mybir.dt.float32
F32R = mybir.dt.float32r
U32 = mybir.dt.uint32
I32 = mybir.dt.int32

P = 128
BANK = 512
RAW = 6
SPLIT = 3
AHEAD = 3
UNIT = 2048

LN_EPS, GN_EPS = 1e-5, 1e-6
NEVER = 3e38


def build(nc, x, ln_g, ln_b, ret_w_in, ret_gn_g, ret_gn_b, ret_w_out, kv_w, moba_w_q, moba_w_out,
          ffn_w_in, ffn_w_out, moe_router, moe_w_in, moe_w_out, out):
    _, SEQ, D = x.shape
    T = SEQ // P
    KD = D // P
    DEPTH = ln_g.shape[0]
    ALPHA = (2 * DEPTH) ** 0.25
    RH = D // 256
    VW = ret_w_out.shape[1]
    DV = VW // RH
    RIN = ret_w_in.shape[2]
    AH = D // P
    FF = ffn_w_out.shape[1]
    FB = 256
    NFB = FF // FB
    EX = moe_router.shape[2]
    EFF = moe_w_out.shape[2]
    NEB = EFF // BANK
    assert T == 2 and KD == 8 and DV == BANK and NFB % 2 == 1 and EX == 8

    U_RET_IN = 0
    U_RET_OUT = U_RET_IN + RIN // BANK * 2
    U_FFN = U_RET_OUT + VW // P // 2
    U_KVQ = U_FFN + 3 * NFB
    U_ATT_OUT = U_KVQ + 3 * D // BANK * 2
    U_MOE = U_ATT_OUT + KD // 2
    JOB_UNITS = 6 * NEB
    FIRST_KEPT, KEPT = 3, 3
    kept_slots = [(U_MOE + FIRST_KEPT + i) % RAW for i in range(KEPT)]
    assert JOB_UNITS % RAW == 0 and RAW % SPLIT == 0

    QK_DRAINED = 4 + RH
    DR_XT = [0, QK_DRAINED + RH, QK_DRAINED + RH + 4, QK_DRAINED + RH + 14]
    FILLED_XT = [0, 4, 8, 12]

    ret_in = ret_w_in.rearrange("a (k p) n -> p (a k) n", p=P)
    ret_out = ret_w_out.rearrange("a (k p) n -> p (a k) n", p=P)
    kv_in = kv_w.rearrange("(k p) n -> p k n", p=P)
    q_in = moba_w_q.rearrange("a (k p) n -> p (a k) n", p=P)
    att_out = moba_w_out.rearrange("a (k p) n -> p (a k) n", p=P)
    ffn_in = ffn_w_in.rearrange("a (k p) n -> p (a k) n", p=P)
    ffn_out = ffn_w_out.rearrange("a (k p) n -> p (a k) n", p=P)
    moe_in = moe_w_in.rearrange("a e (k p) n -> p (a e k) n", p=P)
    moe_out = moe_w_out.rearrange("a e (k p) n -> p (a e k) n", p=P)
    router_in = moe_router.rearrange("a (k p) n -> p (a k) n", p=P)
    x_rows = x.rearrange("b (t p) d -> p (b t) d", p=P)
    out_rows = out.rearrange("b (t p) d -> p (b t) d", p=P)

    KVQ_DRAINED = DR_XT[2] + 4
    LAST_SUM = [U_FFN - 1, U_KVQ - 1, U_MOE - 1]
    IN_SLOTS = 24
    QK_UNITS = 8

    ctx = ExitStack()
    with ctx:
        def sem(name):
            return ctx.enter_context(nc.semaphore(name))

        map_at = [(nc.sbuf_base + 31) // 32 * 32]

        def place(name, shape, dt=F32, at=None):
            start = map_at[0] if at is None else at
            size = (math.prod(shape[1:]) * 4 + 31) // 32 * 32
            assert start + size <= nc.sbuf_usable_end, name
            if at is None:
                map_at[0] = start + size
            return nc.alloc_sbuf_tensor_at(name, shape, dt, offset=start), start

        raw, _ = place("raw", [P, RAW, UNIT])
        whi, _ = place("whi", [P, SPLIT, UNIT], F32R)
        wlo, _ = place("wlo", [P, SPLIT, UNIT], F32R)
        h, _ = place("h", [P, T, D])
        xT_hi, xT_at = place("xT_hi", [P, KD, SEQ], F32R)
        xT_lo, _ = place("xT_lo", [P, KD, SEQ], F32R)
        xT, _ = place("xT", [P, KD, SEQ], at=xT_at)
        ident, _ = place("ident", [P, P])
        eps, _ = place("eps", [P, 2])
        row_sum, _ = place("row_sum", [P, T])
        neg_mean, _ = place("neg_mean", [P, T])
        square_sum, _ = place("square_sum", [P, T])
        std, _ = place("std", [P, T])
        spare, _ = place("spare", [P, 1])
        rstd, _ = place("rstd", [P, T])

        router, _ = place("router", [P, KD, EX])
        iota_expert, _ = place("iota_expert", [P, EX])

        area = map_at[0]
        qkT, _ = place("qkT", [P, 2 * KD, SEQ])
        zT_hi, zT_at = place("zT_hi", [P, VW // P, SEQ], F32R)
        vals, vals_at = place("vals", [P, RH, T, DV])
        zT_lo, _ = place("zT_lo", [P, VW // P, SEQ], F32R, at=vals_at)
        gated, _ = place("gated", [P, RH, T, DV])
        decay, _ = place("decay", [P, RH, SEQ])
        attT, _ = place("attT", [P, 2, 3 * P])
        gn, _ = place("gn", [P, 2, 2, DV])
        normed, _ = place("normed", [P, T, DV])
        gstats, _ = place("gstats", [P, T, 6])
        gmv, _ = place("gmv", [P, T, 2])
        gstd, _ = place("gstd", [P, T])
        grstd, _ = place("grstd", [P, T])

        map_at[0] = area
        ln_gb, _ = place("ln_gb", [P, 2, D])
        ones, _ = place("ones", [P, P])
        before, _ = place("before", [P, P])
        iota_slot, _ = place("iota_slot", [P, P])
        past, _ = place("past", [P, T, SEQ])
        assert map_at[0] <= zT_at
        shared = map_at[0]
        centred, _ = place("centred", [P, T, D], at=shared)
        act2, _ = place("act2", [P, 2 * FB])
        hid2, _ = place("hid2", [P, 2 * FB])
        fT_hi, _ = place("fT_hi", [P, 2, 2, SEQ], F32R)
        fT_lo, _ = place("fT_lo", [P, 2, 2, SEQ], F32R)
        att_v, _ = place("att_v", [P, D // BANK, T, BANK])
        kqT, _ = place("kqT", [P, 2 * KD, SEQ])
        prob, _ = place("prob", [P, T, AH, SEQ])
        pT, _ = place("pT", [P, 2, 3 * P])
        neg_max, _ = place("neg_max", [P, T, AH])
        psum_p, _ = place("psum_p", [P, T, AH])
        inv_p, _ = place("inv_p", [P, T, AH])

        map_at[0] = shared
        h_hi, _ = place("h_hi", [P, T, D], F32R)
        h_lo, _ = place("h_lo", [P, T, D], F32R)
        xg, _ = place("xg", [P, D])
        xg_hi, _ = place("xg_hi", [P, KD, P], F32R)
        xg_lo, _ = place("xg_lo", [P, KD, P], F32R)
        act4, _ = place("act4", [P, BANK])
        hid4, _ = place("hid4", [P, BANK])
        gT_hi, _ = place("gT_hi", [P, 2, 4, P], F32R)
        gT_lo, _ = place("gT_lo", [P, 2, 4, P], F32R)
        y_hi, _ = place("y_hi", [P, D], F32R)
        y_lo, _ = place("y_lo", [P, D], F32R)
        sel, _ = place("sel", [P, T, P], F32R)
        selT, _ = place("selT", [P, T * P], F32R)
        logits, _ = place("logits", [P, T, EX])
        top, _ = place("top", [P, T, 8])
        top_i, _ = place("top_i", [P, T, 8], U32)
        top_f, _ = place("top_f", [P, 2, T])
        hot, _ = place("hot", [P, 2, T, EX])
        hot_w, _ = place("hot_w", [P, 2, T, EX])
        member, _ = place("member", [P, T, EX])
        two, _ = place("two", [P, 4, T])
        slot_of, _ = place("slot_of", [P, T, 2 * EX])
        gate_of, _ = place("gate_of", [P, T, 2 * EX + 1])
        most, _ = place("most", [P, 1])
        over, _ = place("over", [P, 1], I32)
        kept, _ = place("kept", [P, KEPT, UNIT])

        ps = ctx.enter_context(nc.psum_tensor("ps", [P, 8, BANK], F32))

        landed = [sem(f"landed{i}") for i in range(RAW)]
        kept_landed = sem("kept_landed")
        hi_done = sem("hi_done")
        lo_done = sem("lo_done")
        unit_used = sem("unit_used")
        x_landed = sem("x_landed")
        gn_landed = [sem(f"gn_landed{i}") for i in range(RH)]
        ln_landed = [sem(f"ln_landed{i}") for i in range(4)]
        router_landed = sem("router_landed")
        stored = sem("stored")
        zeroed = sem("zeroed")
        tables = sem("tables")
        rel_ready = sem("rel_ready")
        decay_exp = sem("decay_exp")
        decay_ready = sem("decay_ready")
        filled = sem("filled")
        act_drained = sem("act_drained")
        dve_drained = sem("dve_drained")
        score_done = sem("score_done")
        att_ready = sem("att_ready")
        silu_g = sem("silu_g")
        ret_y = sem("ret_y")
        gn_var = sem("gn_var")
        gn_std = sem("gn_std")
        y_read = sem("y_read")
        norm_ready = sem("norm_ready")
        z_ready = sem("z_ready")
        zT_done = sem("zT_done")
        zT_hi_done = sem("zT_hi_done")
        zT_lo_done = sem("zT_lo_done")
        tile0_summed = sem("tile0_summed")
        ln_mean = sem("ln_mean")
        ln_square = sem("ln_square")
        ln_std = sem("ln_std")
        sqrt_loaded = sem("sqrt_loaded")
        h_ready = sem("h_ready")
        f_silu = sem("f_silu")
        f_mul = sem("f_mul")
        fT_done = sem("fT_done")
        fT_hi_done = sem("fT_hi_done")
        fT_lo_done = sem("fT_lo_done")
        s_done = sem("s_done")
        max_ready = sem("max_ready")
        p_exp = sem("p_exp")
        p_ready = sem("p_ready")
        pT_done = sem("pT_done")
        scores_read = sem("scores_read")
        pT_act = sem("pT_act")
        pT_dve = sem("pT_dve")
        o_done = sem("o_done")
        oT_hi_done = sem("oT_hi_done")
        oT_lo_done = sem("oT_lo_done")
        logit_done = sem("logit_done")
        gap_ready = sem("gap_ready")
        gap_exp = sem("gap_exp")
        member_ready = sem("member_ready")
        rank_done = sem("rank_done")
        counted = sem("counted")
        over_ready = sem("over_ready")
        h_hi_done = sem("h_hi_done")
        h_split = sem("h_split")
        sel_ready = sem("sel_ready")
        gathered = sem("gathered")
        xg_rows_act = sem("xg_rows_act")
        xg_rows_dve = sem("xg_rows_dve")
        xgT_done = sem("xgT_done")
        xg_hi_done = sem("xg_hi_done")
        xg_lo_done = sem("xg_lo_done")
        e_silu = sem("e_silu")
        e_mul = sem("e_mul")
        gT_done = sem("gT_done")
        gT_hi_done = sem("gT_hi_done")
        gT_lo_done = sem("gT_lo_done")
        y_hi_done = sem("y_hi_done")
        y_lo_done = sem("y_lo_done")
        selT_done = sem("selT_done")
        selT_ready = sem("selT_ready")
        scattered = sem("scattered")
        summed = sem("summed")
        dve_step = sem("dve_step")

        def number(u, r):
            return u + RAW * r

        def unit_done(eng, u, r):
            eng.wait_ge(unit_used, number(u + 1, r))

        def bank(n, k):
            return ps[:, n, :].rearrange("p (k n) -> p k n", k=k)

        def score_banks(pair):
            return [(0, 1), (6, 7), (0, 1), (4, 5)][pair]

        def x_bank(n, t):
            return 0 if n == 0 and t == 1 else 6

        def load_unit(sp, u, r, src, rows, back=RAW):
            if u >= RAW or not isinstance(r, int):
                sp.wait_ge(lo_done, number(u - back + 1, r))
            dst = raw[:, u % RAW, :].rearrange("p (k n) -> p k n", k=rows)
            sp.dma_start(dst, src).then_inc(landed[u % RAW], 16)

        def split_hi(act, u, r=0, passed=0):
            absent = passed if u % RAW in kept_slots else 0
            act.wait_ge(landed[u % RAW], 16 * (u // RAW + 1 - absent) + 16 * r)
            write_hi(act, u, r, raw[:, u % RAW, :])

        def write_hi(act, u, r, src):
            if u >= SPLIT:
                act.wait_ge(unit_used, number(u - SPLIT + 1, r))
            nc.scalar.activation(whi[:, u % SPLIT, :], src, ACT.Copy).then_inc(hi_done, 1)

        def split_lo(dve, u, r=0):
            write_lo(dve, u, r, raw[:, u % RAW, :])

        def write_lo(dve, u, r, src):
            dve.wait_ge(hi_done, number(u + 1, r))
            nc.vector.tensor_tensor(wlo[:, u % SPLIT, :], src,
                                    whi[:, u % SPLIT, :].bitcast(F32), ALU.subtract).then_inc(lo_done, 1)

        def moe_source(i, e, b):
            if i < 4:
                b, part = 0, i
            elif i < JOB_UNITS - 2:
                part = (i - 4) % 6
            else:
                b, part = NEB, i - (JOB_UNITS - 2) + 4
            if part < 4:
                col = (part // 2) * EFF
                return moe_in[:, bass.ds(e * KD + 4 * (part % 2), 4), bass.ds(col + b * BANK, BANK)], 4
            return moe_out[:, bass.ds(e * (EFF // P) + (b - 1) * 4 + 2 * (part - 4), 2), :], 2

        block = ctx.enter_context(nc.Block())

        @block.sync
        def _(sp):
            for t in range(T):
                sp.dma_start(h[:, t, :], x_rows[:, t, :]).then_inc(x_landed, 16)

            for i in range(QK_UNITS):
                load_unit(sp, U_RET_IN + i, 0, ret_in[:, 0:KD, (i // 2 + i % 2 * RH) * FB:(i // 2 + i % 2 * RH + 1) * FB],
                          KD)
            for i in range(QK_UNITS, IN_SLOTS):
                part, col = i % 2, i // 2 * BANK
                load_unit(sp, U_RET_IN + i, 0, ret_in[:, 4 * part:4 * part + 4, col:col + BANK], 4)
            for i in range(VW // P // 2):
                load_unit(sp, U_RET_OUT + i, 0, ret_out[:, 2 * i:2 * i + 2, :], 2)

            def ffn_unit(u, r, part, b):
                if part < 2:
                    src, rows = ffn_in[:, 0:KD, bass.ds(part * FF + b * FB, FB)], KD
                else:
                    src, rows = ffn_out[:, bass.ds(2 * b, 2), :], 2
                load_unit(sp, u, r, src, rows)

            ffn_unit(U_FFN, 0, 0, 0)
            ffn_unit(U_FFN + 1, 0, 1, 0)
            with sp.Fori(0, NFB // 2) as r:
                for half in range(2):
                    u = U_FFN + 2 + 3 * half
                    ffn_unit(u, r, 0, 2 * r + 1 + half)
                    ffn_unit(u + 1, r, 1, 2 * r + 1 + half)
                    ffn_unit(u + 2, r, 2, 2 * r + half)
            ffn_unit(U_FFN + 3 * NFB - 1, 0, 2, NFB - 1)
            def value_units(s, block):
                for part in range(2):
                    col = D + block * BANK
                    load_unit(sp, U_KVQ + s + part, 0, kv_in[:, 4 * part:4 * part + 4, col:col + BANK], 4)

            value_units(0, 0)
            for pair in range(AH // 2):
                for i, w in enumerate((kv_in, q_in)):
                    load_unit(sp, U_KVQ + 2 + 2 * pair + i, 0, w[:, 0:KD, pair * FB:(pair + 1) * FB], KD)
            value_units(10, 1)
            for i in range(KD // 2):
                load_unit(sp, U_ATT_OUT + i, 0, att_out[:, 2 * i:2 * i + 2, :], 2)

            def first_loads(e, u, r):
                for i in range(AHEAD):
                    load_unit(sp, u + i, r, *moe_source(i, e, 0))

            def kept_loads():
                sp.wait_ge(h_ready, T * 2 + 1)
                for i in range(KEPT):
                    src, rows = moe_source(FIRST_KEPT + i, 0, 1)
                    sp.dma_start(kept[:, i, :].rearrange("p (k n) -> p k n", k=rows), src
                                 ).then_inc(kept_landed, 16)

            def job_loads(e, j, first=False, last=False):
                def block_loads(b, parts, back=RAW):
                    for i in parts:
                        load_unit(sp, U_MOE + i - 6, NEB * j + b, *moe_source(i, e, b), back)

                if first:
                    block_loads(1, (9,), 2 * RAW)
                    block_loads(2, (4, 5), 2 * RAW)
                    block_loads(1, (6, 7, 8))
                    block_loads(2, range(6, 10))
                else:
                    load_unit(sp, U_MOE + 3, NEB * j, *moe_source(3, e, 0))
                with sp.Fori(3 if first else 1, NEB) as b:
                    block_loads(b, range(4, 10))
                for i in (JOB_UNITS - 2, JOB_UNITS - 1):
                    load_unit(sp, U_MOE + i, NEB * j, *moe_source(i, e, 0))
                if not last:
                    first_loads(e + 1, U_MOE + JOB_UNITS, NEB * j)

            def pass_loads(first):
                first_loads(0, U_MOE, NEB * first)
                if first == 0:
                    kept_loads()
                job_loads(0, first, first=True)
                with sp.Fori(1, EX - 1) as e:
                    job_loads(e, e + first)
                job_loads(EX - 1, EX - 1 + first, last=True)

            pass_loads(0)
            sp.wait_ge(over_ready, 1)
            more = sp.value_load(over[0:1, 0:1], min_val=0, max_val=1)
            with sp.If(more > 0):
                pass_loads(EX)
            for t in range(T):
                for half in range(2):
                    n = slice(half * BANK, (half + 1) * BANK)
                    sp.wait_ge(h_ready, T * 3 + 2 * t + half + 1)
                    sp.dma_start(out_rows[:, t, n], h[:, t, n]).then_inc(stored, 16)
            sp.wait_ge(stored, 2 * T * 16)

        @block.gpsimd
        def _(pool):
            def load_gn(head):
                cols = slice(head * DV, (head + 1) * DV)
                for n, w in enumerate((ret_gn_g, ret_gn_b)):
                    pool.dma_start(gn[:, head % 2, n, :], w[0:1, cols].partition_broadcast(P)
                                   ).then_inc(gn_landed[head], 16)

            def load_ln(n):
                for k, w in enumerate((ln_g, ln_b)):
                    pool.dma_start(ln_gb[:, k, :], w[n // 2:n // 2 + 1, n % 2, :].partition_broadcast(P)
                                   ).then_inc(ln_landed[n], 16)

            pool.memset(ident[:, :], 0.0).then_inc(zeroed, 1)
            pool.memset(eps[:, 0:1], LN_EPS).then_inc(zeroed, 1)
            pool.memset(eps[:, 1:2], GN_EPS).then_inc(zeroed, 1)
            pool.wait_ge(zeroed, 3)
            pool.affine_select(out=ident[:, :], in_=ident[:, :], compare_op=ALU.not_equal, fill=1.0, base=0,
                               pattern=[[-1, P]], channel_multiplier=1).then_inc(tables, 1)
            pool.iota(decay[:, :, :], pattern=[[0, RH], [1, SEQ]], base=0, channel_multiplier=-1,
                      allow_small_or_imprecise_dtypes=True).then_inc(rel_ready, 1)
            pool.iota(iota_expert[:, :], pattern=[[1, EX]], base=0, channel_multiplier=0,
                      allow_small_or_imprecise_dtypes=True).then_inc(tables, 1)
            pool.dma_start(router[:, :, :], router_in).then_inc(router_landed, 16)
            load_gn(0)
            load_gn(1)
            pool.wait_ge(decay_exp, RH)
            pool.affine_select(out=decay[:, :, :], in_=decay[:, :, :], compare_op=ALU.is_ge, fill=0.0, base=0,
                               pattern=[[0, RH], [1, SEQ]], channel_multiplier=-1).then_inc(decay_ready, 1)
            for head in range(RH):
                for t in range(T):
                    pool.wait_ge(norm_ready, T * head + t + 1)
                    pool.wait_ge(silu_g, head + 1)
                    g = gated[:, head, t, :]
                    pool.tensor_tensor(g, g, normed[:, t, :], ALU.mult).then_inc(z_ready, 1)
                if head + 2 < RH:
                    load_gn(head + 2)
            pool.wait_ge(score_done, RH)
            load_ln(0)
            pool.memset(ones[:, :], 1.0).then_inc(zeroed, 1)
            pool.wait_ge(zeroed, 4)
            pool.affine_select(out=before[:, :], in_=ones[:, :], compare_op=ALU.is_gt, fill=0.0, base=0,
                               pattern=[[1, P]], channel_multiplier=-1).then_inc(tables, 1)
            pool.iota(iota_slot[:, :], pattern=[[1, P]], base=1, channel_multiplier=0,
                      allow_small_or_imprecise_dtypes=True).then_inc(tables, 1)
            for t in range(T):
                pool.iota(past[:, t, :], pattern=[[-1, SEQ]], base=t * P, channel_multiplier=1,
                          allow_small_or_imprecise_dtypes=True).then_inc(zeroed, 1)
            pool.wait_ge(zeroed, 6)
            for t in range(T):
                pool.affine_select(out=past[:, t, :], in_=past[:, t, :], compare_op=ALU.is_ge, fill=NEVER,
                                   base=t * P, pattern=[[-1, SEQ]], channel_multiplier=1).then_inc(tables, 1)
            for n in (1, 2, 3):
                if n == 3:
                    pool.wait_ge(h_ready, T * (n - 1) + 1)
                    pool.memset(y_hi[:, :].bitcast(F32), 0.0).then_inc(y_lo_done, 1)
                    pool.memset(y_lo[:, :].bitcast(F32), 0.0).then_inc(y_lo_done, 1)
                    pool.memset(selT[:, :].bitcast(F32), 0.0).then_inc(selT_ready, 1)
                    pool.wait_ge(hi_done, U_MOE + 1)
                    pool.tensor_tensor(wlo[:, U_MOE % SPLIT, :], raw[:, U_MOE % RAW, :],
                                       whi[:, U_MOE % SPLIT, :].bitcast(F32), ALU.subtract).then_inc(lo_done, 1)
                pool.wait_ge(h_ready, T * n)
                load_ln(n)

        @block.scalar
        def _(act):
            def drain_xT(n, t):
                for g in (2 * t, 2 * t + 1):
                    c = 4 * (g % 2)
                    act.wait_ge(filled, FILLED_XT[n] + g + 1)
                    nc.scalar.activation(xT_hi[:, c:c + 4, t * P:(t + 1) * P], bank(x_bank(n, t) + g % 2, 4),
                                         ACT.Copy).then_inc(act_drained, 1)

            def drain_block(u, r, dst, at):
                unit_done(act, u, r)
                nc.scalar.activation(dst, ps[:, at, :], ACT.Copy).then_inc(act_drained, 1)

            def drain_columns(u, dst, at):
                unit_done(act, u, 0)
                nc.scalar.activation(dst, bank(at, 2), ACT.Copy).then_inc(act_drained, 1)

            def drain_zT_hi(n):
                head, t = n // T, n % T
                act.wait_ge(zT_done, n + 1)
                nc.scalar.activation(zT_hi[:, 4 * head:4 * head + 4, t * P:(t + 1) * P], bank(7, 4),
                                     ACT.Copy).then_inc(zT_hi_done, 1)

            def norm_squares(n, t):
                act.wait_ge(ln_mean, T * n + t + 1)
                nc.scalar.activation(ps[:, 2 + 2 * t:4 + 2 * t, :].rearrange("p b n -> p (b n)"), h[:, t, :],
                                     ACT.Square, bias=neg_mean[:, t:t + 1],
                                     accum_out=square_sum[:, t:t + 1]).then_inc(ln_square, 1)

            def norm_std(n, t):
                act.wait_ge(ln_square, T * n + t + 1)
                nc.scalar.activation(std[:, t:t + 1], square_sum[:, t:t + 1], ACT.Sqrt, scale=1.0 / D,
                                     bias=eps[:, 0:1]).then_inc(ln_std, 1)

            def load_sqrt():
                nc.scalar.activation(spare[:, :], eps[:, 0:1], ACT.Sqrt).then_inc(sqrt_loaded, 1)

            def norm_between(n, u):
                load_sqrt()
                norm_squares(n, 0)
                norm_std(n, 0)
                if n == 0:
                    split_hi(act, u)
                if n == 0:
                    drain_xT(n + 1, 0)
                    split_hi(act, u + 1)
                    norm_squares(n, 1)
                    norm_std(n, 1)
                else:
                    split_hi(act, u + 1)
                    drain_xT(n + 1, 0)
                    norm_squares(n, 1)
                    norm_std(n, 1)
                drain_xT(n + 1, 1)
                split_hi(act, u + 2)

            def exps(pair):
                act.wait_ge(max_ready, pair + 1)
                for t in range(T):
                    for head in (2 * pair, 2 * pair + 1):
                        p = prob[:, t, head, 0:P * (t + 1)]
                        nc.scalar.activation(p, p, ACT.Exp, bias=neg_max[:, t, head:head + 1],
                                             accum_out=psum_p[:, t, head:head + 1]).then_inc(p_exp, 1)

            act.wait_ge(rel_ready, 1)
            for head in range(RH):
                nc.scalar.activation(decay[:, head, :], decay[:, head, :], ACT.Exp,
                                     scale=math.log1p(-2.0 ** (-5 - head))).then_inc(decay_exp, 1)
            drain_xT(0, 0)
            drain_xT(0, 1)
            split_hi(act, 0)
            for u in range(1, AHEAD):
                split_hi(act, u)
            for i in range(QK_UNITS + 4):
                u = U_RET_IN + i
                if i < QK_UNITS and i % 2 == 0:
                    drain_columns(u, qkT[:, i:i + 2, :], 2 + i % 4)
                elif i >= QK_UNITS and i % 2 == 1:
                    block = (i - QK_UNITS) // 2
                    drain_block(u, 0, vals[:, block, 0, :], 2 + 2 * (block % 2))
                split_hi(act, u + AHEAD)
            for s in range(12):
                u, c = U_RET_IN + QK_UNITS + 4 + s, 2 + s // 2
                if s % 2 == 1 and c < RH:
                    drain_block(u, 0, vals[:, c, 0, :], 2 + 2 * (c % 2))
                elif s % 2 == 1:
                    unit_done(act, u, 0)
                    nc.scalar.activation(gated[:, c - RH, :, :], ps[:, 2 + 2 * (c % 2):4 + 2 * (c % 2), :],
                                         ACT.Silu).then_inc(silu_g, 1)
                if s >= 6:
                    drain_zT_hi(s - 6)
                split_hi(act, u + AHEAD)
                if s >= 2 and s % 2 == 0 and (s - 2) // 2 < RH:
                    act.wait_ge(gn_var, T * ((s - 2) // 2 + 1))
                    nc.scalar.activation(gstd[:, :], gmv[:, :, 1], ACT.Sqrt, bias=eps[:, 1:2]).then_inc(gn_std, 1)
            for u in range(U_RET_OUT, U_FFN - AHEAD):
                if u < U_RET_OUT + T:
                    drain_zT_hi(T * (RH - 1) + u - U_RET_OUT)
                split_hi(act, u + AHEAD)
            norm_between(0, U_FFN)

            def drain_fT(b, buf=0):
                if b is None:
                    act.wait_ge(fT_done, 1)
                    nc.scalar.activation(fT_hi[:, buf], bank(2, 2), ACT.Copy).then_inc(fT_hi_done, 1)
                else:
                    act.wait_ge(f_mul, b + 1)
                    nc.scalar.activation(fT_hi[:, buf].rearrange("p c n -> p (c n)"), hid2[:, :],
                                         ACT.Copy).then_inc(fT_hi_done, 1)

            def ffn_pair(r, first=False, last=False):
                for half in range(2):
                    u, b = U_FFN + 2 + 3 * half, 2 * r + half + 1
                    split_hi(act, u + AHEAD, r)
                    drain_fT(None if first and half == 0 else b - 1)
                    unit_done(act, u, r)
                    nc.scalar.activation(act2[:, :], ps[:, 6 * (1 - half), :], ACT.Silu).then_inc(f_silu, 1)
                    if last and half == 1:
                        drain_fT(b, 1)
                    split_hi(act, u + 1 + AHEAD, r)
                    if not (last and half == 1):
                        split_hi(act, u + 2 + AHEAD, r)

            split_hi(act, U_FFN + AHEAD)
            unit_done(act, U_FFN + 1, 0)
            nc.scalar.activation(act2[:, :].rearrange("p (t n) -> p t n", t=T), ps[:, 0:2, 0:FB],
                                 ACT.Silu).then_inc(f_silu, 1)
            split_hi(act, U_FFN + 1 + AHEAD)
            ffn_pair(0, first=True)
            with act.Fori(1, NFB // 2 - 1) as r:
                ffn_pair(r)
            ffn_pair(NFB // 2 - 1, last=True)
            norm_between(1, U_KVQ)

            def copy_pT(head):
                act.wait_ge(pT_done, head + 1)
                nc.scalar.activation(pT[:, 0, :], ps[:, 6, 0:3 * P], ACT.Copy).then_inc(pT_act, 1)

            for s in range(12):
                u, pair = U_KVQ + s, (s - 2) // 2
                if s == 11:
                    copy_pT(0)
                    exps(3)
                if s in (1, 11):
                    drain_block(u, 0, att_v[:, s // 6, 0, :], 2)
                elif 2 <= s < 10 and s % 2 == 0:
                    drain_columns(u, kqT[:, 2 * pair:2 * pair + 2, :], 4)
                if s in (5, 7, 9):
                    exps((s - 5) // 2)
                if s < 11:
                    split_hi(act, u + AHEAD)
            for pair in range(AH // 2):
                if pair + 1 < AH // 2:
                    copy_pT(2 * pair + 2)
                if pair == 1:
                    split_hi(act, U_ATT_OUT + AHEAD - 1)
                act.wait_ge(o_done, pair + 1)
                nc.scalar.activation(xT_hi[:, 2 * pair:2 * pair + 2, :], bank(pair % 2, 2),
                                     ACT.Copy).then_inc(oT_hi_done, 1)
                if pair == 2:
                    split_hi(act, U_ATT_OUT + AHEAD)

            def drain_router_xT(t):
                act.wait_ge(filled, FILLED_XT[3] + 2 * t + 1)
                nc.scalar.activation(xT[:, 0:4, t * P:(t + 1) * P], bank(6, 4), ACT.Copy).then_inc(act_drained, 1)

            def split_h(t):
                act.wait_ge(h_ready, T * 2 + t + 1)
                nc.scalar.activation(h_hi[:, t, :], h[:, t, :], ACT.Copy).then_inc(h_hi_done, 1)

            load_sqrt()
            norm_squares(2, 0)
            norm_std(2, 0)
            split_h(0)
            split_hi(act, U_MOE)
            drain_router_xT(0)
            norm_squares(2, 1)
            norm_std(2, 1)
            split_h(1)
            drain_router_xT(1)
            split_hi(act, U_MOE + 1)
            act.wait_ge(gap_ready, 1)
            nc.scalar.activation(two[:, 1, :], two[:, 0, :], ACT.Exp).then_inc(gap_exp, 1)

            def copy_xg(j):
                act.wait_ge(gathered, 2 * j + 1)
                nc.scalar.activation(xg[:, 0:BANK], ps[:, 4, :], ACT.Copy).then_inc(xg_rows_act, 1)

            def drain_xgT(j):
                for half, at in enumerate((7, 5)):
                    act.wait_ge(xgT_done, 2 * j + half + 1)
                    nc.scalar.activation(xg_hi[:, 4 * half:4 * half + 4, :], bank(at, 4), ACT.Copy).then_inc(xg_hi_done, 1)

            def silu_e(u_gate, r):
                unit_done(act, u_gate, r)
                nc.scalar.activation(act4[:, :], ps[:, 0, :], ACT.Silu).then_inc(e_silu, 1)

            def drain_gT(n, buf=0):
                act.wait_ge(gT_done, n + 1)
                nc.scalar.activation(gT_hi[:, buf], bank(6, 4), ACT.Copy).then_inc(gT_hi_done, 1)

            def job(j, passed, first=False, last=False):
                def split(i, b=0):
                    if first and isinstance(b, int) and 0 <= 6 * b + i - FIRST_KEPT < KEPT:
                        act.wait_ge(kept_landed, 16 * KEPT)
                        write_hi(act, U_MOE + i, NEB * j + b, kept[:, 6 * b + i - FIRST_KEPT, :])
                    else:
                        split_hi(act, U_MOE + i, NEB * j + b, passed)

                def block(b, splits):
                    n = NEB * j + b
                    split(0, b)
                    split(1, b)
                    act.wait_ge(e_mul, n)
                    silu_e(U_MOE - 1, n)
                    drain_gT(n - 1)
                    for k in range(2, splits):
                        split(k, b)

                split(3)
                silu_e(U_MOE + 1, NEB * j)
                split(4)
                split(5)
                act.wait_ge(selT_done, j + 1)
                nc.scalar.activation(selT[:, :], ps[:, 7, 0:T * P], ACT.Copy).then_inc(selT_ready, 1)
                with act.Fori(1, NEB - 1) as b:
                    block(b, 6)
                block(NEB - 1, 5)
                drain_gT(NEB * j + NEB - 1, 1)
                split(5, NEB - 1)
                if not last:
                    copy_xg(j + 1)
                    split_hi(act, U_MOE + JOB_UNITS, NEB * j, passed)
                    drain_xgT(j + 1)
                    split_hi(act, U_MOE + JOB_UNITS + 1, NEB * j, passed)
                unit_done(act, U_MOE + JOB_UNITS - 1, NEB * j)
                for half in range(2):
                    nc.scalar.activation(y_hi[:, half * BANK:(half + 1) * BANK], ps[:, 2 + half, :],
                                         ACT.Copy).then_inc(y_hi_done, 1)
                if not last:
                    split_hi(act, U_MOE + JOB_UNITS + 2, NEB * j, passed)

            def jobs_from(start, passed):
                job(start, passed, first=True)
                with act.Fori(start + 1, start + EX - 1) as j:
                    job(j, passed)
                job(start + EX - 1, passed, last=True)

            copy_xg(0)
            drain_xgT(0)
            split_hi(act, U_MOE + 2)
            jobs_from(0, 1)
            act.wait_ge(over_ready, 1)
            more = act.value_load(over[0:1, 0:1], min_val=0, max_val=1)
            with act.If(more > 0):
                copy_xg(EX)
                drain_xgT(EX)
                for i in range(AHEAD):
                    split_hi(act, U_MOE + i, NEB * EX)
                jobs_from(EX, 2)
            load_sqrt()
            for t in range(T):
                norm_squares(3, t)
                norm_std(3, t)

        @block.vector
        def _(dve):
            step = [0]

            def then(ins):
                step[0] += 1
                ins.then_inc(dve_step, 1)
                dve.wait_ge(dve_step, step[0])

            def lo_of(dst, src, hi):
                return nc.vector.tensor_tensor(dst, src, hi.bitcast(F32), ALU.subtract)

            def drain_xT(n, t):
                for g in (2 * t, 2 * t + 1):
                    c = 4 * (g % 2)
                    dve.wait_ge(act_drained, DR_XT[n] + g + 1)
                    lo_of(xT_lo[:, c:c + 4, t * P:(t + 1) * P], bank(x_bank(n, t) + g % 2, 4),
                          xT_hi[:, c:c + 4, t * P:(t + 1) * P]).then_inc(dve_drained, 1)

            def drain_block(u, r, dst, at):
                unit_done(dve, u, r)
                nc.vector.tensor_copy(dst, ps[:, at, :]).then_inc(dve_drained, 1)

            def drain_columns(u, dst, at, scale):
                unit_done(dve, u, 0)
                nc.vector.tensor_scalar(dst, bank(at, 2), scale, None, ALU.mult).then_inc(dve_drained, 1)

            def norm_mean(n, t):
                if n < 3:
                    if t == 0:
                        dve.wait_ge(tile0_summed, n + 1)
                    else:
                        unit_done(dve, LAST_SUM[n], 0)
                    then(nc.vector.scalar_tensor_tensor(out=h[:, t, :], in0=h[:, t, :], scalar=ALPHA,
                                                        in1=ps[:, 2 + 2 * t:4 + 2 * t, :].rearrange("p b n -> p (b n)"),
                                                        op0=ALU.mult, op1=ALU.add, accum_out=row_sum[:, t:t + 1]))
                nc.vector.tensor_scalar(neg_mean[:, t:t + 1], row_sum[:, t:t + 1], -1.0 / D, None,
                                        ALU.mult).then_inc(ln_mean, 1)
                dve.wait_ge(ln_mean, T * n + t + 1)
                if t == 0:
                    dve.wait_ge(ln_landed[n], 32)
                then(nc.vector.scalar_tensor_tensor(out=centred[:, t, :], in0=h[:, t, :], scalar=neg_mean[:, t:t + 1],
                                                    in1=ln_gb[:, 0, :], op0=ALU.add, op1=ALU.mult))

            def norm_end(n, t):
                dve.wait_ge(ln_std, T * n + t + 1)
                then(nc.vector.reciprocal(rstd[:, t:t + 1], std[:, t:t + 1]))
                w = D if n < 3 else BANK
                for c in range(0, D, w):
                    nc.vector.scalar_tensor_tensor(out=h[:, t, c:c + w], in0=centred[:, t, c:c + w],
                                                   scalar=rstd[:, t:t + 1], in1=ln_gb[:, 1, c:c + w],
                                                   op0=ALU.mult, op1=ALU.add).then_inc(h_ready, 1)

            def norm_between(n, u):
                norm_mean(n, 0)
                norm_end(n, 0)
                if n == 0:
                    split_lo(dve, u)
                drain_xT(n + 1, 0)
                norm_mean(n, 1)
                norm_end(n, 1)
                split_lo(dve, u + 1)
                drain_xT(n + 1, 1)
                split_lo(dve, u + 2)

            drain_xT(0, 0)
            drain_xT(0, 1)
            split_lo(dve, 0)
            for u in range(1, AHEAD):
                split_lo(dve, u)
            for i in range(QK_UNITS + 4):
                u = U_RET_IN + i
                if i < QK_UNITS and i % 2 == 1:
                    drain_columns(u, qkT[:, KD + i - 1:KD + i + 1, :], 2 + i % 4, 1.0)
                elif i >= QK_UNITS and i % 2 == 1:
                    block = (i - QK_UNITS) // 2
                    drain_block(u, 0, vals[:, block, 1, :], 3 + 2 * (block % 2))
                split_lo(dve, u + AHEAD)

            def decayed(head):
                dve.wait_ge(score_done, head + 1)
                if head == 0:
                    dve.wait_ge(decay_ready, 1)
                if head >= 1:
                    dve.wait_ge(ret_y, T * head)
                for a, b, c in ((0, SEQ, 0), (SEQ, SEQ + P, 0)):
                    nc.vector.scalar_tensor_tensor(out=attT[:, head % 2, a:b], in0=ps[:, 6, a:b],
                                                   scalar=256.0 ** -0.5, in1=decay[:, head, c:c + b - a],
                                                   op0=ALU.mult, op1=ALU.mult).then_inc(att_ready, 1)

            def group_stats(head):
                for t in range(T):
                    dve.wait_ge(ret_y, T * head + t + 1)
                    then(nc.vector.bn_stats(gstats[:, t, :], ps[:, t, :]))
                    nc.vector.bn_aggr(gmv[:, t, :], gstats[:, t, :]).then_inc(gn_var, 1)

            def group_norm(head):
                dve.wait_ge(gn_std, head + 1)
                then(nc.vector.reciprocal(grstd[:, :], gstd[:, :]))
                dve.wait_ge(gn_landed[head], 32)
                for t in range(T):
                    if head >= 1:
                        dve.wait_ge(z_ready, T * (head - 1) + t + 1)
                    nc.vector.scalar_tensor_tensor(out=normed[:, t, :], in0=ps[:, t, :],
                                                   scalar=gmv[:, t, 0:1], in1=gn[:, head % 2, 0, :],
                                                   op0=ALU.subtract, op1=ALU.mult).then_inc(y_read, 1)
                    dve.wait_ge(y_read, T * head + t + 1)
                    nc.vector.scalar_tensor_tensor(out=normed[:, t, :], in0=normed[:, t, :],
                                                   scalar=grstd[:, t:t + 1], in1=gn[:, head % 2, 1, :],
                                                   op0=ALU.mult, op1=ALU.add).then_inc(norm_ready, 1)

            def drain_zT_lo(n):
                head, t = n // T, n % T
                dve.wait_ge(zT_hi_done, n + 1)
                lo_of(zT_lo[:, 4 * head:4 * head + 4, t * P:(t + 1) * P], bank(7, 4),
                      zT_hi[:, 4 * head:4 * head + 4, t * P:(t + 1) * P]).then_inc(zT_lo_done, 1)

            for s in range(12):
                u, c = U_RET_IN + QK_UNITS + 4 + s, 2 + s // 2
                head = (s - 2) // 2
                if s % 2 == 1 and c < RH:
                    drain_block(u, 0, vals[:, c, 1, :], 3 + 2 * (c % 2))
                if s == 1:
                    decayed(0)
                if s >= 2 and s % 2 == 0 and head < RH:
                    group_stats(head)
                    if head + 1 < RH:
                        decayed(head + 1)
                if s >= 6:
                    drain_zT_lo(s - 6)
                split_lo(dve, u + AHEAD)
                if s >= 2 and s % 2 == 0 and head < RH:
                    group_norm(head)
            for u in range(U_RET_OUT, U_FFN - AHEAD):
                if u < U_RET_OUT + T:
                    drain_zT_lo(T * (RH - 1) + u - U_RET_OUT)
                split_lo(dve, u + AHEAD)
            norm_between(0, U_FFN)

            def drain_fT(b, buf=0):
                if b is None:
                    dve.wait_ge(fT_hi_done, 1)
                    lo_of(fT_lo[:, buf], bank(2, 2), fT_hi[:, buf]).then_inc(fT_lo_done, 1)
                else:
                    dve.wait_ge(fT_hi_done, b + 1)
                    lo_of(fT_lo[:, buf].rearrange("p c n -> p (c n)"), hid2[:, :],
                          fT_hi[:, buf].rearrange("p c n -> p (c n)")).then_inc(fT_lo_done, 1)

            def ffn_pair(r, first=False, last=False):
                for half in range(2):
                    u, b = U_FFN + 2 + 3 * half, 2 * r + half + 1
                    split_lo(dve, u + AHEAD, r)
                    drain_fT(None if first and half == 0 else b - 1)
                    unit_done(dve, u + 1, r)
                    dve.wait_ge(f_silu, b + 1)
                    dve.wait_ge(fT_lo_done, b)
                    nc.vector.tensor_tensor(hid2[:, :], act2[:, :], ps[:, 6 * (1 - half) + 1, :],
                                            ALU.mult).then_inc(f_mul, 1)
                    if last and half == 1:
                        drain_fT(b, 1)
                    split_lo(dve, u + 1 + AHEAD, r)
                    if not (last and half == 1):
                        split_lo(dve, u + 2 + AHEAD, r)

            split_lo(dve, U_FFN + AHEAD)
            dve.wait_ge(f_silu, 1)
            nc.vector.tensor_tensor(hid2[:, :].rearrange("p (t n) -> p t n", t=T),
                                    act2[:, :].rearrange("p (t n) -> p t n", t=T), ps[:, 0:2, FB:2 * FB],
                                    ALU.mult).then_inc(f_mul, 1)
            split_lo(dve, U_FFN + 1 + AHEAD)
            ffn_pair(0, first=True)
            with dve.Fori(1, NFB // 2 - 1) as r:
                ffn_pair(r)
            ffn_pair(NFB // 2 - 1, last=True)
            norm_between(1, U_KVQ)

            def scores(pair):
                dve.wait_ge(s_done, pair + 1)
                for t in range(T):
                    w = P * (t + 1)
                    for i in range(2):
                        head = 2 * pair + i
                        ins = nc.vector.scalar_tensor_tensor(out=prob[:, t, head, 0:w], in0=past[:, t, 0:w],
                                                             scalar=-2.0 ** (-8.0 / AH * (head + 1)),
                                                             in1=ps[:, score_banks(pair)[1 - t], i * w:(i + 1) * w],
                                                             op0=ALU.mult, op1=ALU.add)
                ins.then_inc(scores_read, 1)
                dve.wait_ge(scores_read, pair + 1)
                for t in range(T):
                    ins = nc.vector.tensor_reduce(neg_max[:, t, 2 * pair:2 * pair + 2],
                                                  prob[:, t, 2 * pair:2 * pair + 2, 0:P * (t + 1)], AX.X, ALU.max,
                                                  negate=True)
                ins.then_inc(max_ready, 1)

            def probabilities(pair):
                dve.wait_ge(p_exp, 2 * T * (pair + 1))
                then(nc.vector.reciprocal(inv_p[:, :, 2 * pair:2 * pair + 2], psum_p[:, :, 2 * pair:2 * pair + 2]))
                for t in range(T):
                    for head in (2 * pair, 2 * pair + 1):
                        p = prob[:, t, head, 0:P * (t + 1)]
                        ins = nc.vector.tensor_scalar(p, p, inv_p[:, t, head:head + 1], None, ALU.mult)
                ins.then_inc(p_ready, 1)

            def copy_pT(head):
                dve.wait_ge(pT_done, head + 1)
                nc.vector.tensor_copy(pT[:, 1, :], ps[:, 7, 0:3 * P]).then_inc(pT_dve, 1)

            dve.wait_ge(tables, 6)
            for s in range(12):
                u, pair = U_KVQ + s, (s - 3) // 2
                if s == 11:
                    copy_pT(1)
                if s in (1, 11):
                    drain_block(u, 0, att_v[:, s // 6, 1, :], 3)
                elif 3 <= s < 10 and s % 2 == 1:
                    drain_columns(u, kqT[:, AH + 2 * pair:AH + 2 * pair + 2, :], 5, P ** -0.5)
                if s < 11:
                    split_lo(dve, u + AHEAD)
                if s >= 4 and s % 2 == 0:
                    scores((s - 4) // 2)
                elif s >= 5:
                    probabilities((s - 5) // 2)
            for pair in range(AH // 2):
                if pair >= 1:
                    copy_pT(2 * pair + 1)
                if pair == 1:
                    split_lo(dve, U_ATT_OUT + AHEAD - 1)
                dve.wait_ge(oT_hi_done, pair + 1)
                lo_of(xT_lo[:, 2 * pair:2 * pair + 2, :], bank(pair % 2, 2),
                      xT_hi[:, 2 * pair:2 * pair + 2, :]).then_inc(oT_lo_done, 1)
            split_lo(dve, U_ATT_OUT + AHEAD)

            def drain_router_xT(t):
                dve.wait_ge(filled, FILLED_XT[3] + 2 * t + 2)
                nc.vector.tensor_copy(xT[:, 4:8, t * P:(t + 1) * P], bank(7, 4)).then_inc(dve_drained, 1)

            def split_h(t):
                dve.wait_ge(h_hi_done, t + 1)
                lo_of(h_lo[:, t, :], h[:, t, :], h_hi[:, t, :]).then_inc(h_split, 1)

            norm_mean(2, 0)
            norm_end(2, 0)
            split_h(0)
            drain_router_xT(0)
            norm_mean(2, 1)
            norm_end(2, 1)
            drain_router_xT(1)
            nc.vector.memset(gate_of[:, :, 0:1], 0.0).then_inc(dve_step, 1)
            step[0] += 1

            def top_two(t):
                dve.wait_ge(logit_done, t + 1)
                then(nc.vector.tensor_copy(logits[:, t, :], ps[:, t, 0:EX]))
                then(nc.vector.max(top[:, t, :], logits[:, t, :]))
                then(nc.vector.max_index(top_i[:, t, :], top[:, t, :], logits[:, t, :]))

            def experts_of(t):
                top_two(t)
                if t == 1:
                    nc.vector.tensor_tensor(two[:, 0, :], top[:, :, 1], top[:, :, 0], ALU.subtract).then_inc(gap_ready, 1)
                then(nc.vector.tensor_copy(top_f[:, :, t], top_i[:, t, 0:2]))
                for k in range(2):
                    ins = nc.vector.tensor_scalar(hot[:, k, t, :], iota_expert[:, :], top_f[:, k, t:t + 1], None,
                                                  ALU.is_equal)
                then(ins)
                nc.vector.tensor_tensor(member[:, t, :], hot[:, 0, t, :], hot[:, 1, t, :], ALU.add).then_inc(member_ready, 1)

            def by_expert(a):
                return a.unsqueeze(3).broadcast_to([P, 2, T, EX])

            def slots(t):
                dve.wait_ge(rank_done, t + 1)
                then(nc.vector.scalar_tensor_tensor(out=slot_of[:, t, 0:EX], in0=ps[:, 2 + t, 0:EX], scalar=1.0,
                                                    in1=member[:, t, :], op0=ALU.add, op1=ALU.mult))

            def select_tile(j, t):
                nc.vector.tensor_scalar(sel[:, t, :], iota_slot[:, :], slot_of[:, t, bass.ds(j, 1)], None,
                                        ALU.is_equal).then_inc(sel_ready, 1)

            experts_of(0)
            split_h(1)
            dve.wait_ge(lo_done, U_MOE + 1)
            split_lo(dve, U_MOE + 1)
            experts_of(1)
            for t in range(T):
                slots(t)
                select_tile(0, t)

            def select(j):
                for t in range(T):
                    select_tile(j, t)

            def copy_xg(j):
                dve.wait_ge(gathered, 2 * j + 2)
                nc.vector.tensor_copy(xg[:, BANK:2 * BANK], ps[:, 5, :]).then_inc(xg_rows_dve, 1)

            def drain_xgT(j):
                for half, at in enumerate((7, 5)):
                    dve.wait_ge(xg_hi_done, 2 * j + half + 1)
                    lo_of(xg_lo[:, 4 * half:4 * half + 4, :], bank(at, 4),
                          xg_hi[:, 4 * half:4 * half + 4, :]).then_inc(xg_lo_done, 1)

            dve.wait_ge(gap_exp, 1)
            then(nc.vector.tensor_scalar(two[:, 2, :], two[:, 1, :], 1.0, None, ALU.add))
            then(nc.vector.reciprocal(two[:, 2, :], two[:, 2, :]))
            then(nc.vector.tensor_tensor(two[:, 3, :], two[:, 1, :], two[:, 2, :], ALU.mult))
            then(nc.vector.tensor_tensor(hot_w[:, :, :, :], hot[:, :, :, :], by_expert(two[:, 2:4, :]), ALU.mult))
            copy_xg(0)
            drain_xgT(0)
            for k in range(2):
                then(nc.vector.tensor_tensor(gate_of[:, :, 1 + k * EX:1 + (k + 1) * EX], hot_w[:, 0, :, :],
                                             hot_w[:, 1, :, :], ALU.add))
            split_lo(dve, U_MOE + 2)
            then(nc.vector.tensor_scalar(h[:, :, :], h[:, :, :], ALPHA, None, ALU.mult))
            then(nc.vector.tensor_scalar(slot_of[:, :, EX:2 * EX], slot_of[:, :, 0:EX], -float(P), None, ALU.add))
            dve.wait_ge(counted, 1)
            then(nc.vector.tensor_reduce(most[:, :], ps[:, 2, EX:2 * EX], AX.X, ALU.max))
            nc.vector.tensor_scalar(over[:, :], most[:, :], float(P), None, ALU.is_gt).then_inc(over_ready, 1)

            def mul_e(n, u_up, r):
                unit_done(dve, u_up, r)
                dve.wait_ge(e_silu, n + 1)
                nc.vector.tensor_tensor(hid4[:, :], act4[:, :], ps[:, 1, :], ALU.mult).then_inc(e_mul, 1)

            def drain_gT(n, buf=0):
                dve.wait_ge(gT_hi_done, n + 1)
                lo_of(gT_lo[:, buf], bank(6, 4), gT_hi[:, buf]).then_inc(gT_lo_done, 1)

            def add_scattered(j, t, row_sums=None, at=4):
                dve.wait_ge(scattered, T * j + t + 1)
                nc.vector.scalar_tensor_tensor(out=h[:, t, :], in0=ps[:, at:at + 2, :].rearrange("p b n -> p (b n)"),
                                               scalar=gate_of[:, t, bass.ds(j, 1)], in1=h[:, t, :],
                                               op0=ALU.mult, op1=ALU.add, accum_out=row_sums).then_inc(summed, 1)

            def job(j, first=False, last=False):
                def split(i, b=0):
                    if first and isinstance(b, int) and 0 <= 6 * b + i - FIRST_KEPT < KEPT:
                        write_lo(dve, U_MOE + i, NEB * j + b, kept[:, 6 * b + i - FIRST_KEPT, :])
                    else:
                        split_lo(dve, U_MOE + i, NEB * j + b)

                def block(b, splits):
                    n = NEB * j + b
                    split(0, b)
                    split(1, b)
                    drain_gT(n - 1)
                    split(2, b)
                    if splits == 6:
                        split(3, b)
                    mul_e(n, U_MOE + 1, n)
                    for k in range(splits - 2, splits):
                        split(k, b)

                split(3)
                add_scattered(j, 0)
                split(4)
                split(5)
                mul_e(NEB * j, U_MOE + 3, NEB * j)
                add_scattered(j, 1)
                if not last:
                    dve.wait_ge(selT_done, j + 1)
                    select(j + 1)
                with dve.Fori(1, NEB - 1) as b:
                    block(b, 6)
                block(NEB - 1, 5)
                drain_gT(NEB * j + NEB - 1, 1)
                split(5, NEB - 1)
                if not last:
                    copy_xg(j + 1)
                    split_lo(dve, U_MOE + JOB_UNITS, NEB * j)
                    drain_xgT(j + 1)
                    split_lo(dve, U_MOE + JOB_UNITS + 1, NEB * j)
                for half in range(2):
                    n = slice(half * BANK, (half + 1) * BANK)
                    dve.wait_ge(y_hi_done, 2 * j + half + 1)
                    lo_of(y_lo[:, n], ps[:, 2 + half, :], y_hi[:, n]).then_inc(y_lo_done, 1)
                if not last:
                    split_lo(dve, U_MOE + JOB_UNITS + 2, NEB * j)

            def jobs_from(start):
                job(start, first=True)
                with dve.Fori(start + 1, start + EX - 1) as j:
                    job(j)
                job(start + EX - 1, last=True)

            jobs_from(0)
            dve.wait_ge(over_ready, 1)
            more = dve.value_load(over[0:1, 0:1], min_val=0, max_val=1)
            with dve.If(more > 0):
                dve.wait_ge(selT_done, EX)
                select(EX)
                copy_xg(EX)
                for i in range(AHEAD):
                    if i == 1:
                        drain_xgT(EX)
                    split_lo(dve, U_MOE + i, NEB * EX)
                jobs_from(EX)
            jobs = EX + EX * more
            for t in range(T):
                add_scattered(jobs, t, row_sum[:, t:t + 1], 4 * (1 - t))
                dve.wait_ge(summed, T * jobs + t + 1)
                norm_mean(3, t)
            for t in range(T):
                norm_end(3, t)

        @block.tensor
        def _(pe):
            def passes(dst, a_hi, a_lo, b_hi, b_lo, start, stop):
                pe.matmul(dst, a_hi, b_hi, start=start, stop=False, skip_group_check=True)
                pe.matmul(dst, a_hi, b_lo, start=False, stop=False, skip_group_check=True)
                return pe.matmul(dst, a_lo, b_hi, start=False, stop=stop, skip_group_check=True)

            def unit_ready(u, r=0):
                pe.wait_ge(lo_done, number(u + 1, r))

            def transposes_x(n, t):
                if n == 0:
                    pe.wait_ge(x_landed, 16 * T)
                    pe.wait_ge(tables, 1)
                else:
                    pe.wait_ge(h_ready, T * (n - 1) + t + 1)
                if t == 1:
                    if n in (1, 2):
                        pe.wait_ge(dve_drained, DR_XT[n] + 2)
                    elif n == 3:
                        drained(DR_XT[n] + 1)
                for g in range(2):
                    for k in range(4):
                        last = pe.transpose(ps[:, x_bank(n, t) + g, k * P:(k + 1) * P],
                                            h[:, t, (4 * g + k) * P:(4 * g + k + 1) * P], ident[:, :])
                    last.then_inc(filled, 1)

            def xT_ready(n, t):
                pe.wait_ge(dve_drained, DR_XT[n] + 2 * t + 2)

            def project_tile(u, part, t, at):
                tok = slice(t * P, (t + 1) * P)
                for c in range(4):
                    k = 4 * part + c
                    w = slice(c * BANK, (c + 1) * BANK)
                    last = passes(ps[:, at, :], xT_hi[:, k, tok], xT_lo[:, k, tok],
                                  whi[:, u % SPLIT, w], wlo[:, u % SPLIT, w], k == 0, k == KD - 1)
                return last

            def project_unit(u, r, part, banks):
                unit_ready(u, r)
                project_tile(u, part, 0, banks[0])
                project_tile(u, part, 1, banks[1]).then_inc(unit_used, 1)

            def column_unit(u, r, at):
                unit_ready(u, r)
                for c in range(2):
                    for k in range(KD):
                        w = slice(k * FB + c * P, k * FB + (c + 1) * P)
                        last = passes(ps[:, at, c * SEQ:(c + 1) * SEQ], whi[:, u % SPLIT, w], wlo[:, u % SPLIT, w],
                                      xT_hi[:, k, :], xT_lo[:, k, :], k == 0, k == KD - 1)
                last.then_inc(unit_used, 1)

            def drained(n):
                pe.wait_ge(act_drained, n)
                pe.wait_ge(dve_drained, n)

            def out_product(u, r, a_hi, a_lo, first, last_k):
                unit_ready(u, r)
                for t in range(T):
                    last = out_product_tile(u, t, a_hi, a_lo, first, last_k)
                last.then_inc(unit_used, 1)

            def out_product_tile(u, t, a_hi, a_lo, first, last_k, chunks=(0, 1)):
                tok = slice(t * P, (t + 1) * P)
                for c in chunks:
                    for half in range(2):
                        w = slice((2 * c + half) * BANK, (2 * c + half + 1) * BANK)
                        last = passes(ps[:, 2 + 2 * t + half, :], a_hi[:, c, tok], a_lo[:, c, tok],
                                      whi[:, u % SPLIT, w], wlo[:, u % SPLIT, w],
                                      first and c == 0, last_k and c == 1)
                return last

            def out_product_end(units, chunks, next_stage, chunks_ready):
                for t in range(T):
                    for u, (a_hi, a_lo) in zip(units, chunks):
                        if t == 0:
                            unit_ready(u)
                            if u == units[-1]:
                                pe.wait_ge(*chunks_ready)
                        elif u == units[-1] and len(units) > 2:
                            transposes_x(next_stage, 0)
                        elif u == units[-1]:
                            out_product_tile(u, t, a_hi, a_lo, False, False, (0,))
                            transposes_x(next_stage, 0)
                        halves = (1,) if t == 1 and u == units[-1] and len(units) == 2 else (0, 1)
                        last = out_product_tile(u, t, a_hi, a_lo, False, u == units[-1], halves)
                        if t == 1:
                            last.then_inc(unit_used, 1)
                    if t == 0:
                        last.then_inc(tile0_summed, 1)

            for t in range(T):
                transposes_x(0, t)
            xT_ready(0, 1)
            for i in range(QK_UNITS):
                if i >= 4:
                    pe.wait_ge((act_drained, dve_drained)[i % 2], 4 + (i - 4) // 2 + 1)
                column_unit(U_RET_IN + i, 0, 2 + i % 4)

            def ret_row_unit(i):
                block = (i - QK_UNITS) // 2
                if i % 2 == 0 and block < RH + 2:
                    drained(4 + RH - 2 + block + 1)
                elif i % 2 == 0:
                    pe.wait_ge(silu_g, block - RH - 1)
                project_unit(U_RET_IN + i, 0, i % 2, (2 + 2 * (block % 2), 3 + 2 * (block % 2)))

            for i in range(QK_UNITS, QK_UNITS + 4):
                ret_row_unit(i)

            def ret_scores(head):
                q, k = 2 * head, KD + 2 * head
                for c in range(2):
                    pe.matmul(ps[:, 6, 0:SEQ], qkT[:, k + c, 0:P], qkT[:, q + c, :],
                              start=(c == 0), stop=(c == 1))
                for c in range(2):
                    last = pe.matmul(ps[:, 6, SEQ:SEQ + P], qkT[:, k + c, P:SEQ], qkT[:, q + c, P:SEQ],
                                     start=(c == 0), stop=(c == 1))
                last.then_inc(score_done, 1)

            def ret_values(head):
                pe.wait_ge(att_ready, 2 * (head + 1))
                if head >= 1:
                    pe.wait_ge(y_read, T * head)
                a = attT[:, head % 2]
                pe.matmul(ps[:, 0, :], a[:, 0:P], vals[:, head, 0, :], start=True, stop=True).then_inc(ret_y, 1)
                pe.matmul(ps[:, 1, :], a[:, P:SEQ], vals[:, head, 0, :], start=True, stop=False)
                pe.matmul(ps[:, 1, :], a[:, SEQ:SEQ + P], vals[:, head, 1, :], start=False,
                          stop=True).then_inc(ret_y, 1)

            def transposes_z(n):
                head, t = n // T, n % T
                pe.wait_ge(z_ready, n + 1)
                if n >= 1:
                    pe.wait_ge(zT_lo_done, n)
                for k in range(4):
                    last = pe.transpose(ps[:, 7, k * P:(k + 1) * P], gated[:, head, t, k * P:(k + 1) * P],
                                        ident[:, :])
                last.then_inc(zT_done, 1)

            for s in range(12):
                ret_row_unit(QK_UNITS + 4 + s)
                if s == 1:
                    ret_scores(0)
                if s >= 2 and s % 2 == 0 and (s - 2) // 2 < RH:
                    ret_values((s - 2) // 2)
                    if s // 2 < RH:
                        ret_scores(s // 2)
                if s >= 6:
                    transposes_z(s - 6)

            def zT_chunks(i):
                return zT_hi[:, 2 * i:2 * i + 2], zT_lo[:, 2 * i:2 * i + 2]

            pe.wait_ge(silu_g, RH)
            for i in range(U_FFN - U_RET_OUT - 3):
                pe.wait_ge(zT_lo_done, T * (i // 2 + 1))
                out_product(U_RET_OUT + i, 0, *zT_chunks(i), i == 0, False)
                if i < T:
                    transposes_z(T * (RH - 1) + i)
            pe.wait_ge(zT_lo_done, T * (RH - 1))
            out_product_end(range(U_FFN - 3, U_FFN), [zT_chunks(U_FFN - U_RET_OUT - 3 + i) for i in range(3)],
                            1, (zT_lo_done, T * RH))

            def ffn_in_tile(u, part, t):
                tok = slice(t * P, (t + 1) * P)
                for k in range(KD):
                    w = slice(k * FB, (k + 1) * FB)
                    last = passes(ps[:, t, part * FB:(part + 1) * FB], xT_hi[:, k, tok], xT_lo[:, k, tok],
                                  whi[:, u % SPLIT, w], wlo[:, u % SPLIT, w], k == 0, k == KD - 1)
                return last

            def first_block(n, u, tile_of):
                xT_ready(n, 0)
                unit_ready(u)
                tile_of(u, 0, 0)
                transposes_x(n, 1)
                unit_ready(u + 1)
                tile_of(u + 1, 1, 0)
                xT_ready(n, 1)
                for part in range(2):
                    tile_of(u + part, part, 1).then_inc(unit_used, 1)

            def transposes_f():
                pe.wait_ge(f_mul, 1)
                for c in range(2):
                    for t in range(T):
                        at = t * FB + c * P
                        last = pe.transpose(ps[:, 2, (2 * c + t) * P:(2 * c + t + 1) * P],
                                            hid2[:, at:at + P], ident[:, :])
                last.then_inc(fT_done, 1)

            def ffn_pair(r, first=False, last=False):
                for half in range(2):
                    u, b = U_FFN + 2 + 3 * half, 2 * r + half + 1
                    column_unit(u, r, 6 * (1 - half))
                    if first and half == 0:
                        transposes_f()
                    column_unit(u + 1, r, 6 * (1 - half) + 1)
                    if not (last and half == 1):
                        pe.wait_ge(fT_lo_done, b)
                        out_product(u + 2, r, fT_hi[:, 0], fT_lo[:, 0], first and half == 0, False)

            first_block(1, U_FFN, ffn_in_tile)
            ffn_pair(0, first=True)
            with pe.Fori(1, NFB // 2 - 1) as r:
                ffn_pair(r)
            ffn_pair(NFB // 2 - 1, last=True)
            pe.wait_ge(fT_lo_done, NFB - 1)
            out_product_end([U_KVQ - 2, U_KVQ - 1], [(fT_hi[:, i], fT_lo[:, i]) for i in range(2)], 2,
                            (fT_lo_done, NFB))

            first_block(2, U_KVQ, lambda u, part, t: project_tile(u, part, t, 2 + t))
            def att_scores(pair):
                drained(KVQ_DRAINED + 1 + pair + 1)
                if pair == 2:
                    pe.wait_ge(scores_read, 1)
                for t in (1, 0):
                    w = P * (t + 1)
                    for i in range(2):
                        head = 2 * pair + i
                        last = pe.matmul(ps[:, score_banks(pair)[1 - t], i * w:(i + 1) * w],
                                         kqT[:, AH + head, t * P:(t + 1) * P], kqT[:, head, 0:w],
                                         start=True, stop=True)
                last.then_inc(s_done, 1)

            def transposes_p(head):
                pe.wait_ge(p_ready, head // 2 + 1)
                for c, piece in enumerate((prob[:, 0, head, 0:P], prob[:, 1, head, 0:P], prob[:, 1, head, P:SEQ])):
                    last = pe.transpose(ps[:, 6 + head % 2, c * P:(c + 1) * P], piece, ident[:, :])
                last.then_inc(pT_done, 1)

            for pair in range(AH // 2):
                if pair >= 1:
                    pe.wait_ge(act_drained, KVQ_DRAINED + 1 + pair)
                column_unit(U_KVQ + 2 + 2 * pair, 0, 4)
                if pair >= 1:
                    att_scores(pair - 1)
                column_unit(U_KVQ + 3 + 2 * pair, 0, 5)
            for part in range(2):
                project_unit(U_KVQ + 10 + part, 0, part, (2, 3))
                if part == 0:
                    att_scores(AH // 2 - 1)
                    pe.wait_ge(scores_read, 2)
                    transposes_p(0)
                    transposes_p(1)

            def oT_chunks(i):
                return xT_hi[:, 2 * i:2 * i + 2], xT_lo[:, 2 * i:2 * i + 2]

            for head in range(AH):
                pe.wait_ge((pT_act, pT_dve)[head % 2], head // 2 + 1)
                pair = head // 2
                if head == 4:
                    drained(KVQ_DRAINED + AH // 2 + 2)
                if head == 2:
                    pe.wait_ge(scores_read, AH // 2)
                if head % 2 == 0 and pair >= 2:
                    pe.wait_ge(oT_lo_done, pair - 1)
                o = ps[:, pair % 2, (head % 2) * SEQ:(head % 2 + 1) * SEQ]
                v = slice((head % 4) * P, (head % 4 + 1) * P)
                pe.matmul(o, att_v[:, head // 4, 0, v], pT[:, head % 2, 0:SEQ], start=True, stop=False,
                          skip_group_check=True)
                last = pe.matmul(o[:, P:SEQ], att_v[:, head // 4, 1, v], pT[:, head % 2, SEQ:SEQ + P],
                                 start=False, stop=True, skip_group_check=True)
                if head % 2 == 1:
                    last.then_inc(o_done, 1)
                if head + 2 < AH:
                    transposes_p(head + 2)
                if head == 3:
                    pe.wait_ge(oT_lo_done, 1)
                    out_product(U_ATT_OUT, 0, *oT_chunks(0), True, False)
            pe.wait_ge(oT_lo_done, AH // 2 - 1)
            out_product_end(range(U_ATT_OUT + 1, U_MOE), [oT_chunks(i) for i in range(1, KD // 2)], 3,
                            (oT_lo_done, AH // 2))

            pe.wait_ge(router_landed, 16)
            pe.wait_ge(tables, 6)
            for t in range(T):
                if t == 1:
                    transposes_x(3, t)
                drained(DR_XT[3] + t + 1)
                for k in range(KD):
                    last = pe.matmul(ps[:, t, 0:EX], xT[:, k, t * P:(t + 1) * P], router[:, k, :],
                                     start=(k == 0), stop=(k == KD - 1), skip_group_check=True)
                last.then_inc(logit_done, 1)
            pe.wait_ge(member_ready, 1)
            pe.matmul(ps[:, 2, 0:EX], before[:, :], member[:, 0, :], start=True, stop=True).then_inc(rank_done, 1)
            pe.matmul(ps[:, 3, 0:EX], ones[:, :], member[:, 0, :], start=True, stop=False, skip_group_check=True)
            pe.wait_ge(member_ready, 2)
            pe.matmul(ps[:, 3, 0:EX], before[:, :], member[:, 1, :], start=False, stop=True,
                      skip_group_check=True).then_inc(rank_done, 1)

            def gather(j):
                for t in range(T):
                    pe.wait_ge(sel_ready, T * j + t + 1)
                    for half in range(2):
                        for src in (h_hi, h_lo):
                            last = pe.matmul(ps[:, 4 + half, :], sel[:, t, :], src[:, t, half * BANK:(half + 1) * BANK],
                                             start=(t == 0 and src is h_hi), stop=(t == T - 1 and src is h_lo),
                                             skip_group_check=True)
                        if t == 1:
                            last.then_inc(gathered, 1)

            def transposes_xg(j):
                for half, (copied, at) in enumerate(((xg_rows_act, 7), (xg_rows_dve, 5))):
                    pe.wait_ge(copied, j + 1)
                    if half == 0:
                        pe.wait_ge(selT_ready, j + 1)
                    for k in range(4):
                        last = pe.transpose(ps[:, at, k * P:(k + 1) * P],
                                            xg[:, (4 * half + k) * P:(4 * half + k + 1) * P], ident[:, :])
                    last.then_inc(xgT_done, 1)

            def scatter(j, t, at=4):
                for half in range(2):
                    n = slice(half * BANK, (half + 1) * BANK)
                    pe.matmul(ps[:, at + half, :], selT[:, t * P:(t + 1) * P], y_hi[:, n], start=True, stop=False)
                    last = pe.matmul(ps[:, at + half, :], selT[:, t * P:(t + 1) * P], y_lo[:, n],
                                     start=False, stop=True)
                last.then_inc(scattered, 1)

            def moe_in_product(u, r, part, first_of=None):
                for q in range(2):
                    if first_of is not None:
                        pe.wait_ge(xg_lo_done, 2 * first_of + q + 1)
                    unit_ready(u + q, r)
                    for c in range(4):
                        k = 4 * q + c
                        w = slice(c * BANK, (c + 1) * BANK)
                        last = passes(ps[:, part, :], xg_hi[:, k, :], xg_lo[:, k, :],
                                      whi[:, (u + q) % SPLIT, w], wlo[:, (u + q) % SPLIT, w], k == 0, k == KD - 1)
                    last.then_inc(unit_used, 1)

            def moe_out_product(u, r, first, last_k, parts=(0, 1), buf=0):
                for q in parts:
                    unit_ready(u + q, r)
                    for c in range(2):
                        for half in range(2):
                            w = slice((2 * c + half) * BANK, (2 * c + half + 1) * BANK)
                            last = passes(ps[:, 2 + half, :], gT_hi[:, buf, 2 * q + c, :],
                                          gT_lo[:, buf, 2 * q + c, :],
                                          whi[:, (u + q) % SPLIT, w], wlo[:, (u + q) % SPLIT, w],
                                          first and q == 0 and c == 0, last_k and q == 1 and c == 1)
                    last.then_inc(unit_used, 1)

            def transposes_g(n):
                pe.wait_ge(e_mul, n + 1)
                for k in range(4):
                    last = pe.transpose(ps[:, 6, k * P:(k + 1) * P], hid4[:, k * P:(k + 1) * P], ident[:, :])
                last.then_inc(gT_done, 1)

            def moe_block(j, b, first, parts=(0, 1)):
                n = NEB * j + b
                pe.wait_ge(e_silu, n)
                moe_in_product(U_MOE - 2, n, 0)
                transposes_g(n - 1)
                moe_in_product(U_MOE, n, 1)
                pe.wait_ge(gT_lo_done, n)
                moe_out_product(U_MOE + 2, n, first, False, parts)

            def job(j, last_job=False):
                moe_in_product(U_MOE, NEB * j, 0, first_of=j)
                pe.wait_ge(y_lo_done, 2 * j + 2)
                pe.wait_ge(selT_ready, j + 1)
                scatter(j, 0)
                moe_in_product(U_MOE + 2, NEB * j, 1)
                pe.wait_ge(summed, T * j + 1)
                scatter(j, 1)
                for t in range(T):
                    last = pe.transpose(ps[:, 7, t * P:(t + 1) * P], sel[:, t, :].bitcast(F32), ident[:, :])
                last.then_inc(selT_done, 1)
                moe_block(j, 1, True)
                with pe.Fori(2, NEB - 1) as b:
                    moe_block(j, b, False)
                n = NEB * j + NEB - 1
                moe_block(j, NEB - 1, False, (0,))
                transposes_g(n)
                if not last_job:
                    pe.wait_ge(summed, T * j + T)
                    gather(j + 1)
                moe_out_product(U_MOE + 2, n, False, False, (1,))
                if not last_job:
                    transposes_xg(j + 1)
                pe.wait_ge(gT_lo_done, n + 1)
                moe_out_product(U_MOE + JOB_UNITS - 2, NEB * j, False, True, buf=1)

            def jobs_from(first):
                with pe.Fori(first, first + EX - 1) as j:
                    job(j)
                job(first + EX - 1, last_job=True)

            pe.wait_ge(h_split, T)
            gather(0)
            transposes_xg(0)
            for t in range(T):
                last = pe.matmul(ps[:, 2, EX:2 * EX], ones[:, :], member[:, t, :], start=(t == 0), stop=(t == T - 1))
            last.then_inc(counted, 1)
            jobs_from(0)
            pe.wait_ge(over_ready, 1)
            more = pe.value_load(over[0:1, 0:1], min_val=0, max_val=1)
            with pe.If(more > 0):
                pe.wait_ge(summed, T * EX)
                gather(EX)
                transposes_xg(EX)
                jobs_from(EX)
            jobs = EX + EX * more
            pe.wait_ge(y_lo_done, 2 * jobs + 2)
            pe.wait_ge(selT_ready, jobs + 1)
            for t in range(T):
                scatter(jobs, t, 4 * (1 - t))


_INS = ['x', 'ln_g', 'ln_b', 'ret_w_in', 'ret_gn_g', 'ret_gn_b', 'ret_w_out', 'kv_w', 'moba_w_q', 'moba_w_out',
        'ffn_w_in', 'ffn_w_out', 'moe_router', 'moe_w_in', 'moe_w_out']


def kernel(**inputs):
    import numpy as np
    import concourse.bacc as bacc
    from concourse.bass_utils import run_bass_kernel_spmd

    nc = bacc.Bacc("TRN2", target_bir_lowering=False, num_devices=1)
    arrays, args = {}, []
    for name in _INS:
        a = np.ascontiguousarray(inputs[name])
        arrays[f"in_{name}"] = a
        args.append(nc.dram_tensor(f"in_{name}", a.shape, mybir.dt.from_np(a.dtype), kind="ExternalInput").ap())
    args.append(nc.dram_tensor("out_h", inputs["x"].shape, F32, kind="ExternalOutput").ap())
    build(nc, *args)
    r = run_bass_kernel_spmd(nc, [arrays], core_ids=[0])
    return r.results[0]["out_h"]
```
